# Optimizing a Trainium2 kernel written in Bass

```python
import math
import jax, jax.numpy as jnp
from jax import lax
import numpy as np

D_MODEL = 1024
BATCH = 1
SEQ = 1024
DEPTH = 1

D_MIX = D_MODEL
ATTN_HEADS = 8
HEAD_DIM = 64
D_ATTN = ATTN_HEADS * HEAD_DIM
SGU_GROUPS = 4
SGU_CH = 128
D_SGU = SGU_GROUPS * SGU_CH
D_IN_PROJ = 3 * D_ATTN + 2 * D_SGU
CHUNK = 128
DILATED = ((128, 1), (512, 4), (2048, 16))
BLK = 128
NUM_BUCKETS = 32
MAX_DISTANCE = 2048
PEER_HEADS = 8
PEER_KEYS = 128
PEER_EXPERTS = PEER_KEYS * PEER_KEYS
PEER_D_KEY = 256
PEER_TOPK = 16
PEER_CHUNK = 128
EPS = 1e-6
NEG = -1e30

kernel_name = "hymba_sgu_dilated_attn_peer_layer"

def _rms(x, w):
    xf = x.astype(jnp.float32)
    y = xf * lax.rsqrt(jnp.mean(xf * xf, axis=-1, keepdims=True) + EPS)
    return (y * w.astype(jnp.float32)).astype(x.dtype)

def _t5_bucket(dist):
    max_exact = NUM_BUCKETS // 2
    d_f = jnp.maximum(dist, max_exact).astype(jnp.float32)
    large = max_exact + (jnp.log(d_f / max_exact) / math.log(MAX_DISTANCE / max_exact)
                         * (NUM_BUCKETS - max_exact)).astype(jnp.int32)
    large = jnp.minimum(large, NUM_BUCKETS - 1)
    return jnp.where(dist < max_exact, dist, large)

def _dilated_window_attention(q, k, v, rel_bias, window, dil):
    b, s, h, dh = q.shape
    w_sub = window // dil
    assert w_sub <= BLK
    L = s // dil
    nblk = -(-L // BLK)
    Lp = nblk * BLK

    def to_res(t):
        return t.reshape(b, L, dil, h, dh).transpose(0, 2, 1, 3, 4).reshape(b * dil, L, h, dh)

    qr, kr, vr = to_res(q), to_res(k), to_res(v)
    qb = jnp.pad(qr, ((0, 0), (0, Lp - L), (0, 0), (0, 0))).reshape(b * dil, nblk, BLK, h, dh)

    def kv_blocks(t):
        tp = jnp.pad(t, ((0, 0), (BLK, Lp - L), (0, 0), (0, 0))).reshape(b * dil, nblk + 1, BLK, h, dh)
        return jnp.concatenate([tp[:, :-1], tp[:, 1:]], axis=2)

    kb, vb = kv_blocks(kr), kv_blocks(vr)
    logits = jnp.einsum('bnqhd,bnkhd->bnhqk', qb, kb).astype(jnp.float32) * (HEAD_DIM ** -0.5)
    qi = jnp.arange(BLK)[:, None]
    kj = jnp.arange(2 * BLK)[None, :]
    rel = BLK + qi - kj
    bias = rel_bias[_t5_bucket(jnp.maximum(rel, 0) * dil)]
    logits = logits + bias.transpose(2, 0, 1).astype(jnp.float32)[None, None]
    kpos = jnp.arange(nblk)[:, None, None] * BLK - BLK + kj[None]
    valid = (rel >= 0)[None] & (rel <= w_sub)[None] & (kpos >= 0)
    logits = jnp.where(valid[None, :, None], logits, NEG)
    m = jnp.max(logits, axis=-1, keepdims=True)
    p = jnp.exp(logits - m)
    denom = jnp.sum(p, axis=-1, keepdims=True)
    o = jnp.einsum('bnhqk,bnkhd->bnqhd', p, vb.astype(jnp.float32)) / denom.transpose(0, 1, 3, 2, 4)
    lse = (m + jnp.log(denom))[..., 0].transpose(0, 1, 3, 2)
    o = o.reshape(b * dil, Lp, h, dh)[:, :L].reshape(b, dil, L, h, dh).transpose(0, 2, 1, 3, 4).reshape(b, s, h, dh)
    lse = lse.reshape(b * dil, Lp, h)[:, :L].reshape(b, dil, L, h).transpose(0, 2, 1, 3).reshape(b, s, h)
    return o, lse

def _spatial_gating(u, va, norm_w, w_s, b_s):
    b, s, _ = u.shape
    nc = s // CHUNK
    u = u.reshape(b, nc, CHUNK, SGU_GROUPS, SGU_CH)
    va = _rms(va.reshape(b, nc, CHUNK, SGU_GROUPS, SGU_CH), norm_w)
    w_masked = w_s * jnp.tril(jnp.ones((CHUNK, CHUNK), w_s.dtype))[None]
    spatial = jnp.einsum('gts,bnsgc->bntgc', w_masked, va) + b_s.T[None, None, :, :, None]
    return (u * spatial).reshape(b, s, D_SGU)

def _peer(xn, w_query, keys1, keys2, u_tab, v_tab):
    b, s, d = xn.shape
    t = b * s
    half = PEER_D_KEY // 2
    xf = xn.reshape(t, d)
    q = (xf @ w_query).reshape(t, PEER_HEADS, PEER_D_KEY)
    s1 = jnp.einsum('thd,hkd->thk', q[..., :half], keys1).astype(jnp.float32)
    s2 = jnp.einsum('thd,hkd->thk', q[..., half:], keys2).astype(jnp.float32)
    v1, i1 = lax.top_k(s1, PEER_TOPK)
    v2, i2 = lax.top_k(s2, PEER_TOPK)
    cand = (v1[..., :, None] + v2[..., None, :]).reshape(t, PEER_HEADS, PEER_TOPK * PEER_TOPK)
    cidx = (i1[..., :, None] * PEER_KEYS + i2[..., None, :]).reshape(t, PEER_HEADS, PEER_TOPK * PEER_TOPK)
    best, pos = lax.top_k(cand, PEER_TOPK)
    idx = jnp.take_along_axis(cidx, pos, axis=-1)
    gate = jax.nn.softmax(best, axis=-1)
    n_chunks = t // PEER_CHUNK
    n_sel = PEER_HEADS * PEER_TOPK

    def expert_block(args):
        xc, ic, gc = args
        u = jnp.take(u_tab, ic, axis=0)
        act = jax.nn.gelu(jnp.einsum('cd,ced->ce', xc, u).astype(jnp.float32))
        vv = jnp.take(v_tab, ic, axis=0)
        return jnp.einsum('ce,ced->cd', gc * act, vv.astype(jnp.float32)).astype(xc.dtype)

    y = lax.map(expert_block, (xf.reshape(n_chunks, PEER_CHUNK, d),
                               idx.reshape(n_chunks, PEER_CHUNK, n_sel),
                               gate.reshape(n_chunks, PEER_CHUNK, n_sel)))
    return y.reshape(b, s, d)

def setup_inputs(seed: int = 0) -> dict:
    key = jax.random.key(seed)
    ks = jax.random.split(key, 20)
    f32 = jnp.float32
    nrm = lambda k, shape, scale: jax.random.normal(k, shape, f32) * scale
    gain = lambda k, shape: 1.0 + 0.05 * jax.random.normal(k, shape, f32)
    return {
        "x": nrm(ks[0], (BATCH, SEQ, D_MODEL), 1.0),
        "ln1_w": gain(ks[1], (DEPTH, D_MODEL)),
        "w_in": nrm(ks[2], (DEPTH, D_MODEL, D_IN_PROJ), D_MODEL ** -0.5),
        "q_norm_w": gain(ks[3], (DEPTH, HEAD_DIM)),
        "k_norm_w": gain(ks[4], (DEPTH, HEAD_DIM)),
        "sgu_norm_w": gain(ks[5], (DEPTH, SGU_GROUPS, SGU_CH)),
        "sgu_w": nrm(ks[6], (DEPTH, SGU_GROUPS, CHUNK, CHUNK), CHUNK ** -0.5),
        "sgu_b": gain(ks[7], (DEPTH, SGU_GROUPS, CHUNK)),
        "mix_norm_w": gain(ks[8], (DEPTH, D_MIX)),
        "w_out": nrm(ks[9], (DEPTH, D_MIX, D_MODEL), D_MIX ** -0.5),
        "ln2_w": gain(ks[10], (DEPTH, D_MODEL)),
        "peer_w_query": nrm(ks[11], (DEPTH, D_MODEL, PEER_HEADS * PEER_D_KEY), D_MODEL ** -0.5),
        "peer_keys1": nrm(ks[12], (DEPTH, PEER_HEADS, PEER_KEYS, PEER_D_KEY // 2), (PEER_D_KEY // 2) ** -0.5),
        "peer_keys2": nrm(ks[13], (DEPTH, PEER_HEADS, PEER_KEYS, PEER_D_KEY // 2), (PEER_D_KEY // 2) ** -0.5),
        "peer_u": nrm(ks[14], (DEPTH, PEER_EXPERTS, D_MODEL), D_MODEL ** -0.5),
        "peer_v": nrm(ks[15], (DEPTH, PEER_EXPERTS, D_MODEL), D_MODEL ** -0.5),
        "rel_bias": nrm(ks[16], (NUM_BUCKETS, ATTN_HEADS), 0.1),
    }

def reference(x, ln1_w, w_in, q_norm_w, k_norm_w, sgu_norm_w, sgu_w, sgu_b, mix_norm_w, w_out,
              ln2_w, peer_w_query, peer_keys1, peer_keys2, peer_u, peer_v, rel_bias):
    b, s, _ = x.shape
    for l in range(DEPTH):
        h = _rms(x, ln1_w[l])
        proj = h @ w_in[l]
        q = proj[..., 0:D_ATTN].reshape(b, s, ATTN_HEADS, HEAD_DIM)
        k = proj[..., D_ATTN:2 * D_ATTN].reshape(b, s, ATTN_HEADS, HEAD_DIM)
        v = proj[..., 2 * D_ATTN:3 * D_ATTN].reshape(b, s, ATTN_HEADS, HEAD_DIM)
        ua = jax.nn.gelu(proj[..., 3 * D_ATTN:3 * D_ATTN + D_SGU])
        va = jax.nn.gelu(proj[..., 3 * D_ATTN + D_SGU:])
        q = _rms(q, q_norm_w[l])
        k = _rms(k, k_norm_w[l])
        outs, lses = [], []
        for window, dil in DILATED:
            o_p, lse_p = _dilated_window_attention(q, k, v, rel_bias, window, dil)
            outs.append(o_p)
            lses.append(lse_p)
        wts = jax.nn.softmax(jnp.stack(lses, axis=0), axis=0)
        attn = jnp.sum(wts[..., None] * jnp.stack(outs, axis=0), axis=0)
        attn = attn.astype(x.dtype).reshape(b, s, D_ATTN)
        sgu = _spatial_gating(ua, va, sgu_norm_w[l], sgu_w[l], sgu_b[l])
        mix = jnp.concatenate([_rms(attn, mix_norm_w[l, :D_ATTN]),
                               _rms(sgu, mix_norm_w[l, D_ATTN:])], axis=-1)
        x = x + mix @ w_out[l]
        hn = _rms(x, ln2_w[l])
        x = x + _peer(hn, peer_w_query[l], peer_keys1[l], peer_keys2[l], peer_u[l], peer_v[l])
    return x


_drawn_inputs = setup_inputs


def setup_inputs(seed=0):
    import zlib

    import numpy as np

    out = dict(_drawn_inputs(seed))
    spreads = {}
    factors = {'sgu_norm_w': 3.97,
     'sgu_b': 2.968,
     'ln2_w': 8.0,
     'peer_w_query': 5.271,
     'peer_keys1': 5.353,
     'peer_keys2': 5.377,
     'peer_u': 5.821,
     'peer_v': 5.243}
    for name, (base, spread) in spreads.items():
        noise = np.random.default_rng([zlib.crc32(name.encode()), seed]).standard_normal(out[name].shape)
        drawn = base * np.exp(spread * noise) if base else spread * noise
        out[name] = __import__('jax').numpy.asarray(drawn.astype(out[name].dtype))
    for name, factor in factors.items():
        out[name] = (out[name] * factor).astype(out[name].dtype)
    return out
```

```python
from contextlib import ExitStack

import numpy as np
import concourse.bass as bass
from concourse import mybir

F32 = mybir.dt.float32
BF16 = mybir.dt.bfloat16
U32 = mybir.dt.uint32
ALU = mybir.AluOpType
ACT = mybir.ActivationFunctionType
AX_X = mybir.AxisListType.X

P = 128
SEQ = 1024
D = 1024
NT = SEQ // P
NK = D // P
HEADS = 8
DH = 64
DA = HEADS * DH
GROUPS = 4
D_IN = 5 * DA
NPROJ = D_IN // 512
EPS = 1e-6
NEG = -1e30
BUCKETS = 32
PH = 8
TOPK = 16
KEYS = 128
HALVES = 2 * PH
LOWEST = -3.0e38
BIAS_LEN = SEQ + P
GROUP = 4
NGROUP = KEYS // GROUP
TG = 32
BANK = 512


def patterns(distance):
    r = distance
    return sum(((r >= 0) & (r <= w) & (r % d == 0)).astype(np.int64) for w, d in ((128, 1), (512, 4), (2048, 16)))


def shape_constants():
    r = (SEQ - 1) - np.arange(BIAS_LEN)
    d = np.maximum(r, 0)
    exact = BUCKETS // 2
    large = exact + (np.log(np.maximum(d, exact).astype(np.float32) / np.float32(exact))
                     / np.float32(np.log(2048 / exact)) * np.float32(BUCKETS - exact)).astype(np.int32)
    bucket = np.where(d < exact, d, np.minimum(large, BUCKETS - 1))
    count = patterns(r)
    table = np.zeros((BUCKETS + 1, BIAS_LEN), np.float32)
    table[bucket, np.arange(BIAS_LEN)] = 1.0
    table[BUCKETS] = np.where(count > 0, np.log(np.maximum(count, 1)), NEG)
    ident = np.eye(P, dtype=np.float32)
    return {"bias_table": table, "ident": ident, "flip": np.ascontiguousarray(ident[::-1])}


class Steps:

    def __init__(self, engine, sem):
        self.engine, self.sem, self.count = engine, sem, 0

    def __call__(self, instruction):
        self.count += 1
        instruction.then_inc(self.sem, 1)
        return self.count

    def done(self, upto=None):
        self.engine.wait_ge(self.sem, self.count if upto is None else upto)


def input_projection(nc, dram, keep):
    with ExitStack() as ctx:
        sb = lambda name, shape, dt=F32: ctx.enter_context(nc.sbuf_tensor(name, shape, dt))
        sem = lambda name: ctx.enter_context(nc.semaphore(name))
        xs = keep["wide"].rearrange("p (k t) -> p k t", t=SEQ)
        w = sb("w_in", [P, 2, NK, 512])
        junk = sb("square_junk", [P, D])
        ssq, ms, rms, rstd = (sb(f"ln1_{n}", [P, NT]) for n in ("ssq", "ms", "inv", "rstd"))
        ln1 = sb("ln1", [P, NK])
        acc = [ctx.enter_context(nc.psum_tensor(f"proj_acc{b}", [P, BANK], F32)) for b in range(8)]
        x_in, xT_in, ln1_in = sem("x_loaded"), sem("xT_loaded"), sem("ln1_loaded")
        w_in = [sem("w_in_loaded0"), sem("w_in_loaded1")]
        ssq_ready, ms_ready, inv_ready, rstd_ready = sem("ssq_ready"), sem("ms_ready"), sem("inv_ready"), sem("rstd_ready")
        xs_ready, proj_ready, proj_read_v, proj_read_a = sem("xs_ready"), sem("proj_ready"), sem("proj_read_v"), sem("proj_read_a")
        x_sb, outs = keep["x"], [keep[n] for n in ("q", "k", "v", "u", "va")]
        w_dram = dram["w_in"].rearrange("(k p) n -> p k n", p=P)
        block = ctx.enter_context(nc.Block())

        @block.sync
        def _(sp):
            sp.dma_start(keep["ident"][:], dram["ident"]).then_inc(ln1_in, 16)
            sp.dma_start(ln1[:], dram["ln1"]).then_inc(ln1_in, 16)
            sp.dma_start(xs[:], dram["xT"].rearrange("(k p) t -> p k t", p=P)).then_inc(xT_in, 16)
            for n in range(NPROJ):
                if n >= 2:
                    sp.wait_ge(proj_ready, NT * (n - 1))
                sp.dma_start(w[:, n % 2], w_dram[:, :, n * 512:(n + 1) * 512]).then_inc(w_in[n % 2], 16)

        @block.gpsimd
        def _(pool):
            pool.dma_start(x_sb[:], dram["x"].rearrange("(i p) d -> p i d", p=P)).then_inc(x_in, 16)

        @block.vector
        def _(dve):
            dve.wait_ge(ln1_in, 32)
            dve.wait_ge(xT_in, 16)
            for k in range(NK):
                dve.tensor_scalar(xs[:, k], xs[:, k], ln1[:, k:k + 1], None, ALU.mult).then_inc(xs_ready, 1)
            dve.wait_ge(ssq_ready, NT)
            dve.tensor_scalar(ms[:], ssq[:], 1.0 / D, EPS, ALU.mult, ALU.add).then_inc(ms_ready, 1)
            dve.wait_ge(ms_ready, 1)
            dve.reciprocal(rms[:], ms[:]).then_inc(inv_ready, 1)
            dve.wait_ge(rstd_ready, 1)
            for n in (0, 1):
                for i in range(NT):
                    g = n * NT + i
                    dve.wait_ge(proj_ready, g + 1)
                    dve.tensor_scalar(outs[n][:, i], acc[g % 8][:], rstd[:, i:i + 1], None, ALU.mult).then_inc(proj_read_v, 1)

        @block.scalar
        def _(act):
            act.wait_ge(x_in, 16)
            for i in range(NT):
                if i:
                    act.wait_ge(ssq_ready, i)
                act.activation(junk[:], x_sb[:, i], ACT.Square, accum_out=ssq[:, i:i + 1]).then_inc(ssq_ready, 1)
            act.wait_ge(inv_ready, 1)
            act.activation(rstd[:], rms[:], ACT.Sqrt).then_inc(rstd_ready, 1)
            act.wait_ge(rstd_ready, 1)
            for n in (2, 3, 4):
                for i in range(NT):
                    g = n * NT + i
                    act.wait_ge(proj_ready, g + 1)
                    act.activation(outs[n][:, i], acc[g % 8][:], ACT.Copy if n == 2 else ACT.Gelu_apprx_tanh,
                                   scale=rstd[:, i:i + 1]).then_inc(proj_read_a, 1)

        @block.tensor
        def _(pe):
            pe.wait_ge(xs_ready, NK)
            for n in range(NPROJ):
                pe.wait_ge(w_in[n % 2], 16 * (n // 2 + 1))
                for i in range(NT):
                    g = n * NT + i
                    if 8 <= g < 24:
                        pe.wait_ge(proj_read_v, g - 7)
                    elif g >= 24:
                        pe.wait_ge(proj_read_a, g - 7 - 16)
                    for k in range(NK):
                        last = pe.matmul(acc[g % 8][:], xs[:, k, i * P:(i + 1) * P], w[:, n % 2, k], start=(k == 0), stop=(k == NK - 1))
                    last.then_inc(proj_ready, 1)


def attention_and_gating(nc, dram, keep):
    with ExitStack() as ctx:
        sb = lambda name, shape, dt=F32: ctx.enter_context(nc.sbuf_tensor(name, shape, dt))
        sem = lambda name: ctx.enter_context(nc.semaphore(name))
        psum = lambda name: ctx.enter_context(nc.psum_tensor(name, [P, BANK], F32))
        q, k, v, u, va = (keep[n] for n in ("q", "k", "v", "u", "va"))
        ident = keep["ident"]
        qT, kT = sb("qT", [P, 4, SEQ]), sb("kT", [P, 4, SEQ])
        wide = keep["wide"].rearrange("p (h t) -> p h t", t=SEQ)
        square = keep["wide"][:, 0:NT * DA]
        logits = sb("logits", [P, 2, SEQ])
        probs = logits
        probsT = sb("probsT", [P, 2, SEQ])
        flip = sb("flip", [P, P])
        table = logits[0:BUCKETS + 1].rearrange("p a s -> p (a s)")[:, 0:BIAS_LEN]
        bias_sb = probsT[0:HEADS].rearrange("p a s -> p (a s)")[:, 0:BIAS_LEN]
        relb = sb("rel_bias", [BUCKETS + 1, HEADS])
        qw, kw = sb("q_norm_w", [P, 1]), sb("k_norm_w", [P, 1])
        hs = [sb(f"head_ssq{n}", [P, NT * HEADS]) for n in range(3)]
        sw = sb("sgu_w", [P, GROUPS, P])
        sgn = sb("sgu_norm", [P, DA])
        sgb = sb("sgu_b", [P, GROUPS])
        mx, nmx, den, rden = (sb(f"row_{n}", [P, NT * HEADS]) for n in ("max", "neg_max", "sum", "inv_sum"))
        s_ps = [ctx.enter_context(nc.psum_tensor(f"scores{b}", [P, 2 * BANK], F32)) for b in range(2)]
        t_ps = [psum("turned0"), psum("turned1")]
        o_ps = [psum("out0"), psum("out1")]
        small_in, bias_out, bias_in = sem("small_loaded"), sem("bias_stored"), sem("bias_loaded")
        sgu_in = sem("sgu_loaded")
        dv, ac = sem("dve_steps"), sem("act_steps")
        inv_ready, std_ready, normed = sem("head_inv"), sem("head_rstd"), sem("qkv_normed")
        turned, turned_read = sem("qk_turned"), sem("qk_turned_read")
        row_ready, row_read = sem("bias_row_ready"), sem("bias_row_read")
        flipped, flipped_read = sem("bias_flipped"), sem("bias_flipped_read")
        scored, biased, exped, nmax_ready = sem("scored"), sem("biased"), sem("exped"), sem("neg_max_ready")
        pt_ready, pt_read, pv_ready, pv_read = sem("probs_turned"), sem("probs_turned_read"), sem("pv_ready"), sem("pv_read")
        masked, mixed, gated = sem("sgu_w_masked"), sem("spatial_ready"), sem("spatial_read")
        ones_row = sem("ones_row_ready")
        block = ctx.enter_context(nc.Block())
        units = [(h, i) for h in range(HEADS) for i in range(NT)]
        scratch = dram["bias_scratch"]

        @block.sync
        def _(sp):
            for dst, src in ((flip[:], dram["flip"]), (table, dram["bias_table"]), (relb[0:BUCKETS], dram["rel_bias"]),
                             (qw[0:DH], dram["q_norm_w"]), (qw[DH:P], dram["q_norm_w"]),
                             (kw[0:DH], dram["k_norm_w"]), (kw[DH:P], dram["k_norm_w"])):
                sp.dma_start(dst, src).then_inc(small_in, 16)
            for dst, src in ((sw[:], dram["sgu_wT"]), (sgn[:], dram["sgu_norm_w"].to_broadcast([P, DA])), (sgb[:], dram["sgu_b"])):
                sp.dma_start(dst, src).then_inc(sgu_in, 16)
            sp.wait_ge(row_read, 3)
            sp.dma_start(scratch, bias_sb).then_inc(bias_out, 16)
            sp.wait_ge(bias_out, 16)
            sp.wait_ge(normed, 3)
            skewed = bass.AP(scratch.tensor, scratch.offset, [[1, P], [BIAS_LEN, HEADS], [1, SEQ]])
            sp.dma_start(wide, skewed).then_inc(bias_in, 16)

        @block.gpsimd
        def _(pool):
            pool.memset(relb[BUCKETS:BUCKETS + 1], 1.0).then_inc(ones_row, 1)
            pool.wait_ge(ones_row, 1)
            pool.wait_ge(sgu_in, 48)
            pool.affine_select(out=sw[:], in_=sw[:], compare_op=ALU.is_ge, fill=0.0, base=0,
                               pattern=[[0, GROUPS], [1, P]], channel_multiplier=-1).then_inc(masked, 1)

        @block.vector
        def _(dve):
            own = Steps(dve, dv)

            def norm(n, t, width, dim):
                runs = t.rearrange("p i (h d) -> p (i h) d", d=dim)
                nrun = NT * width // dim
                sq = square.rearrange("p (r d) -> p r d", d=dim)
                own(dve.tensor_tensor(sq, runs, runs, ALU.mult))
                own.done()
                own(dve.tensor_reduce(hs[n][:, 0:nrun], sq, AX_X, ALU.add))
                own.done()
                own(dve.tensor_scalar(hs[n][:, 0:nrun], hs[n][:, 0:nrun], 1.0 / dim, EPS, ALU.mult, ALU.add))
                own.done()
                dve.reciprocal(hs[n][:, 0:nrun], hs[n][:, 0:nrun]).then_inc(inv_ready, 1)
                dve.wait_ge(std_ready, n + 1)
                last = dve.tensor_tensor(runs, runs, hs[n][:, 0:nrun].unsqueeze(2).broadcast_to([P, nrun, dim]), ALU.mult)
                last.then_inc(normed, 1)

            norm(0, q, DA, DH)
            norm(1, k, DA, DH)
            norm(2, va, DA, P)
            dve.wait_ge(normed, 3)
            dve.wait_ge(sgu_in, 48)
            own(dve.tensor_tensor(va[:], va[:], sgn[:].unsqueeze(1).broadcast_to([P, NT, DA]), ALU.mult))
            for c in range(3):
                dve.wait_ge(row_ready, c + 1)
                dve.tensor_copy(bias_sb[:, c * 384:(c + 1) * 384], s_ps[0][0:HEADS, 0:384] if c == 0 else
                                (s_ps[0][0:HEADS, BANK:BANK + 384] if c == 1 else s_ps[1][0:HEADS, 0:384])).then_inc(row_read, 1)
            dve.wait_ge(small_in, 16 * 7)
            for n in range(16):
                t, pair, half = n // 8, (n // 2) % 4, n % 2
                dve.wait_ge(turned, n + 1)
                dst = (qT if t == 0 else kT)[:, pair, half * 512:(half + 1) * 512]
                dve.tensor_scalar(dst, t_ps[n % 2][:], (qw if t == 0 else kw)[:, 0:1], DH ** -0.5 if t == 0 else 1.0,
                                  ALU.mult, ALU.mult).then_inc(turned_read, 1)
            for n in range(16):
                dve.wait_ge(flipped, n + 1)
                dve.tensor_copy(wide[:, n // 2, (n % 2) * 512:(n % 2 + 1) * 512], s_ps[n % 2][:, 0:BANK]).then_inc(flipped_read, 1)
            dve.wait_ge(flipped_read, 16)

            def add_bias(n):
                h, i = units[n]
                w = (i + 1) * P
                dve.wait_ge(scored, n + 1)
                if n >= 2:
                    dve.wait_ge(exped, n - 1)
                dve.tensor_tensor_reduce(logits[:, n % 2, 0:w], s_ps[n % 2][:, 0:w], wide[:, h, SEQ - w:SEQ], 1.0, LOWEST,
                                         ALU.add, ALU.max, mx[:, n:n + 1]).then_inc(biased, 1)
                dve.wait_ge(biased, n + 1)
                dve.tensor_scalar(nmx[:, n:n + 1], mx[:, n:n + 1], -1.0, None, ALU.mult).then_inc(nmax_ready, 1)

            def out(n):
                h, i = units[n]
                dve.wait_ge(exped, n + 1)
                own(dve.reciprocal(rden[:, n:n + 1], den[:, n:n + 1]))
                own.done()
                dve.wait_ge(pv_ready, n + 1)
                dve.tensor_scalar(q[:, i, h * DH:(h + 1) * DH], o_ps[n % 2][:, 0:DH], rden[:, n:n + 1], None, ALU.mult).then_inc(pv_read, 1)

            add_bias(0)
            for n in range(len(units)):
                if n + 1 < len(units):
                    add_bias(n + 1)
                if n >= 1:
                    out(n - 1)
            out(len(units) - 1)
            for n in range(NT * GROUPS):
                i, g = n // GROUPS, n % GROUPS
                dve.wait_ge(mixed, n + 1)
                cols = slice(g * P, (g + 1) * P)
                dve.scalar_tensor_tensor(out=u[:, i, cols], in0=t_ps[n % 2][:, 0:P], scalar=sgb[:, g:g + 1], in1=u[:, i, cols],
                                         op0=ALU.add, op1=ALU.mult).then_inc(gated, 1)

        @block.scalar
        def _(act):
            own = Steps(act, ac)
            for n in range(3):
                act.wait_ge(inv_ready, n + 1)
                c = NT * HEADS if n < 2 else NT * GROUPS
                act.activation(hs[n][:, 0:c], hs[n][:, 0:c], ACT.Sqrt).then_inc(std_ready, 1)
            turns = 0
            for n, (h, i) in enumerate(units):
                w = (i + 1) * P
                act.wait_ge(nmax_ready, n + 1)
                act.wait_ge(biased, n + 1)
                act.activation(probs[:, n % 2, 0:w], logits[:, n % 2, 0:w], ACT.Exp, bias=nmx[:, n:n + 1],
                               accum_out=den[:, n:n + 1]).then_inc(exped, 1)
                if n >= 2:
                    act.wait_ge(pv_ready, n - 1)
                for c in range(0, i + 1, 4):
                    m = min(4, i + 1 - c)
                    act.wait_ge(pt_ready, turns + 1)
                    act.activation(probsT[:, n % 2, c * P:(c + m) * P], t_ps[turns % 2][:, 0:m * P], ACT.Copy).then_inc(pt_read, 1)
                    turns += 1

        @block.tensor
        def _(pe):
            pe.wait_ge(small_in, 16 * 7)
            pe.wait_ge(ones_row, 1)
            for c in range(3):
                dst = s_ps[c // 2][0:HEADS, (c % 2) * BANK:(c % 2) * BANK + 384]
                pe.matmul(dst, relb[:], table[:, c * 384:(c + 1) * 384], start=True, stop=True).then_inc(row_ready, 1)
            for n in range(16):
                t, pair, half = n // 8, (n // 2) % 4, n % 2
                pe.wait_ge(normed, t + 1)
                if n >= 2:
                    pe.wait_ge(turned_read, n - 1)
                for j in range(4):
                    last = pe.transpose(t_ps[n % 2][:, j * P:(j + 1) * P], (q if t == 0 else k)[:, half * 4 + j, pair * P:(pair + 1) * P], ident[:])
                last.then_inc(turned, 1)
            pe.wait_ge(turned_read, 16)
            pe.wait_ge(bias_in, 16)
            pe.wait_ge(row_read, 3)
            for n in range(16):
                if n >= 2:
                    pe.wait_ge(flipped_read, n - 1)
                pe.matmul(s_ps[n % 2][:, 0:BANK], flip[:], wide[:, n // 2, (n % 2) * 512:(n % 2 + 1) * 512],
                          start=True, stop=True).then_inc(flipped, 1)
            pe.wait_ge(flipped_read, 16)

            def scores(n):
                h, i = units[n]
                base, w = DH * (h % 2), (i + 1) * P
                if n >= 2:
                    pe.wait_ge(biased, n - 1)
                for c in range(0, w, BANK):
                    m = min(BANK, w - c)
                    last = pe.matmul(s_ps[n % 2][:, c:c + m], qT[base:base + DH, h // 2, i * P:(i + 1) * P],
                                     kT[base:base + DH, h // 2, c:c + m], start=True, stop=True)
                last.then_inc(scored, 1)

            turns = 0
            scores(0)
            for n, (h, i) in enumerate(units):
                if n + 1 < len(units):
                    scores(n + 1)
                pe.wait_ge(exped, n + 1)
                for c in range(0, i + 1, 4):
                    m = min(4, i + 1 - c)
                    if turns >= 2:
                        pe.wait_ge(pt_read, turns - 1)
                    for j in range(m):
                        last = pe.transpose(t_ps[turns % 2][:, j * P:(j + 1) * P], probs[:, n % 2, (c + j) * P:(c + j + 1) * P], ident[:])
                    last.then_inc(pt_ready, 1)
                    turns += 1
                pe.wait_ge(pt_read, turns)
                if n >= 2:
                    pe.wait_ge(pv_read, n - 1)
                for j in range(i + 1):
                    last = pe.matmul(o_ps[n % 2][:, 0:DH], probsT[:, n % 2, j * P:(j + 1) * P], v[:, j, h * DH:(h + 1) * DH],
                                     start=(j == 0), stop=(j == i))
                last.then_inc(pv_ready, 1)
            pe.wait_ge(masked, 1)
            for n in range(NT * GROUPS):
                i, g = n // GROUPS, n % GROUPS
                if n >= 2:
                    pe.wait_ge(gated, n - 1)
                pe.matmul(t_ps[n % 2][:, 0:P], sw[:, g], va[:, i, g * P:(g + 1) * P], start=True, stop=True).then_inc(mixed, 1)


def output_projection(nc, dram, keep):
    with ExitStack() as ctx:
        sb = lambda name, shape, dt=F32: ctx.enter_context(nc.sbuf_tensor(name, shape, dt))
        sem = lambda name: ctx.enter_context(nc.semaphore(name))
        x_sb, attn, gate, ident = keep["x"], keep["q"], keep["u"], keep["ident"]
        hnT = keep["hnT"]
        mixT = sb("mixT", [P, 2, NK, P])
        w = sb("w_out", [P, NK, D])
        junk = sb("square_junk2", [P, D])
        hn = sb("hn", [P, 2, D])
        mw, ln2 = sb("mix_norm_w", [P, NK]), sb("ln2", [P, NK])
        ssq, rstd = sb("mix_ssq", [P, 2 * NT]), sb("mix_rstd", [P, 2 * NT])
        ssq2, rstd2 = sb("ln2_ssq", [P, NT]), sb("ln2_rstd", [P, NT])
        turn_ps = [ctx.enter_context(nc.psum_tensor(f"mix_turn{b}", [P, BANK], F32)) for b in range(4)]
        out_ps = [ctx.enter_context(nc.psum_tensor(f"mix_out{b}", [P, BANK], F32)) for b in range(4)]
        w_in, small_in = sem("w_out_loaded"), sem("norms_loaded")
        dv = sem("dve_steps_o")
        ssq_ready, inv_ready, rstd_ready, scaled = sem("mix_ssq_ready"), sem("mix_inv_ready"), sem("mix_rstd_ready"), sem("mix_scaled")
        turned, turned_read, out_ready, added = sem("mix_turned"), sem("mix_turned_read"), sem("mix_product"), sem("x2_ready")
        ssq2_ready, inv2_ready, rstd2_ready = sem("x2_ssq_ready"), sem("x2_inv_ready"), sem("x2_rstd_ready")
        hn_ready, hn_turned, hn_read, hi_ready = sem("hn_ready"), sem("hn_turned"), sem("hn_turned_read"), sem("hn_hi_ready")
        block = ctx.enter_context(nc.Block())

        @block.sync
        def _(sp):
            sp.dma_start(mw[:], dram["mix_norm_w"]).then_inc(small_in, 16)
            sp.dma_start(ln2[:], dram["ln2"]).then_inc(small_in, 16)
            sp.dma_start(w[:], dram["w_out"].rearrange("(k p) n -> p k n", p=P)).then_inc(w_in, 16)

        @block.vector
        def _(dve):
            own = Steps(dve, dv)
            dve.wait_ge(small_in, 32)
            dve.wait_ge(ssq_ready, 2 * NT)
            own(dve.tensor_scalar(ssq[:], ssq[:], 1.0 / DA, EPS, ALU.mult, ALU.add))
            own.done()
            dve.reciprocal(ssq[:], ssq[:]).then_inc(inv_ready, 1)
            dve.wait_ge(rstd_ready, 1)

            def scale(i):
                dve.tensor_scalar(attn[:, i], attn[:, i], rstd[:, 2 * i:2 * i + 1], None, ALU.mult).then_inc(scaled, 1)
                dve.tensor_scalar(gate[:, i], gate[:, i], rstd[:, 2 * i + 1:2 * i + 2], None, ALU.mult).then_inc(scaled, 1)

            def mix_turned(i):
                if i >= 2:
                    dve.wait_ge(out_ready, 2 * (i - 1))
                for k in range(NK):
                    if k % 4 == 0:
                        dve.wait_ge(turned, 2 * i + k // 4 + 1)
                    last = dve.tensor_scalar(mixT[:, i % 2, k], turn_ps[2 * (i % 2) + k // 4][:, (k % 4) * P:(k % 4 + 1) * P],
                                             mw[:, k:k + 1], None, ALU.mult)
                    if k % 4 == 3:
                        last.then_inc(turned_read, 1)

            def residual(i):
                for c in range(2):
                    dve.wait_ge(out_ready, 2 * i + c + 1)
                    dve.tensor_tensor(x_sb[:, i, c * 512:(c + 1) * 512], x_sb[:, i, c * 512:(c + 1) * 512],
                                      out_ps[2 * (i % 2) + c][:], ALU.add).then_inc(added, 1)

            def inverse(i):
                dve.wait_ge(ssq2_ready, i + 1)
                own(dve.tensor_scalar(ssq2[:, i:i + 1], ssq2[:, i:i + 1], 1.0 / D, EPS, ALU.mult, ALU.add))
                own.done()
                dve.reciprocal(ssq2[:, i:i + 1], ssq2[:, i:i + 1]).then_inc(inv2_ready, 1)
                dve.wait_ge(rstd2_ready, i + 1)
                if i >= 2:
                    dve.wait_ge(hn_turned, 2 * (i - 1))
                dve.tensor_scalar(hn[:, i % 2], x_sb[:, i], rstd2[:, i:i + 1], None, ALU.mult).then_inc(hn_ready, 1)

            def hn_out(i):
                cols = slice(i * P, (i + 1) * P)
                for k in range(NK):
                    if k % 4 == 0:
                        dve.wait_ge(hn_turned, 2 * i + k // 4 + 1)
                    last = dve.tensor_scalar(hnT[:, k, cols], out_ps[2 * (i % 2) + k // 4][:, (k % 4) * P:(k % 4 + 1) * P],
                                             ln2[:, k:k + 1], None, ALU.mult)
                    if k % 4 == 3:
                        last.then_inc(hn_read, 1)

            for i in range(NT):
                scale(i)
            mix_turned(0)
            for i in range(NT):
                residual(i)
                if i + 1 < NT:
                    mix_turned(i + 1)
                inverse(i)
                hn_out(i)

        @block.scalar
        def _(act):
            for i in range(NT):
                for n, t in enumerate((attn, gate)):
                    if i or n:
                        act.wait_ge(ssq_ready, 2 * i + n)
                    act.activation(junk[:, 0:DA], t[:, i], ACT.Square, accum_out=ssq[:, 2 * i + n:2 * i + n + 1]).then_inc(ssq_ready, 1)
            act.wait_ge(inv_ready, 1)
            act.activation(rstd[:], ssq[:], ACT.Sqrt).then_inc(rstd_ready, 1)
            for i in range(NT):
                act.wait_ge(added, 2 * i + 2)
                act.wait_ge(ssq_ready, 2 * NT)
                if i:
                    act.wait_ge(ssq2_ready, i)
                act.activation(junk[:], x_sb[:, i], ACT.Square, accum_out=ssq2[:, i:i + 1]).then_inc(ssq2_ready, 1)
                act.wait_ge(inv2_ready, i + 1)
                act.activation(rstd2[:, i:i + 1], ssq2[:, i:i + 1], ACT.Sqrt).then_inc(rstd2_ready, 1)

        @block.tensor
        def _(pe):
            def turn_mix(i):
                pe.wait_ge(scaled, 2 * (i + 1))
                if i >= 2:
                    pe.wait_ge(turned_read, 2 * (i - 1))
                for k in range(NK):
                    src = attn if k < 4 else gate
                    last = pe.transpose(turn_ps[2 * (i % 2) + k // 4][:, (k % 4) * P:(k % 4 + 1) * P], src[:, i, (k % 4) * P:(k % 4 + 1) * P], ident[:])
                    if k % 4 == 3:
                        last.then_inc(turned, 1)

            def project(i):
                pe.wait_ge(turned_read, 2 * (i + 1))
                if i >= 2:
                    pe.wait_ge(hn_read, 2 * (i - 1))
                for c in range(2):
                    for k in range(NK):
                        last = pe.matmul(out_ps[2 * (i % 2) + c][:], mixT[:, i % 2, k], w[:, k, c * 512:(c + 1) * 512],
                                         start=(k == 0), stop=(k == NK - 1))
                    last.then_inc(out_ready, 1)

            def turn_hn(i):
                pe.wait_ge(hn_ready, i + 1)
                pe.wait_ge(added, 2 * (i + 1))
                for k in range(NK):
                    last = pe.transpose(out_ps[2 * (i % 2) + k // 4][:, (k % 4) * P:(k % 4 + 1) * P], hn[:, i % 2, k * P:(k + 1) * P], ident[:])
                    if k % 4 == 3:
                        last.then_inc(hn_turned, 1)

            turn_mix(0)
            pe.wait_ge(w_in, 16)
            for i in range(NT):
                project(i)
                if i + 1 < NT:
                    turn_mix(i + 1)
                turn_hn(i)


def retrieval(nc, dram, keep):
    with ExitStack() as ctx:
        sb = lambda name, shape, dt=F32: ctx.enter_context(nc.sbuf_tensor(name, shape, dt))
        sem = lambda name: ctx.enter_context(nc.semaphore(name))
        hnT, ident = keep["hnT"], keep["ident"]
        wq = sb("w_query", [P, NK, HALVES * P])
        keys = sb("keysT", [P, HALVES, KEYS])
        qT = sb("queryT", [P, HALVES, P])
        rest = sb("scores_left", [P, HALVES, KEYS])
        top = sb("top_values", [P, HALVES, TOPK])
        topi = sb("top_index", [P, HALVES, TOPK], U32)
        topf = sb("top_index_bf16", [P, HALVES, TOPK], BF16)
        cand = sb("candidates", [P, PH, TOPK * TOPK])
        cand2 = sb("candidates_left", [P, PH, TOPK * TOPK])
        best = sb("best", [P, PH, TOPK])
        pos = sb("best_pos", [P, PH, TOPK], U32)
        pa = [sb(f"pos_part{n}", [P, PH * TOPK], U32) for n in range(2)]
        pf = [sb(f"pos_part_f{n}", [P, PH * TOPK]) for n in range(2)]
        onehot = [sb(f"pos_onehot{n}", [P, PH * TOPK, TOPK], BF16) for n in range(2)]
        picks = sb("picks", [P, 3, PH * TOPK])
        esum = sb("gate_sum", [P, PH])
        iota16 = sb("iota16", [P, TOPK])
        wait_mark = sb("wait_mark", [P, 32])
        q_ps = [ctx.enter_context(nc.psum_tensor(f"query{b}", [P, 4, P], F32)) for b in range(4)]
        s_ps = [ctx.enter_context(nc.psum_tensor(f"key_scores{b}", [P, 4, KEYS], F32)) for b in range(4)]
        loaded = sem("query_weights_loaded")
        dv = sem("dve_steps_r")
        iota_ready = sem("iota16_ready")
        q_ready, q_read, s_ready, s_read = sem("query_ready"), sem("query_read"), sem("key_scores_ready"), sem("key_scores_read")
        shifted, exped, picked, picks_turned, picks_read = (sem("best_shifted"), sem("gates_exped"), sem("picks_ready"),
                                                            sem("picks_turned"), sem("picks_turned_read"))
        block = ctx.enter_context(nc.Block())

        @block.sync
        def _(sp):
            sp.dma_start(keys[:], dram["keysT"]).then_inc(loaded, 16)
            sp.dma_start(wq[:], dram["w_query"].rearrange("(k p) n -> p k n", p=P)).then_inc(loaded, 16)

        @block.gpsimd
        def _(pool):
            pool.iota(iota16[:], [[1, TOPK]], base=0, channel_multiplier=0, allow_small_or_imprecise_dtypes=True).then_inc(iota_ready, 1)

        @block.tensor
        def _(pe):
            pe.wait_ge(loaded, 32)
            with pe.Fori(0, NT) as i:
                for b in range(4):
                    for n in range(4):
                        for k in range(NK):
                            last = pe.matmul(q_ps[b][:, n], wq[:, k, (4 * b + n) * P:(4 * b + n + 1) * P], hnT[:, k, bass.ts(i, P)],
                                             start=(k == 0), stop=(k == NK - 1))
                    last.then_inc(q_ready, 1)
                for b in range(4):
                    pe.wait_ge(q_read, 4 * i + b + 1)
                    for n in range(4):
                        last = pe.matmul(s_ps[b][:, n], qT[:, 4 * b + n], keys[:, 4 * b + n], start=True, stop=True)
                    last.then_inc(s_ready, 1)
                pe.wait_ge(picked, i + 1)
                for n in range(3):
                    last = pe.transpose(q_ps[0][:, n], picks[:, n], ident[:])
                last.then_inc(picks_turned, 1)
                pe.wait_ge(picks_read, i + 1)

        @block.scalar
        def _(act):
            with act.Fori(0, NT) as i:
                for b in range(4):
                    act.wait_ge(q_ready, 4 * i + b + 1)
                    act.activation(qT[:, 4 * b:4 * b + 4], q_ps[b][:], ACT.Copy).then_inc(q_read, 1)
                act.wait_ge(shifted, i + 1)
                act.activation(picks[:, 2].rearrange("p (h k) -> p h k", k=TOPK), best[:], ACT.Exp).then_inc(exped, 1)

        @block.vector
        def _(dve):
            dve.wait_ge(iota_ready, 1)
            with dve.Fori(0, NT) as i:
                count, marks = [0], [0]

                def own(instruction):
                    count[0] += 1
                    instruction.then_inc(dv, 1)

                def wait_before_max(semaphore, value):
                    dve.wait_ge(semaphore, value)
                    dve.memset(wait_mark[:, marks[0]:marks[0] + 1], 0.0)
                    marks[0] += 1

                def done():
                    wait_before_max(dv, i * STEPS_PER_TILE + count[0])

                for hh in range(HALVES):
                    if hh % 4 == 0:
                        wait_before_max(s_ready, 4 * i + hh // 4 + 1)
                    own(dve.max(top[:, hh, 0:8], s_ps[hh // 4][:, hh % 4]))
                done()
                for hh in range(HALVES):
                    own(dve.max_index(topi[:, hh, 0:8], top[:, hh, 0:8], s_ps[hh // 4][:, hh % 4]))
                    dve.match_replace(rest[:, hh], top[:, hh, 0:8], s_ps[hh // 4][:, hh % 4], LOWEST).then_inc(s_read, 1)
                wait_before_max(s_read, 16 * i + 16)
                for hh in range(HALVES):
                    own(dve.max(top[:, hh, 8:16], rest[:, hh]))
                done()
                for hh in range(HALVES):
                    own(dve.max_index(topi[:, hh, 8:16], top[:, hh, 8:16], rest[:, hh]))
                halves = top[:].rearrange("p (h s) k -> p h s k", s=2)
                own(dve.tensor_tensor(cand[:].rearrange("p h (a b) -> p h a b", b=TOPK),
                                      halves[:, :, 0].unsqueeze(3).broadcast_to([P, PH, TOPK, TOPK]),
                                      halves[:, :, 1].unsqueeze(2).broadcast_to([P, PH, TOPK, TOPK]), ALU.add))
                done()
                own(dve.tensor_copy(topf[:], topi[:]))
                for h in range(PH):
                    own(dve.max(best[:, h, 0:8], cand[:, h]))
                done()
                for h in range(PH):
                    own(dve.max_index(pos[:, h, 0:8], best[:, h, 0:8], cand[:, h]))
                    own(dve.match_replace(cand2[:, h], best[:, h, 0:8], cand[:, h], LOWEST))
                done()
                for h in range(PH):
                    own(dve.max(best[:, h, 8:16], cand2[:, h]))
                done()
                for h in range(PH):
                    own(dve.max_index(pos[:, h, 8:16], best[:, h, 8:16], cand2[:, h]))
                done()
                own(dve.tensor_copy(esum[:], best[:, :, 0]))
                own(dve.tensor_single_scalar(pa[0][:], pos[:].rearrange("p h k -> p (h k)"), 4, ALU.logical_shift_right))
                own(dve.tensor_single_scalar(pa[1][:], pos[:].rearrange("p h k -> p (h k)"), 15, ALU.bitwise_and))
                done()
                dve.tensor_tensor(best[:], best[:], esum[:].unsqueeze(2).broadcast_to([P, PH, TOPK]), ALU.subtract).then_inc(shifted, 1)
                for n in range(2):
                    own(dve.tensor_copy(pf[n][:], pa[n][:]))
                done()
                for n in range(2):
                    own(dve.tensor_tensor(onehot[n][:], pf[n][:].unsqueeze(2).broadcast_to([P, PH * TOPK, TOPK]),
                                          iota16[:].unsqueeze(1).broadcast_to([P, PH * TOPK, TOPK]), ALU.is_equal))
                done()
                pairs = topf[:].rearrange("p (h s) k -> p h s k", s=2)
                for n in range(2):
                    four = onehot[n][:].rearrange("p (h j) k -> p h j k", j=TOPK)
                    own(dve.tensor_tensor(four, four, pairs[:, :, n].unsqueeze(2).broadcast_to([P, PH, TOPK, TOPK]), ALU.mult))
                dve.wait_ge(exped, i + 1)
                gates = picks[:, 2].rearrange("p (h k) -> p h k", k=TOPK)
                own(dve.tensor_reduce(esum[:], gates, AX_X, ALU.add))
                done()
                own(dve.reciprocal(esum[:], esum[:]))
                for n in range(2):
                    own(dve.tensor_reduce(picks[:, n], onehot[n][:], AX_X, ALU.add))
                done()
                dve.tensor_tensor(gates, gates, esum[:].unsqueeze(2).broadcast_to([P, PH, TOPK]), ALU.mult).then_inc(picked, 1)
                dve.wait_ge(picks_turned, i + 1)
                own(dve.tensor_copy(keep["i1T"][:, bass.ts(i, P)], q_ps[0][:, 0]))
                own(dve.tensor_copy(keep["i2T"][:, bass.ts(i, P)], q_ps[0][:, 1]))
                own(dve.tensor_copy(keep["gate_hi"][:, bass.ts(i, P)], q_ps[0][:, 2]))
                done()
                dve.tensor_tensor(keep["gate_lo"][:, bass.ts(i, P)], q_ps[0][:, 2], keep["gate_hi"][:, bass.ts(i, P)], ALU.subtract).then_inc(picks_read, 1)
                assert count[0] == STEPS_PER_TILE, count


STEPS_PER_TILE = 122


def gate_matrices(nc, dram, keep):
    with ExitStack() as ctx:
        sb = lambda name, shape, dt=F32: ctx.enter_context(nc.sbuf_tensor(name, shape, dt))
        sem = lambda name: ctx.enter_context(nc.semaphore(name))
        iota = sb("iota", [P, KEYS, TG], BF16)
        hnT, hn_split, tile_copy = keep["hnT"], keep["hn_split"], sb("tile_copy", [P, SEQ])
        split_steps = sem("split_steps")
        a = sb("onehot_i1", [P, 2, KEYS, TG], BF16)
        b = sb("onehot_i2", [P, KEYS, TG], BF16)
        bh, bl = sb("gated_hi", [P, 2, KEYS, TG], BF16), sb("gated_lo", [P, 2, KEYS, TG], BF16)
        stage = sb("gate_stage", [P, 2, KEYS, TG])
        g_ps = [ctx.enter_context(nc.psum_tensor(f"gates{n}", [P, 4, KEYS], F32)) for n in range(8)]
        iota_ready, b_ready, onehots = sem("iota_ready"), sem("onehot_i2_ready"), sem("onehots_ready")
        gates_ready, gates_read = sem("gates_ready"), sem("gates_read")
        stored = [sem("gates_stored0"), sem("gates_stored1")]
        block = ctx.enter_context(nc.Block())
        per = TG // 4
        gates_dram = dram["gates"]

        def over_groups(engine, body):
            body(0, 0, True)
            body(1, 1, True)
            with engine.Fori(1, SEQ // TG // 2) as pair:
                body(pair * 2, 0, False)
                body(pair * 2 + 1, 1, False)

        @block.gpsimd
        def _(pool):
            pool.iota(iota[:], [[1, KEYS], [0, TG]], base=0, channel_multiplier=0, allow_small_or_imprecise_dtypes=True).then_inc(iota_ready, 1)
            for k in range(NK):
                pool.tensor_copy(tile_copy[:], hnT[:, k]).then_inc(split_steps, 1)
                pool.wait_ge(split_steps, 3 * k + 1)
                pool.tensor_copy(hn_split[:, k, 0], tile_copy[:]).then_inc(split_steps, 1)
                pool.wait_ge(split_steps, 3 * k + 2)
                pool.tensor_tensor(hn_split[:, k, 1], tile_copy[:], hn_split[:, k, 0], ALU.subtract).then_inc(split_steps, 1)
                pool.wait_ge(split_steps, 3 * k + 3)

        @block.vector
        def _(dve):
            dve.wait_ge(iota_ready, 1)

            def build(m, s, fresh):
                tokens = lambda name: keep[name][:, bass.ts(m, TG)].unsqueeze(1).broadcast_to([P, KEYS, TG])
                dve.tensor_tensor(b[:], iota[:], tokens("i2T"), ALU.is_equal).then_inc(b_ready, 1)
                if not fresh:
                    dve.wait_ge(gates_ready, per * (m - 1))
                dve.tensor_tensor(a[:, s], iota[:], tokens("i1T"), ALU.is_equal).then_inc(onehots, 1)
                dve.wait_ge(b_ready, m + 1)
                dve.tensor_tensor(bh[:, s], b[:], tokens("gate_hi"), ALU.mult).then_inc(onehots, 1)
                dve.tensor_tensor(bl[:, s], b[:], tokens("gate_lo"), ALU.mult).then_inc(onehots, 1)
                dve.wait_ge(onehots, 3 * m + 3)

            over_groups(dve, build)

        @block.tensor
        def _(pe):
            def multiply(m, s, fresh):
                pe.wait_ge(onehots, 3 * m + 3)
                for n in range(per):
                    if not fresh or s:
                        pe.wait_ge(gates_read, per * (m - 1) + n + 1)
                    for t in range(4):
                        at = 4 * n + t
                        pe.matmul(g_ps[n][:, t], a[:, s, :, at], bh[:, s, :, at], start=True, stop=False)
                        last = pe.matmul(g_ps[n][:, t], a[:, s, :, at], bl[:, s, :, at], start=False, stop=True)
                    last.then_inc(gates_ready, 1)

            over_groups(pe, multiply)

        @block.scalar
        def _(act):
            def evacuate(m, s, fresh):
                if not fresh:
                    act.wait_ge(stored[s], (m - s) * 8)
                for n in range(per):
                    act.wait_ge(gates_ready, per * m + n + 1)
                    act.activation(stage[:, s, :, 4 * n:4 * n + 4].rearrange("p i t -> p t i"), g_ps[n][:], ACT.Copy).then_inc(gates_read, 1)
            over_groups(act, evacuate)

        @block.sync
        def _(sp):
            def store(m, s, fresh):
                sp.wait_ge(gates_read, per * (m + 1))
                sp.dma_start(gates_dram[:, :, bass.ds(m, 1)].rearrange("p g o i t -> p g (o i t)"),
                             stage[:, s].rearrange("p (g i) t -> p g (i t)", i=GROUP)).then_inc(stored[s], 16)
            over_groups(sp, store)
            for s in range(2):
                sp.wait_ge(stored[s], 16 * SEQ // TG // 2)


def experts(nc, dram, keep):
    with ExitStack() as ctx:
        sb = lambda name, shape, dt=F32: ctx.enter_context(nc.sbuf_tensor(name, shape, dt))
        sem = lambda name: ctx.enter_context(nc.semaphore(name))
        hn_hi, hn_lo, y = keep["hn_split"][:, :, 0], keep["hn_split"][:, :, 1], keep["x"]
        u_raw, v_raw = sb("u_raw", [P, 2, NK, P]), sb("v_raw", [P, 2, D])
        u_hi, u_lo = sb("u_hi", [P, 2, NK, P], BF16), sb("u_lo", [P, 2, NK, P], BF16)
        v_hi, v_lo = sb("v_hi", [P, 2, GROUP, D], BF16), sb("v_lo", [P, 2, GROUP, D], BF16)
        gates = sb("gates", [P, 2, SEQ // TG, GROUP, TG])
        act_sb = sb("gelu", [P, 2, SEQ])
        h_hi, h_lo = sb("h_hi", [P, 2, GROUP, SEQ], BF16), sb("h_lo", [P, 2, GROUP, SEQ], BF16)
        a_ps = [ctx.enter_context(nc.psum_tensor(f"act{b}", [P, SEQ], F32)) for b in range(2)]
        y_ps = [ctx.enter_context(nc.psum_tensor(f"y{b}", [P, BANK], F32)) for b in range(4)]
        u_loaded, v_loaded, g_loaded = ([sem(f"{n}_loaded{s}") for s in range(2)] for n in ("u", "v", "gates"))
        u_hi_ready, u_split, v_hi_ready, v_split = sem("u_hi_ready"), sem("u_split"), sem("v_hi_ready"), sem("v_split")
        u_mult, gelu_ready, h_gated, h_hi_ready, h_product = sem("u_multiplied"), sem("gelu_ready"), sem("h_gated"), sem("h_hi_ready"), sem("h_product")
        y_ready, y_added, out_done = sem("y_ready"), sem("y_added"), sem("out_stored")
        block = ctx.enter_context(nc.Block())
        u_dram, v_dram, g_dram = dram["peer_u"], dram["peer_v"], dram["gates"]
        LAST = NGROUP - 1

        def over_groups(engine, body):
            body(0, 0)
            body(1, 1)
            with engine.Fori(1, NGROUP // 2 - 1) as pair:
                body(pair * 2, 0)
                body(pair * 2 + 1, 1)
            body(NGROUP - 2, 0)
            body(LAST, 1)

        def first(g):
            return isinstance(g, int) and g == 0

        @block.sync
        def _(sp):
            def load_u(n, s):
                sp.dma_start(u_raw[:, s], u_dram[bass.ds(n, 1)].rearrange("o p k e -> (o p) k e")).then_inc(u_loaded[s], 16)

            def load_v(n, s):
                sp.dma_start(v_raw[:, s], v_dram[:, bass.ds(n, 1)].rearrange("p o d -> p (o d)")).then_inc(v_loaded[s], 16)

            def load_g(g, s):
                sp.dma_start(gates[:, s].rearrange("p g i t -> p (g i t)"),
                             g_dram[:, bass.ds(g, 1)].rearrange("p o g i t -> p (o g i t)")).then_inc(g_loaded[s], 16)

            for n in range(2):
                load_u(n, n)
                load_v(n, n)
            load_g(0, 0)

            def group(g, s):
                if not (isinstance(g, int) and g == LAST):
                    if not first(g):
                        sp.wait_ge(h_gated, 2 * GROUP * g)
                    load_g(g + 1, 1 - s)
                for c in range(GROUP):
                    n = g * GROUP + c
                    if isinstance(g, int) and n + 2 >= KEYS:
                        continue
                    sp.wait_ge(u_split, n + 1)
                    load_u(n + 2, c % 2)
                    sp.wait_ge(v_split, n + 1)
                    load_v(n + 2, c % 2)

            over_groups(sp, group)
            for i in range(NT):
                sp.wait_ge(y_added, 16 * LAST + 2 * i + 2)
                sp.dma_start(dram["out"][i * P:(i + 1) * P], y[:, i]).then_inc(out_done, 16)
            sp.wait_ge(out_done, 16 * NT)

        @block.scalar
        def _(act):
            def split_u(n, c):
                act.wait_ge(u_loaded[c % 2], ((n - c % 2) // 2 + 1) * 16 if isinstance(n, int) else (n - c % 2) * 8 + 16)
                act.activation(u_hi[:, c % 2], u_raw[:, c % 2], ACT.Copy).then_inc(u_hi_ready, 1)

            split_u(0, 0)
            split_u(1, 1)

            def group(g, s):
                for c in range(GROUP):
                    n = g * GROUP + c
                    act.wait_ge(u_mult, n + 1)
                    if not first(g) or c >= 2:
                        act.wait_ge(h_gated, 2 * n - 2)
                    for half in range(2):
                        cols = slice(half * BANK, (half + 1) * BANK)
                        act.activation(act_sb[:, c % 2, cols], a_ps[c % 2][:, cols], ACT.Gelu_apprx_tanh).then_inc(gelu_ready, 1)
                    if not (isinstance(g, int) and n + 2 >= KEYS):
                        split_u(n + 2, c)
                    act.wait_ge(v_loaded[c % 2], (n - c % 2) * 8 + 16)
                    if not (isinstance(g, int) and g < 2):
                        act.wait_ge(y_ready, 16 * (g - 1))
                    act.activation(v_hi[:, s, c], v_raw[:, c % 2], ACT.Copy).then_inc(v_hi_ready, 1)

            over_groups(act, group)

        @block.vector
        def _(dve):
            def split_u(n, c):
                dve.wait_ge(u_hi_ready, n + 1)
                dve.tensor_tensor(u_lo[:, c % 2], u_raw[:, c % 2], u_hi[:, c % 2], ALU.subtract).then_inc(u_split, 1)

            def add_y(g, c):
                for b in range(4):
                    dve.wait_ge(y_ready, 16 * g + 4 * c + b + 1)
                    part = y[:, 2 * c + b // 2, (b % 2) * BANK:(b % 2 + 1) * BANK]
                    if not first(g):
                        dve.wait_ge(y_added, 16 * (g - 1) + 4 * c + b + 1)
                    dve.tensor_tensor(part, part, y_ps[b][:], ALU.add).then_inc(y_added, 1)

            split_u(0, 0)
            split_u(1, 1)

            def group(g, s):
                dve.wait_ge(g_loaded[s], (g - s) * 8 + 16)
                for c in range(GROUP):
                    n = g * GROUP + c
                    for half in range(2):
                        cols = slice(half * BANK, (half + 1) * BANK)
                        dve.wait_ge(gelu_ready, 2 * n + half + 1)
                        g_part = gates[:, s, half * 16:(half + 1) * 16, c]
                        a_part = act_sb[:, c % 2, cols].rearrange("p (g t) -> p g t", t=TG)
                        dve.tensor_tensor(a_part, a_part, g_part, ALU.mult).then_inc(h_product, 1)
                    if not (isinstance(g, int) and g < 2):
                        dve.wait_ge(y_ready, 16 * (g - 1))
                    for half in range(2):
                        cols = slice(half * BANK, (half + 1) * BANK)
                        dve.wait_ge(h_product, 2 * n + half + 1)
                        dve.tensor_copy(h_hi[:, s, c, cols], act_sb[:, c % 2, cols]).then_inc(h_hi_ready, 1)
                    if not (isinstance(g, int) and n + 2 >= KEYS):
                        split_u(n + 2, c)
                    for half in range(2):
                        cols = slice(half * BANK, (half + 1) * BANK)
                        dve.wait_ge(h_hi_ready, 2 * n + half + 1)
                        dve.tensor_tensor(h_lo[:, s, c, cols], act_sb[:, c % 2, cols], h_hi[:, s, c, cols], ALU.subtract).then_inc(h_gated, 1)
                    dve.wait_ge(v_hi_ready, n + 1)
                    dve.tensor_tensor(v_lo[:, s, c], v_raw[:, c % 2], v_hi[:, s, c], ALU.subtract).then_inc(v_split, 1)
                    if not first(g):
                        add_y(g - 1, c)

            over_groups(dve, group)
            for c in range(GROUP):
                add_y(LAST, c)

        @block.tensor
        def _(pe):
            def up(n, c):
                pe.wait_ge(u_split, n + 1)
                if not (isinstance(n, int) and n < 2):
                    pe.wait_ge(gelu_ready, 2 * n - 2)
                for half in range(2):
                    cols = slice(half * BANK, (half + 1) * BANK)
                    terms = [(w, x, k) for k in range(NK) for w, x in ((u_hi, hn_hi), (u_hi, hn_lo), (u_lo, hn_hi))]
                    for t, (w, x, k) in enumerate(terms):
                        last = pe.matmul(a_ps[c % 2][:, cols], w[:, c % 2, k], x[:, k, cols], start=(t == 0), stop=(t == len(terms) - 1))
                last.then_inc(u_mult, 1)

            def down(g, s, c):
                if c == 0:
                    pe.wait_ge(h_gated, 2 * GROUP * (g + 1))
                    pe.wait_ge(v_split, GROUP * (g + 1))
                for b in range(4):
                    if not (first(g) and c == 0):
                        pe.wait_ge(y_added, 16 * g + 4 * c + b + 1 - 4)
                    i, cols = 2 * c + b // 2, slice((b % 2) * BANK, (b % 2 + 1) * BANK)
                    terms = [(h, v, e) for e in range(GROUP) for h, v in ((h_hi, v_hi), (h_hi, v_lo), (h_lo, v_hi))]
                    for t, (h, v, e) in enumerate(terms):
                        last = pe.matmul(y_ps[b][:], h[:, s, e, i * P:(i + 1) * P], v[:, s, e, cols], start=(t == 0), stop=(t == len(terms) - 1))
                    last.then_inc(y_ready, 1)

            def group(g, s):
                for c in range(GROUP):
                    up(g * GROUP + c, c)
                    if not first(g):
                        down(g - 1, 1 - s, c)

            over_groups(pe, group)
            for c in range(GROUP):
                down(LAST, 1, c)


def build(nc, dram):
    with ExitStack() as ctx:
        sb = lambda name, shape, dt=F32: ctx.enter_context(nc.sbuf_tensor(name, shape, dt))
        keep = {"x": sb("x", [P, NT, D]), "ident": sb("ident", [P, P])}
        wide = sb("wide", [P, NK * SEQ])
        keep["wide"] = wide[:]
        keep["hnT"] = wide[:].rearrange("p (k t) -> p k t", t=SEQ)
        keep["hn_split"] = wide[:].bitcast(BF16).rearrange("p (k s t) -> p k s t", s=2, t=SEQ)
        for name in ("i1T", "i2T", "gate_hi", "gate_lo"):
            keep[name] = sb(name, [P, SEQ], BF16)
        with ExitStack() as mixed:
            for name in ("q", "u"):
                keep[name] = mixed.enter_context(nc.sbuf_tensor(name, [P, NT, DA], F32))
            with ExitStack() as inner:
                for name in ("k", "v", "va"):
                    keep[name] = inner.enter_context(nc.sbuf_tensor(name, [P, NT, DA], F32))
                input_projection(nc, dram, keep)
                attention_and_gating(nc, dram, keep)
            if dram.get("stop") == "attn":
                return dump(nc, dram, [keep["q"], keep["u"]])
            output_projection(nc, dram, keep)
        if dram.get("stop") == "hn":
            return dump(nc, dram, [keep["x"], keep["hnT"]])
        retrieval(nc, dram, keep)
        if dram.get("stop") == "picks":
            return dump(nc, dram, [keep["i1T"], keep["i2T"], keep["gate_hi"], keep["gate_lo"]])
        gate_matrices(nc, dram, keep)
        experts(nc, dram, keep)


def dump(nc, dram, tensors):
    with nc.semaphore("dumped") as s, nc.Block() as block:
        @block.sync
        def _(sp):
            for n, t in enumerate(tensors):
                sp.dma_start(dram[f"dump{n}"], t[:] ).then_inc(s, 16)
            sp.wait_ge(s, 16 * len(tensors))


def laid_out(inputs):
    a = {k: np.asarray(v) for k, v in inputs.items()}
    column = lambda w: w.reshape(-1, P).T
    w_s = a["sgu_w"][0]
    u = a["peer_u"][0].reshape(KEYS, KEYS, NK, P)
    arrays = {
        "x": a["x"][0], "xT": a["x"][0].T, "ln1": column(a["ln1_w"][0]), "w_in": a["w_in"][0],
        "q_norm_w": a["q_norm_w"][0].reshape(DH, 1), "k_norm_w": a["k_norm_w"][0].reshape(DH, 1),
        "sgu_norm_w": a["sgu_norm_w"][0].reshape(1, DA), "sgu_wT": w_s.transpose(2, 0, 1), "sgu_b": a["sgu_b"][0].T,
        "mix_norm_w": column(a["mix_norm_w"][0]), "w_out": a["w_out"][0], "ln2": column(a["ln2_w"][0]),
        "rel_bias": a["rel_bias"], "w_query": a["peer_w_query"][0],
        "keysT": np.stack([a["peer_keys1"][0], a["peer_keys2"][0]], 1).reshape(HALVES, KEYS, P).transpose(2, 0, 1),
        "peer_u": u.transpose(1, 3, 2, 0),
        "peer_v": a["peer_v"][0].reshape(KEYS, KEYS, D),
    }
    arrays.update(shape_constants())
    return {k: np.ascontiguousarray(v) for k, v in arrays.items()}


def kernel(**inputs):
    import concourse.bacc as bacc
    from concourse.bass_utils import run_bass_kernel_spmd as run

    nc = bacc.Bacc("TRN2", target_bir_lowering=False, num_devices=1)
    arrays = laid_out(inputs)
    dram = {k: nc.dram_tensor(f"in_{k}", v.shape, F32, kind="ExternalInput").ap() for k, v in arrays.items()}
    dram["bias_scratch"] = nc.dram_tensor("bias_scratch", (HEADS, BIAS_LEN), F32, kind="Internal").ap()
    dram["gates"] = nc.dram_tensor("gates_scratch", (P, NGROUP, SEQ // TG, GROUP, TG), F32, kind="Internal").ap()
    dram["out"] = nc.dram_tensor("out", (SEQ, D), F32, kind="ExternalOutput").ap()
    build(nc, dram)
    result = run(nc, [{f"in_{k}": v for k, v in arrays.items()}], core_ids=[0])
    return result.results[0]["out"].reshape(1, SEQ, D)
```

```python
from contextlib import ExitStack

import numpy as np
import concourse.bass as bass
from concourse import mybir

F32 = mybir.dt.float32
BF16 = mybir.dt.bfloat16
U32 = mybir.dt.uint32
ALU = mybir.AluOpType
ACT = mybir.ActivationFunctionType
AX_X = mybir.AxisListType.X

P = 128
SEQ = 1024
D = 1024
NT = SEQ // P
NK = D // P
HEADS = 8
DH = 64
DA = HEADS * DH
GROUPS = 4
D_IN = 5 * DA
NPROJ = D_IN // 512
EPS = 1e-6
NEG = -1e30
BUCKETS = 32
PH = 8
TOPK = 16
KEYS = 128
HALVES = 2 * PH
LOWEST = -3.0e38
BIAS_LEN = SEQ + P
GROUP = 4
NGROUP = KEYS // GROUP
TG = 32
BANK = 512
ROW_TILES = 2
ROW_TOKENS = ROW_TILES * P
DENSE = SEQ - ROW_TOKENS
HALF = DENSE // 2
PICKS = PH * TOPK


def patterns(distance):
    r = distance
    return sum(((r >= 0) & (r <= w) & (r % d == 0)).astype(np.int64) for w, d in ((128, 1), (512, 4), (2048, 16)))


def shape_constants():
    r = (SEQ - 1) - np.arange(BIAS_LEN)
    d = np.maximum(r, 0)
    exact = BUCKETS // 2
    large = exact + (np.log(np.maximum(d, exact).astype(np.float32) / np.float32(exact))
                     / np.float32(np.log(2048 / exact)) * np.float32(BUCKETS - exact)).astype(np.int32)
    bucket = np.where(d < exact, d, np.minimum(large, BUCKETS - 1))
    count = patterns(r)
    table = np.zeros((BUCKETS + 1, BIAS_LEN), np.float32)
    table[bucket, np.arange(BIAS_LEN)] = 1.0
    table[BUCKETS] = np.where(count > 0, np.log(np.maximum(count, 1)), NEG)
    ident = np.eye(P, dtype=np.float32)
    return {"bias_table": table, "ident": ident, "flip": np.ascontiguousarray(ident[::-1])}


class Steps:

    def __init__(self, engine, sem):
        self.engine, self.sem, self.count = engine, sem, 0

    def __call__(self, instruction):
        self.count += 1
        instruction.then_inc(self.sem, 1)
        return self.count

    def done(self, upto=None):
        self.engine.wait_ge(self.sem, self.count if upto is None else upto)


def input_projection(nc, dram, keep):
    with ExitStack() as ctx:
        sb = lambda name, shape, dt=F32: ctx.enter_context(nc.sbuf_tensor(name, shape, dt))
        sem = lambda name: ctx.enter_context(nc.semaphore(name))
        xs = keep["wide"].rearrange("p (k t) -> p k t", t=SEQ)
        w = sb("w_in", [P, 2, NK, 512])
        junk = sb("square_junk", [P, D])
        ssq, ms, rms, rstd = (sb(f"ln1_{n}", [P, NT]) for n in ("ssq", "ms", "inv", "rstd"))
        ln1 = sb("ln1", [P, NK])
        acc = [ctx.enter_context(nc.psum_tensor(f"proj_acc{b}", [P, BANK], F32)) for b in range(8)]
        x_in, xT_in, ln1_in = sem("x_loaded"), sem("xT_loaded"), sem("ln1_loaded")
        w_in = [sem("w_in_loaded0"), sem("w_in_loaded1")]
        ssq_ready, ms_ready, inv_ready, rstd_ready = sem("ssq_ready"), sem("ms_ready"), sem("inv_ready"), sem("rstd_ready")
        xs_ready, proj_ready, proj_read_v, proj_read_a = sem("xs_ready"), sem("proj_ready"), sem("proj_read_v"), sem("proj_read_a")
        x_sb, outs = keep["x"], [keep[n] for n in ("q", "k", "v", "u", "va")]
        w_dram = dram["w_in"].rearrange("(k p) n -> p k n", p=P)
        block = ctx.enter_context(nc.Block())

        @block.sync
        def _(sp):
            sp.dma_start(keep["ident"][:], dram["ident"]).then_inc(ln1_in, 16)
            sp.dma_start(ln1[:], dram["ln1"]).then_inc(ln1_in, 16)
            sp.dma_start(xs[:], dram["xT"].rearrange("(k p) t -> p k t", p=P)).then_inc(xT_in, 16)
            for n in range(NPROJ):
                if n >= 2:
                    sp.wait_ge(proj_ready, NT * (n - 1))
                sp.dma_start(w[:, n % 2], w_dram[:, :, n * 512:(n + 1) * 512]).then_inc(w_in[n % 2], 16)

        @block.gpsimd
        def _(pool):
            pool.dma_start(x_sb[:], dram["x"].rearrange("(i p) d -> p i d", p=P)).then_inc(x_in, 16)

        @block.vector
        def _(dve):
            dve.wait_ge(ln1_in, 32)
            dve.wait_ge(xT_in, 16)
            for k in range(NK):
                dve.tensor_scalar(xs[:, k], xs[:, k], ln1[:, k:k + 1], None, ALU.mult).then_inc(xs_ready, 1)
            dve.wait_ge(ssq_ready, NT)
            dve.tensor_scalar(ms[:], ssq[:], 1.0 / D, EPS, ALU.mult, ALU.add).then_inc(ms_ready, 1)
            dve.wait_ge(ms_ready, 1)
            dve.reciprocal(rms[:], ms[:]).then_inc(inv_ready, 1)
            dve.wait_ge(rstd_ready, 1)
            for n in (0, 1):
                for i in range(NT):
                    g = n * NT + i
                    dve.wait_ge(proj_ready, g + 1)
                    dve.tensor_scalar(outs[n][:, i], acc[g % 8][:], rstd[:, i:i + 1], None, ALU.mult).then_inc(proj_read_v, 1)

        @block.scalar
        def _(act):
            act.wait_ge(x_in, 16)
            for i in range(NT):
                if i:
                    act.wait_ge(ssq_ready, i)
                act.activation(junk[:], x_sb[:, i], ACT.Square, accum_out=ssq[:, i:i + 1]).then_inc(ssq_ready, 1)
            act.wait_ge(inv_ready, 1)
            act.activation(rstd[:], rms[:], ACT.Sqrt).then_inc(rstd_ready, 1)
            act.wait_ge(rstd_ready, 1)
            for n in (2, 3, 4):
                for i in range(NT):
                    g = n * NT + i
                    act.wait_ge(proj_ready, g + 1)
                    act.activation(outs[n][:, i], acc[g % 8][:], ACT.Copy if n == 2 else ACT.Gelu_apprx_tanh,
                                   scale=rstd[:, i:i + 1]).then_inc(proj_read_a, 1)

        @block.tensor
        def _(pe):
            pe.wait_ge(xs_ready, NK)
            for n in range(NPROJ):
                pe.wait_ge(w_in[n % 2], 16 * (n // 2 + 1))
                for i in range(NT):
                    g = n * NT + i
                    if 8 <= g < 24:
                        pe.wait_ge(proj_read_v, g - 7)
                    elif g >= 24:
                        pe.wait_ge(proj_read_a, g - 7 - 16)
                    for k in range(NK):
                        last = pe.matmul(acc[g % 8][:], xs[:, k, i * P:(i + 1) * P], w[:, n % 2, k], start=(k == 0), stop=(k == NK - 1))
                    last.then_inc(proj_ready, 1)


def attention_and_gating(nc, dram, keep):
    with ExitStack() as ctx:
        sb = lambda name, shape, dt=F32: ctx.enter_context(nc.sbuf_tensor(name, shape, dt))
        sem = lambda name: ctx.enter_context(nc.semaphore(name))
        psum = lambda name: ctx.enter_context(nc.psum_tensor(name, [P, BANK], F32))
        q, k, v, u, va = (keep[n] for n in ("q", "k", "v", "u", "va"))
        ident = keep["ident"]
        qT, kT = sb("qT", [P, 4, SEQ]), sb("kT", [P, 4, SEQ])
        wide = keep["wide"].rearrange("p (h t) -> p h t", t=SEQ)
        square = keep["wide"][:, 0:NT * DA]
        logits = sb("logits", [P, 2, SEQ])
        probs = logits
        probsT = sb("probsT", [P, 2, SEQ])
        flip = sb("flip", [P, P])
        table = logits[0:BUCKETS + 1].rearrange("p a s -> p (a s)")[:, 0:BIAS_LEN]
        bias_sb = probsT[0:HEADS].rearrange("p a s -> p (a s)")[:, 0:BIAS_LEN]
        relb = sb("rel_bias", [BUCKETS + 1, HEADS])
        qw, kw = sb("q_norm_w", [P, 1]), sb("k_norm_w", [P, 1])
        hs = [sb(f"head_ssq{n}", [P, NT * HEADS]) for n in range(3)]
        sw = sb("sgu_w", [P, GROUPS, P])
        sgn = sb("sgu_norm", [P, DA])
        sgb = sb("sgu_b", [P, GROUPS])
        mx, nmx, den, rden = (sb(f"row_{n}", [P, NT * HEADS]) for n in ("max", "neg_max", "sum", "inv_sum"))
        s_ps = [ctx.enter_context(nc.psum_tensor(f"scores{b}", [P, 2 * BANK], F32)) for b in range(2)]
        t_ps = [psum("turned0"), psum("turned1")]
        o_ps = [psum("out0"), psum("out1")]
        small_in, bias_out, bias_in = sem("small_loaded"), sem("bias_stored"), sem("bias_loaded")
        sgu_in = sem("sgu_loaded")
        dv, ac = sem("dve_steps"), sem("act_steps")
        inv_ready, std_ready, normed = sem("head_inv"), sem("head_rstd"), sem("qkv_normed")
        turned, turned_read = sem("qk_turned"), sem("qk_turned_read")
        row_ready, row_read = sem("bias_row_ready"), sem("bias_row_read")
        flipped, flipped_read = sem("bias_flipped"), sem("bias_flipped_read")
        scored, biased, exped, nmax_ready = sem("scored"), sem("biased"), sem("exped"), sem("neg_max_ready")
        pt_ready, pt_read, pv_ready, pv_read = sem("probs_turned"), sem("probs_turned_read"), sem("pv_ready"), sem("pv_read")
        masked, mixed, gated = sem("sgu_w_masked"), sem("spatial_ready"), sem("spatial_read")
        ones_row = sem("ones_row_ready")
        block = ctx.enter_context(nc.Block())
        units = [(h, i) for h in range(HEADS) for i in range(NT)]
        scratch = dram["bias_scratch"]

        @block.sync
        def _(sp):
            for dst, src in ((flip[:], dram["flip"]), (table, dram["bias_table"]), (relb[0:BUCKETS], dram["rel_bias"]),
                             (qw[0:DH], dram["q_norm_w"]), (qw[DH:P], dram["q_norm_w"]),
                             (kw[0:DH], dram["k_norm_w"]), (kw[DH:P], dram["k_norm_w"])):
                sp.dma_start(dst, src).then_inc(small_in, 16)
            for dst, src in ((sw[:], dram["sgu_wT"]), (sgn[:], dram["sgu_norm_w"].to_broadcast([P, DA])), (sgb[:], dram["sgu_b"])):
                sp.dma_start(dst, src).then_inc(sgu_in, 16)
            sp.wait_ge(row_read, 3)
            sp.dma_start(scratch, bias_sb).then_inc(bias_out, 16)
            sp.wait_ge(bias_out, 16)
            sp.wait_ge(normed, 3)
            skewed = bass.AP(scratch.tensor, scratch.offset, [[1, P], [BIAS_LEN, HEADS], [1, SEQ]])
            sp.dma_start(wide, skewed).then_inc(bias_in, 16)

        @block.gpsimd
        def _(pool):
            pool.memset(relb[BUCKETS:BUCKETS + 1], 1.0).then_inc(ones_row, 1)
            pool.wait_ge(ones_row, 1)
            pool.wait_ge(sgu_in, 48)
            pool.affine_select(out=sw[:], in_=sw[:], compare_op=ALU.is_ge, fill=0.0, base=0,
                               pattern=[[0, GROUPS], [1, P]], channel_multiplier=-1).then_inc(masked, 1)

        @block.vector
        def _(dve):
            own = Steps(dve, dv)

            def norm(n, t, width, dim):
                runs = t.rearrange("p i (h d) -> p (i h) d", d=dim)
                nrun = NT * width // dim
                sq = square.rearrange("p (r d) -> p r d", d=dim)
                own(dve.tensor_tensor(sq, runs, runs, ALU.mult))
                own.done()
                own(dve.tensor_reduce(hs[n][:, 0:nrun], sq, AX_X, ALU.add))
                own.done()
                own(dve.tensor_scalar(hs[n][:, 0:nrun], hs[n][:, 0:nrun], 1.0 / dim, EPS, ALU.mult, ALU.add))
                own.done()
                dve.reciprocal(hs[n][:, 0:nrun], hs[n][:, 0:nrun]).then_inc(inv_ready, 1)
                dve.wait_ge(std_ready, n + 1)
                last = dve.tensor_tensor(runs, runs, hs[n][:, 0:nrun].unsqueeze(2).broadcast_to([P, nrun, dim]), ALU.mult)
                last.then_inc(normed, 1)

            norm(0, q, DA, DH)
            norm(1, k, DA, DH)
            norm(2, va, DA, P)
            dve.wait_ge(normed, 3)
            dve.wait_ge(sgu_in, 48)
            own(dve.tensor_tensor(va[:], va[:], sgn[:].unsqueeze(1).broadcast_to([P, NT, DA]), ALU.mult))
            for c in range(3):
                dve.wait_ge(row_ready, c + 1)
                dve.tensor_copy(bias_sb[:, c * 384:(c + 1) * 384], s_ps[0][0:HEADS, 0:384] if c == 0 else
                                (s_ps[0][0:HEADS, BANK:BANK + 384] if c == 1 else s_ps[1][0:HEADS, 0:384])).then_inc(row_read, 1)
            dve.wait_ge(small_in, 16 * 7)
            for n in range(16):
                t, pair, half = n // 8, (n // 2) % 4, n % 2
                dve.wait_ge(turned, n + 1)
                dst = (qT if t == 0 else kT)[:, pair, half * 512:(half + 1) * 512]
                dve.tensor_scalar(dst, t_ps[n % 2][:], (qw if t == 0 else kw)[:, 0:1], DH ** -0.5 if t == 0 else 1.0,
                                  ALU.mult, ALU.mult).then_inc(turned_read, 1)
            for n in range(16):
                dve.wait_ge(flipped, n + 1)
                dve.tensor_copy(wide[:, n // 2, (n % 2) * 512:(n % 2 + 1) * 512], s_ps[n % 2][:, 0:BANK]).then_inc(flipped_read, 1)
            dve.wait_ge(flipped_read, 16)

            def add_bias(n):
                h, i = units[n]
                w = (i + 1) * P
                dve.wait_ge(scored, n + 1)
                if n >= 2:
                    dve.wait_ge(exped, n - 1)
                dve.tensor_tensor_reduce(logits[:, n % 2, 0:w], s_ps[n % 2][:, 0:w], wide[:, h, SEQ - w:SEQ], 1.0, LOWEST,
                                         ALU.add, ALU.max, mx[:, n:n + 1]).then_inc(biased, 1)
                dve.wait_ge(biased, n + 1)
                dve.tensor_scalar(nmx[:, n:n + 1], mx[:, n:n + 1], -1.0, None, ALU.mult).then_inc(nmax_ready, 1)

            def out(n):
                h, i = units[n]
                dve.wait_ge(exped, n + 1)
                own(dve.reciprocal(rden[:, n:n + 1], den[:, n:n + 1]))
                own.done()
                dve.wait_ge(pv_ready, n + 1)
                dve.tensor_scalar(q[:, i, h * DH:(h + 1) * DH], o_ps[n % 2][:, 0:DH], rden[:, n:n + 1], None, ALU.mult).then_inc(pv_read, 1)

            add_bias(0)
            for n in range(len(units)):
                if n + 1 < len(units):
                    add_bias(n + 1)
                if n >= 1:
                    out(n - 1)
            out(len(units) - 1)
            for n in range(NT * GROUPS):
                i, g = n // GROUPS, n % GROUPS
                dve.wait_ge(mixed, n + 1)
                cols = slice(g * P, (g + 1) * P)
                dve.scalar_tensor_tensor(out=u[:, i, cols], in0=t_ps[n % 2][:, 0:P], scalar=sgb[:, g:g + 1], in1=u[:, i, cols],
                                         op0=ALU.add, op1=ALU.mult).then_inc(gated, 1)

        @block.scalar
        def _(act):
            own = Steps(act, ac)
            for n in range(3):
                act.wait_ge(inv_ready, n + 1)
                c = NT * HEADS if n < 2 else NT * GROUPS
                act.activation(hs[n][:, 0:c], hs[n][:, 0:c], ACT.Sqrt).then_inc(std_ready, 1)
            turns = 0
            for n, (h, i) in enumerate(units):
                w = (i + 1) * P
                act.wait_ge(nmax_ready, n + 1)
                act.wait_ge(biased, n + 1)
                act.activation(probs[:, n % 2, 0:w], logits[:, n % 2, 0:w], ACT.Exp, bias=nmx[:, n:n + 1],
                               accum_out=den[:, n:n + 1]).then_inc(exped, 1)
                if n >= 2:
                    act.wait_ge(pv_ready, n - 1)
                for c in range(0, i + 1, 4):
                    m = min(4, i + 1 - c)
                    act.wait_ge(pt_ready, turns + 1)
                    act.activation(probsT[:, n % 2, c * P:(c + m) * P], t_ps[turns % 2][:, 0:m * P], ACT.Copy).then_inc(pt_read, 1)
                    turns += 1

        @block.tensor
        def _(pe):
            pe.wait_ge(small_in, 16 * 7)
            pe.wait_ge(ones_row, 1)
            for c in range(3):
                dst = s_ps[c // 2][0:HEADS, (c % 2) * BANK:(c % 2) * BANK + 384]
                pe.matmul(dst, relb[:], table[:, c * 384:(c + 1) * 384], start=True, stop=True).then_inc(row_ready, 1)
            for n in range(16):
                t, pair, half = n // 8, (n // 2) % 4, n % 2
                pe.wait_ge(normed, t + 1)
                if n >= 2:
                    pe.wait_ge(turned_read, n - 1)
                for j in range(4):
                    last = pe.transpose(t_ps[n % 2][:, j * P:(j + 1) * P], (q if t == 0 else k)[:, half * 4 + j, pair * P:(pair + 1) * P], ident[:])
                last.then_inc(turned, 1)
            pe.wait_ge(turned_read, 16)
            pe.wait_ge(bias_in, 16)
            pe.wait_ge(row_read, 3)
            for n in range(16):
                if n >= 2:
                    pe.wait_ge(flipped_read, n - 1)
                pe.matmul(s_ps[n % 2][:, 0:BANK], flip[:], wide[:, n // 2, (n % 2) * 512:(n % 2 + 1) * 512],
                          start=True, stop=True).then_inc(flipped, 1)
            pe.wait_ge(flipped_read, 16)

            def scores(n):
                h, i = units[n]
                base, w = DH * (h % 2), (i + 1) * P
                if n >= 2:
                    pe.wait_ge(biased, n - 1)
                for c in range(0, w, BANK):
                    m = min(BANK, w - c)
                    last = pe.matmul(s_ps[n % 2][:, c:c + m], qT[base:base + DH, h // 2, i * P:(i + 1) * P],
                                     kT[base:base + DH, h // 2, c:c + m], start=True, stop=True)
                last.then_inc(scored, 1)

            turns = 0
            scores(0)
            for n, (h, i) in enumerate(units):
                if n + 1 < len(units):
                    scores(n + 1)
                pe.wait_ge(exped, n + 1)
                for c in range(0, i + 1, 4):
                    m = min(4, i + 1 - c)
                    if turns >= 2:
                        pe.wait_ge(pt_read, turns - 1)
                    for j in range(m):
                        last = pe.transpose(t_ps[turns % 2][:, j * P:(j + 1) * P], probs[:, n % 2, (c + j) * P:(c + j + 1) * P], ident[:])
                    last.then_inc(pt_ready, 1)
                    turns += 1
                pe.wait_ge(pt_read, turns)
                if n >= 2:
                    pe.wait_ge(pv_read, n - 1)
                for j in range(i + 1):
                    last = pe.matmul(o_ps[n % 2][:, 0:DH], probsT[:, n % 2, j * P:(j + 1) * P], v[:, j, h * DH:(h + 1) * DH],
                                     start=(j == 0), stop=(j == i))
                last.then_inc(pv_ready, 1)
            pe.wait_ge(masked, 1)
            for n in range(NT * GROUPS):
                i, g = n // GROUPS, n % GROUPS
                if n >= 2:
                    pe.wait_ge(gated, n - 1)
                pe.matmul(t_ps[n % 2][:, 0:P], sw[:, g], va[:, i, g * P:(g + 1) * P], start=True, stop=True).then_inc(mixed, 1)


def output_projection(nc, dram, keep):
    with ExitStack() as ctx:
        sb = lambda name, shape, dt=F32: ctx.enter_context(nc.sbuf_tensor(name, shape, dt))
        sem = lambda name: ctx.enter_context(nc.semaphore(name))
        x_sb, attn, gate, ident = keep["x"], keep["q"], keep["u"], keep["ident"]
        hnT = keep["hnT"]
        mixT = sb("mixT", [P, 2, NK, P])
        w = sb("w_out", [P, NK, D])
        junk = sb("square_junk2", [P, D])
        hn = sb("hn", [P, 2, D])
        mw, ln2 = sb("mix_norm_w", [P, NK]), sb("ln2", [P, NK])
        ln2_row, hn_rows = sb("ln2_row", [P, D]), sb("hn_rows", [P, ROW_TILES, D])
        ssq, rstd = sb("mix_ssq", [P, 2 * NT]), sb("mix_rstd", [P, 2 * NT])
        ssq2, rstd2 = sb("ln2_ssq", [P, NT]), sb("ln2_rstd", [P, NT])
        turn_ps = [ctx.enter_context(nc.psum_tensor(f"mix_turn{b}", [P, BANK], F32)) for b in range(4)]
        out_ps = [ctx.enter_context(nc.psum_tensor(f"mix_out{b}", [P, BANK], F32)) for b in range(4)]
        w_in, small_in = sem("w_out_loaded"), sem("norms_loaded")
        dv = sem("dve_steps_o")
        ssq_ready, inv_ready, rstd_ready, scaled = sem("mix_ssq_ready"), sem("mix_inv_ready"), sem("mix_rstd_ready"), sem("mix_scaled")
        turned, turned_read, out_ready, added = sem("mix_turned"), sem("mix_turned_read"), sem("mix_product"), sem("x2_ready")
        ssq2_ready, inv2_ready, rstd2_ready = sem("x2_ssq_ready"), sem("x2_inv_ready"), sem("x2_rstd_ready")
        hn_ready, hn_turned, hn_read = sem("hn_ready"), sem("hn_turned"), sem("hn_turned_read")
        rows_ready, rows_stored = sem("hn_rows_ready"), sem("hn_rows_stored")
        block = ctx.enter_context(nc.Block())

        @block.sync
        def _(sp):
            sp.dma_start(mw[:], dram["mix_norm_w"]).then_inc(small_in, 16)
            sp.dma_start(ln2[:], dram["ln2"]).then_inc(small_in, 16)
            sp.dma_start(ln2_row[:], dram["ln2_row"].to_broadcast([P, D])).then_inc(small_in, 16)
            sp.dma_start(w[:], dram["w_out"].rearrange("(k p) n -> p k n", p=P)).then_inc(w_in, 16)
            sp.wait_ge(rows_ready, ROW_TILES)
            sp.dma_start(dram["hn_rows"], hn_rows[:]).then_inc(rows_stored, 16)
            sp.wait_ge(rows_stored, 16)

        @block.vector
        def _(dve):
            own = Steps(dve, dv)
            dve.wait_ge(small_in, 48)
            dve.wait_ge(ssq_ready, 2 * NT)
            own(dve.tensor_scalar(ssq[:], ssq[:], 1.0 / DA, EPS, ALU.mult, ALU.add))
            own.done()
            dve.reciprocal(ssq[:], ssq[:]).then_inc(inv_ready, 1)
            dve.wait_ge(rstd_ready, 1)

            def scale(i):
                dve.tensor_scalar(attn[:, i], attn[:, i], rstd[:, 2 * i:2 * i + 1], None, ALU.mult).then_inc(scaled, 1)
                dve.tensor_scalar(gate[:, i], gate[:, i], rstd[:, 2 * i + 1:2 * i + 2], None, ALU.mult).then_inc(scaled, 1)

            def mix_turned(i):
                if i >= 2:
                    dve.wait_ge(out_ready, 2 * (i - 1))
                for k in range(NK):
                    if k % 4 == 0:
                        dve.wait_ge(turned, 2 * i + k // 4 + 1)
                    last = dve.tensor_scalar(mixT[:, i % 2, k], turn_ps[2 * (i % 2) + k // 4][:, (k % 4) * P:(k % 4 + 1) * P],
                                             mw[:, k:k + 1], None, ALU.mult)
                    if k % 4 == 3:
                        last.then_inc(turned_read, 1)

            def residual(i):
                for c in range(2):
                    dve.wait_ge(out_ready, 2 * i + c + 1)
                    dve.tensor_tensor(x_sb[:, i, c * 512:(c + 1) * 512], x_sb[:, i, c * 512:(c + 1) * 512],
                                      out_ps[2 * (i % 2) + c][:], ALU.add).then_inc(added, 1)

            def inverse(i):
                dve.wait_ge(ssq2_ready, i + 1)
                own(dve.tensor_scalar(ssq2[:, i:i + 1], ssq2[:, i:i + 1], 1.0 / D, EPS, ALU.mult, ALU.add))
                own.done()
                dve.reciprocal(ssq2[:, i:i + 1], ssq2[:, i:i + 1]).then_inc(inv2_ready, 1)
                dve.wait_ge(rstd2_ready, i + 1)
                if i >= 2:
                    dve.wait_ge(hn_turned, 2 * (i - 1))
                dve.tensor_scalar(hn[:, i % 2], x_sb[:, i], rstd2[:, i:i + 1], None, ALU.mult).then_inc(hn_ready, 1)
                if i < ROW_TILES:
                    dve.wait_ge(hn_ready, i + 1)
                    dve.tensor_tensor(hn_rows[:, i], hn[:, i % 2], ln2_row[:], ALU.mult).then_inc(rows_ready, 1)

            def hn_out(i):
                cols = slice(i * P, (i + 1) * P)
                for k in range(NK):
                    if k % 4 == 0:
                        dve.wait_ge(hn_turned, 2 * i + k // 4 + 1)
                    last = dve.tensor_scalar(hnT[:, k, cols], out_ps[2 * (i % 2) + k // 4][:, (k % 4) * P:(k % 4 + 1) * P],
                                             ln2[:, k:k + 1], None, ALU.mult)
                    if k % 4 == 3:
                        last.then_inc(hn_read, 1)

            for i in range(NT):
                scale(i)
            mix_turned(0)
            for i in range(NT):
                residual(i)
                if i + 1 < NT:
                    mix_turned(i + 1)
                inverse(i)
                hn_out(i)

        @block.scalar
        def _(act):
            for i in range(NT):
                for n, t in enumerate((attn, gate)):
                    if i or n:
                        act.wait_ge(ssq_ready, 2 * i + n)
                    act.activation(junk[:, 0:DA], t[:, i], ACT.Square, accum_out=ssq[:, 2 * i + n:2 * i + n + 1]).then_inc(ssq_ready, 1)
            act.wait_ge(inv_ready, 1)
            act.activation(rstd[:], ssq[:], ACT.Sqrt).then_inc(rstd_ready, 1)
            for i in range(NT):
                act.wait_ge(added, 2 * i + 2)
                act.wait_ge(ssq_ready, 2 * NT)
                if i:
                    act.wait_ge(ssq2_ready, i)
                act.activation(junk[:], x_sb[:, i], ACT.Square, accum_out=ssq2[:, i:i + 1]).then_inc(ssq2_ready, 1)
                act.wait_ge(inv2_ready, i + 1)
                act.activation(rstd2[:, i:i + 1], ssq2[:, i:i + 1], ACT.Sqrt).then_inc(rstd2_ready, 1)

        @block.tensor
        def _(pe):
            def turn_mix(i):
                pe.wait_ge(scaled, 2 * (i + 1))
                if i >= 2:
                    pe.wait_ge(turned_read, 2 * (i - 1))
                for k in range(NK):
                    src = attn if k < 4 else gate
                    last = pe.transpose(turn_ps[2 * (i % 2) + k // 4][:, (k % 4) * P:(k % 4 + 1) * P], src[:, i, (k % 4) * P:(k % 4 + 1) * P], ident[:])
                    if k % 4 == 3:
                        last.then_inc(turned, 1)

            def project(i):
                pe.wait_ge(turned_read, 2 * (i + 1))
                if i >= 2:
                    pe.wait_ge(hn_read, 2 * (i - 1))
                for c in range(2):
                    for k in range(NK):
                        last = pe.matmul(out_ps[2 * (i % 2) + c][:], mixT[:, i % 2, k], w[:, k, c * 512:(c + 1) * 512],
                                         start=(k == 0), stop=(k == NK - 1))
                    last.then_inc(out_ready, 1)

            def turn_hn(i):
                pe.wait_ge(hn_ready, i + 1)
                pe.wait_ge(added, 2 * (i + 1))
                for k in range(NK):
                    last = pe.transpose(out_ps[2 * (i % 2) + k // 4][:, (k % 4) * P:(k % 4 + 1) * P], hn[:, i % 2, k * P:(k + 1) * P], ident[:])
                    if k % 4 == 3:
                        last.then_inc(hn_turned, 1)

            turn_mix(0)
            pe.wait_ge(w_in, 16)
            for i in range(NT):
                project(i)
                if i + 1 < NT:
                    turn_mix(i + 1)
                turn_hn(i)


def retrieval(nc, dram, keep):
    with ExitStack() as ctx:
        sb = lambda name, shape, dt=F32: ctx.enter_context(nc.sbuf_tensor(name, shape, dt))
        sem = lambda name: ctx.enter_context(nc.semaphore(name))
        psum = lambda name, shape: ctx.enter_context(nc.psum_tensor(name, shape, F32))
        hnT, hn_split, ident = keep["hnT"], keep["hn_split"], keep["ident"]
        wq = sb("w_query", [P, NK, HALVES * P])
        keys = sb("keysT", [P, HALVES, KEYS])
        qT = sb("queryT", [P, HALVES, P])
        scores = sb("key_scores", [P, HALVES, KEYS])
        top = sb("top_values", [P, HALVES, TOPK])
        topi = sb("top_index", [P, HALVES, TOPK], U32)
        topf = sb("top_index_bf16", [P, HALVES, TOPK], BF16)
        cand = sb("candidates", [P, PH, TOPK * TOPK])
        best = sb("best", [P, PH, TOPK])
        pos = sb("best_pos", [P, PH, TOPK], U32)
        pa = [sb(f"pos_part{n}", [P, PH * TOPK], U32) for n in range(2)]
        pf = [sb(f"pos_part_f{n}", [P, PH * TOPK]) for n in range(2)]
        onehot = [sb(f"pos_onehot{n}", [P, PH * TOPK, TOPK], BF16) for n in range(2)]
        picks = sb("picks", [P, 4, PH * TOPK])
        gates = sb("gates_by_token", [P, PH, TOPK])
        gate_hi = sb("gates_hi", [P, PH * TOPK], BF16)
        esum = sb("gate_sum", [P, PH])
        iota16 = sb("iota16", [P, TOPK])
        wait_mark = sb("wait_mark", [P, 32])
        u_raw, act_sb = sb("u_early", [P, NK, P]), sb("act_early", [P, DENSE])
        tile_copy = sb("tile_copy", [P, 2, DENSE])
        q_ps = [psum(f"query{b}", [P, 4, P]) for b in range(2)]
        s_ps = [psum(f"score_banks{b}", [P, 4, KEYS]) for b in range(2)]
        t_ps = psum("picks_bank", [P, 4, P])
        a_ps = [psum(f"act_bank{b}", [P, BANK]) for b in range(2)]
        keys_in, wq_in = sem("keys_loaded"), [sem(f"w_query_loaded{b}") for b in range(4)]
        dv = sem("dve_steps_r")
        iota_ready = sem("iota16_ready")
        q_ready, q_read, s_ready, s_read = sem("query_ready"), sem("query_read"), sem("key_scores_ready"), sem("key_scores_read")
        scores_used = sem("key_scores_used")
        shifted, exped, picked, turned, turned_read = (sem("best_shifted"), sem("gates_exped"), sem("picks_ready"),
                                                       sem("picks_turned"), sem("picks_turned_read"))
        u_in, act_ready, act_read, act_stored = sem("u_early_loaded"), sem("act_early_ready"), sem("act_early_read"), sem("act_early_stored")
        picks_stored = sem("picks_stored")
        copied, hi_done, lo_done = sem("hn_tile_copied"), sem("hn_hi_done"), sem("hn_lo_done")
        block = ctx.enter_context(nc.Block())
        FIRST_CHUNK = EARLY_FP32 - 1

        @block.sync
        def _(sp):
            def load_u(chunk):
                sp.dma_start(u_raw[:], dram["peer_u"][bass.ds(chunk, 1)].rearrange("o p k e -> (o p) k e")).then_inc(u_in, 16)

            def store_act(chunk, count):
                sp.wait_ge(act_read, 2 * count)
                sp.dma_start(dram["acts"][bass.ds(chunk, 1)].rearrange("o p t -> (o p) t"), act_sb[:]).then_inc(act_stored, 16)

            def store_picks(i):
                sp.wait_ge(picked, 2 * i + 2)
                sp.dma_start(dram["picks"][bass.ds(i, 1)].rearrange("o p n j -> (o p) (n j)"), picks[:].rearrange("p n j -> p (n j)")).then_inc(picks_stored, 16)

            w_dram = dram["w_query"].rearrange("(k p) n -> p k n", p=P)
            sp.dma_start(keys[:], dram["keysT"]).then_inc(keys_in, 16)
            for b in range(4):
                sp.dma_start(wq[:, :, b * 4 * P:(b + 1) * 4 * P], w_dram[:, :, b * 4 * P:(b + 1) * 4 * P]).then_inc(wq_in[b], 16)
            load_u(FIRST_CHUNK)
            sp.wait_ge(act_ready, 2)
            load_u(0)
            store_act(FIRST_CHUNK, 1)
            with sp.Fori(0, NT - 2) as i:
                sp.wait_ge(act_ready, 2 * i + 4)
                load_u(i + 1)
                store_act(i, i + 2)
                store_picks(i)
            store_act(NT - 2, NT)
            store_picks(NT - 2)
            store_picks(NT - 1)
            sp.wait_ge(act_stored, 16 * EARLY_FP32)
            sp.wait_ge(picks_stored, 16 * NT)

        @block.gpsimd
        def _(pool):
            pool.iota(iota16[:], [[1, TOPK]], base=0, channel_multiplier=0, allow_small_or_imprecise_dtypes=True).then_inc(iota_ready, 1)
            pool.wait_ge(iota_ready, 1)
            for k in range(NK):
                pool.wait_ge(hi_done, k + 1)
                pool.tensor_tensor(hn_split[:, k, 1, ROW_TOKENS:], tile_copy[:, k % 2], hn_split[:, k, 0, ROW_TOKENS:], ALU.subtract).then_inc(lo_done, 1)
                pool.wait_ge(lo_done, k + 1)

        @block.tensor
        def _(pe):
            def query(i, waits):
                for b in range(4):
                    if waits:
                        pe.wait_ge(wq_in[b], 16)
                    if not waits or b >= 2:
                        pe.wait_ge(q_read, 4 * i + b - 1)
                    for n in range(4):
                        for k in range(NK):
                            last = pe.matmul(q_ps[b % 2][:, n], wq[:, k, (4 * b + n) * P:(4 * b + n + 1) * P], hnT[:, k, bass.ts(i, P)],
                                             start=(k == 0), stop=(k == NK - 1))
                    last.then_inc(q_ready, 1)

            def score(i, fresh):
                for b in range(4):
                    pe.wait_ge(q_read, 4 * i + b + 1)
                    if not fresh or b >= 2:
                        pe.wait_ge(s_read, 4 * i + b - 1)
                    for n in range(4):
                        last = pe.matmul(s_ps[b % 2][:, n], qT[:, 4 * b + n], keys[:, 4 * b + n], start=True, stop=True)
                    last.then_inc(s_ready, 1)

            def early_chunk(count):
                pe.wait_ge(u_in, 16 * count)
                for half in range(2):
                    if not isinstance(count, int):
                        pe.wait_ge(act_read, 2 * count + half - 3)
                    for k in range(NK):
                        last = pe.matmul(a_ps[half][:, 0:HALF], u_raw[:, k], hnT[:, k, ROW_TOKENS + half * HALF:ROW_TOKENS + (half + 1) * HALF],
                                         start=(k == 0), stop=(k == NK - 1))
                    last.then_inc(act_ready, 1)

            def turn(i):
                pe.wait_ge(picked, 2 * i + 2)
                for n in range(4):
                    last = pe.transpose(t_ps[:, n], picks[:, n], ident[:])
                last.then_inc(turned, 1)

            pe.wait_ge(keys_in, 16)
            query(0, True)
            score(0, True)
            early_chunk(1)
            with pe.Fori(0, NT - 1) as i:
                query(i + 1, False)
                early_chunk(i + 2)
                score(i + 1, False)
                turn(i)
            turn(NT - 1)

        @block.scalar
        def _(act):
            def query_out(i):
                for b in range(4):
                    act.wait_ge(q_ready, 4 * i + b + 1)
                    if not isinstance(i, int):
                        act.wait_ge(s_ready, 4 * i)
                    act.activation(qT[:, 4 * b:4 * b + 4], q_ps[b % 2][:], ACT.Copy).then_inc(q_read, 1)

            def scores_out(i):
                for b in range(4):
                    act.wait_ge(s_ready, 4 * i + b + 1)
                    if not isinstance(i, int):
                        act.wait_ge(scores_used, HALVES * i)
                    act.activation(scores[:, 4 * b:4 * b + 4], s_ps[b % 2][:], ACT.Copy).then_inc(s_read, 1)

            def act_out(count):
                for half in range(2):
                    act.wait_ge(act_ready, 2 * count + half - 1)
                    if not isinstance(count, int):
                        act.wait_ge(act_stored, 16 * count - 16)
                    act.activation(act_sb[:, half * HALF:(half + 1) * HALF], a_ps[half][:, 0:HALF], ACT.Gelu_apprx_tanh).then_inc(act_read, 1)

            def exponents(i):
                act.wait_ge(shifted, i + 1)
                act.activation(gates[:], best[:], ACT.Exp).then_inc(exped, 1)

            def turned_out(i):
                act.wait_ge(turned, i + 1)
                act.wait_ge(picks_stored, 16 * i + 16)
                act.activation(keep["picksT"][:, :, bass.ts(i, P)], t_ps[:], ACT.Copy).then_inc(turned_read, 1)

            query_out(0)
            scores_out(0)
            act_out(1)
            with act.Fori(0, NT - 1) as i:
                query_out(i + 1)
                exponents(i)
                act_out(i + 2)
                scores_out(i + 1)
                turned_out(i)
            for k in range(NK):
                if k >= 2:
                    act.wait_ge(lo_done, k - 1)
                act.activation(tile_copy[:, k % 2], hnT[:, k, ROW_TOKENS:], ACT.Copy).then_inc(copied, 1)
                act.wait_ge(copied, k + 1)
                act.activation(hn_split[:, k, 0, ROW_TOKENS:], tile_copy[:, k % 2], ACT.Copy).then_inc(hi_done, 1)
            exponents(NT - 1)
            turned_out(NT - 1)

        @block.vector
        def _(dve):
            dve.wait_ge(iota_ready, 1)
            with dve.Fori(0, NT) as i:
                count, marks = [0], [0]

                def own(instruction):
                    count[0] += 1
                    instruction.then_inc(dv, 1)

                def wait_before_max(semaphore, value):
                    dve.wait_ge(semaphore, value)
                    dve.memset(wait_mark[:, marks[0]:marks[0] + 1], 0.0)
                    marks[0] += 1

                def done():
                    wait_before_max(dv, i * STEPS_PER_TILE + count[0])

                for hh in range(HALVES):
                    if hh % 4 == 0:
                        wait_before_max(s_read, 4 * i + hh // 4 + 1)
                    own(dve.max(top[:, hh, 0:8], scores[:, hh]))
                done()
                for hh in range(HALVES):
                    own(dve.max_index(topi[:, hh, 0:8], top[:, hh, 0:8], scores[:, hh]))
                done()
                for hh in range(HALVES):
                    own(dve.match_replace(scores[:, hh], top[:, hh, 0:8], scores[:, hh], LOWEST))
                done()
                for hh in range(HALVES):
                    own(dve.max(top[:, hh, 8:16], scores[:, hh]))
                done()
                for hh in range(HALVES):
                    dve.max_index(topi[:, hh, 8:16], top[:, hh, 8:16], scores[:, hh]).then_inc(scores_used, 1)
                halves = top[:].rearrange("p (h s) k -> p h s k", s=2)
                own(dve.tensor_tensor(cand[:].rearrange("p h (a b) -> p h a b", b=TOPK),
                                      halves[:, :, 0].unsqueeze(3).broadcast_to([P, PH, TOPK, TOPK]),
                                      halves[:, :, 1].unsqueeze(2).broadcast_to([P, PH, TOPK, TOPK]), ALU.add))
                dve.wait_ge(scores_used, HALVES * i + HALVES)
                own(dve.tensor_copy(topf[:], topi[:]))
                done()
                for h in range(PH):
                    own(dve.max(best[:, h, 0:8], cand[:, h]))
                done()
                for h in range(PH):
                    own(dve.max_index(pos[:, h, 0:8], best[:, h, 0:8], cand[:, h]))
                done()
                for h in range(PH):
                    own(dve.match_replace(cand[:, h], best[:, h, 0:8], cand[:, h], LOWEST))
                done()
                for h in range(PH):
                    own(dve.max(best[:, h, 8:16], cand[:, h]))
                done()
                for h in range(PH):
                    own(dve.max_index(pos[:, h, 8:16], best[:, h, 8:16], cand[:, h]))
                own(dve.tensor_copy(esum[:], best[:, :, 0]))
                done()
                dve.tensor_tensor(best[:], best[:], esum[:].unsqueeze(2).broadcast_to([P, PH, TOPK]), ALU.subtract).then_inc(shifted, 1)
                own(dve.tensor_single_scalar(pa[0][:], pos[:].rearrange("p h k -> p (h k)"), 4, ALU.logical_shift_right))
                own(dve.tensor_single_scalar(pa[1][:], pos[:].rearrange("p h k -> p (h k)"), 15, ALU.bitwise_and))
                done()
                for n in range(2):
                    own(dve.tensor_copy(pf[n][:], pa[n][:]))
                done()
                for n in range(2):
                    own(dve.tensor_tensor(onehot[n][:], pf[n][:].unsqueeze(2).broadcast_to([P, PH * TOPK, TOPK]),
                                          iota16[:].unsqueeze(1).broadcast_to([P, PH * TOPK, TOPK]), ALU.is_equal))
                done()
                pairs = topf[:].rearrange("p (h s) k -> p h s k", s=2)
                for n in range(2):
                    four = onehot[n][:].rearrange("p (h j) k -> p h j k", j=TOPK)
                    own(dve.tensor_tensor(four, four, pairs[:, :, n].unsqueeze(2).broadcast_to([P, PH, TOPK, TOPK]), ALU.mult))
                dve.wait_ge(exped, i + 1)
                own(dve.tensor_reduce(esum[:], gates[:], AX_X, ALU.add))
                done()
                own(dve.reciprocal(esum[:], esum[:]))
                for n in range(2):
                    own(dve.tensor_reduce(picks[:, n], onehot[n][:], AX_X, ALU.add))
                done()
                own(dve.tensor_tensor(gates[:], gates[:], esum[:].unsqueeze(2).broadcast_to([P, PH, TOPK]), ALU.mult))
                done()
                flat = gates[:].rearrange("p h k -> p (h k)")
                own(dve.tensor_copy(gate_hi[:], flat))
                done()
                dve.tensor_copy(picks[:, 2], gate_hi[:]).then_inc(picked, 1)
                dve.tensor_tensor(picks[:, 3], flat, gate_hi[:], ALU.subtract).then_inc(picked, 1)
                assert count[0] == STEPS_PER_TILE, count


STEPS_PER_TILE = 121
EARLY_FP32 = NT
EARLY = EARLY_FP32 + DENSE // TG // 2
EARLY_GROUPS = EARLY // GROUP
SCRATCH = {"gates": (P, NGROUP, DENSE // TG, GROUP, TG), "acts": (EARLY, P, DENSE), "picks": (NT, P, 4, PICKS),
           "hn_rows": (P, ROW_TILES, D)}


def gate_matrices(nc, dram, keep):
    with ExitStack() as ctx:
        sb = lambda name, shape, dt=F32: ctx.enter_context(nc.sbuf_tensor(name, shape, dt))
        sem = lambda name: ctx.enter_context(nc.semaphore(name))
        iota = sb("iota", [P, KEYS, TG], BF16)
        a = sb("onehot_i1", [P, 2, KEYS, TG], BF16)
        b = sb("onehot_i2", [P, KEYS, TG], BF16)
        bh, bl = sb("gated_hi", [P, 2, KEYS, TG], BF16), sb("gated_lo", [P, 2, KEYS, TG], BF16)
        stage = sb("gate_stage", [P, 2, KEYS, TG])
        u_raw, u_hi, u_lo = sb("u_early_raw", [P, 2, 4, P]), sb("u_early_hi", [P, 2, 4, P], BF16), sb("u_early_lo", [P, 2, 4, P], BF16)
        act_sb = sb("act_early2", [P, DENSE])
        g_ps = [ctx.enter_context(nc.psum_tensor(f"gates{n}", [P, 4, KEYS], F32)) for n in range(4)]
        a_ps = [ctx.enter_context(nc.psum_tensor(f"act_bank_g{n}", [P, BANK], F32)) for n in range(2)]
        hn_split, picksT = keep["hn_split"], keep["picksT"]
        iota_ready, b_ready, onehots = sem("iota_ready"), sem("onehot_i2_ready"), sem("onehots_ready")
        gates_ready, gates_read = sem("gates_ready"), sem("gates_read")
        stored = [sem("gates_stored0"), sem("gates_stored1")]
        u_in = [sem("u_part_loaded0"), sem("u_part_loaded1")]
        hi_ready, u_ready, u_used = sem("u_part_hi_ready"), sem("u_part_ready"), sem("u_part_used")
        act_ready, act_read, act_stored = sem("act2_ready"), sem("act2_read"), sem("act2_stored")
        block = ctx.enter_context(nc.Block())
        per = TG // 4
        PAIRS = DENSE // TG // 2
        gates_dram = dram["gates"]

        def over_pairs(engine, body):
            body(0, True)
            with engine.Fori(1, PAIRS) as pair:
                body(pair, False)

        @block.vector
        def _(dve):
            dve.wait_ge(iota_ready, 1)

            def build(pair, fresh):
                for s in range(2):
                    m = pair * 2 + s
                    tokens = lambda n: picksT[:, n, bass.ts(m + ROW_TOKENS // TG, TG)].unsqueeze(1).broadcast_to([P, KEYS, TG])
                    dve.tensor_tensor(b[:], iota[:], tokens(1), ALU.is_equal).then_inc(b_ready, 1)
                    if not fresh:
                        dve.wait_ge(gates_ready, per * (m - 1))
                    dve.tensor_tensor(a[:, s], iota[:], tokens(0), ALU.is_equal).then_inc(onehots, 1)
                    dve.wait_ge(b_ready, m + 1)
                    dve.tensor_tensor(bh[:, s], b[:], tokens(2), ALU.mult).then_inc(onehots, 1)
                    dve.tensor_tensor(bl[:, s], b[:], tokens(3), ALU.mult).then_inc(onehots, 1)
                    dve.wait_ge(onehots, 3 * m + 3)

            over_pairs(dve, build)

        @block.gpsimd
        def _(pool):
            pool.iota(iota[:], [[1, KEYS], [0, TG]], base=0, channel_multiplier=0, allow_small_or_imprecise_dtypes=True).then_inc(iota_ready, 1)
            pool.wait_ge(iota_ready, 1)

            def low(part, p):
                pool.wait_ge(hi_ready, part + 1)
                pool.tensor_tensor(u_lo[:, p], u_raw[:, p], u_hi[:, p], ALU.subtract).then_inc(u_ready, 1)
                pool.wait_ge(u_ready, part + 1)

            with pool.Fori(0, PAIRS) as pair:
                for p in range(2):
                    low(pair * 2 + p, p)

        @block.tensor
        def _(pe):
            def multiply(pair, fresh):
                for s in range(2):
                    m = pair * 2 + s
                    pe.wait_ge(onehots, 3 * m + 3)
                    for n in range(per):
                        if not (fresh and s == 0 and n < 4):
                            pe.wait_ge(gates_read, per * m + n - 3)
                        for t in range(4):
                            at = 4 * n + t
                            pe.matmul(g_ps[n % 4][:, t], a[:, s, :, at], bh[:, s, :, at], start=True, stop=False)
                            last = pe.matmul(g_ps[n % 4][:, t], a[:, s, :, at], bl[:, s, :, at], start=False, stop=True)
                        last.then_inc(gates_ready, 1)
                        k, half = (per * s + n) // 2, n % 2
                        if n == 0:
                            pe.wait_ge(u_ready, 2 * pair + s + 1)
                        if not fresh and s == 0 and n < 2:
                            pe.wait_ge(act_read, 2 * pair + half - 1)
                        for w, part in ((u_hi, 0), (u_hi, 1), (u_lo, 0)):
                            first, final = k == 0 and w is u_hi and part == 0, k == NK - 1 and w is u_lo
                            last = pe.matmul(a_ps[half][:, 0:HALF], w[:, s, k % 4],
                                             hn_split[:, k, part, ROW_TOKENS + half * HALF:ROW_TOKENS + (half + 1) * HALF],
                                             start=first, stop=final)
                        if k == NK - 1:
                            last.then_inc(act_ready, 1)
                        elif n == per - 1:
                            last.then_inc(u_used, 1)

            over_pairs(pe, multiply)

        @block.scalar
        def _(act):
            def high(part, p, fresh=False):
                act.wait_ge(u_in[p], (part - p) * 8 + 16)
                act.activation(u_hi[:, p], u_raw[:, p], ACT.Copy).then_inc(hi_ready, 1)

            def evacuate(pair, fresh):
                for s in range(2):
                    m = pair * 2 + s
                    if not fresh:
                        act.wait_ge(stored[s], pair * 16)
                    for n in range(per):
                        act.wait_ge(gates_ready, per * m + n + 1)
                        act.activation(stage[:, s, :, 4 * n:4 * n + 4].rearrange("p i t -> p t i"), g_ps[n % 4][:], ACT.Copy).then_inc(gates_read, 1)
                    if s == 0:
                        act.wait_ge(u_used, pair + 1)
                        high_next(pair, 0)
                for half in range(2):
                    act.wait_ge(act_ready, 2 * pair + half + 1)
                    if not fresh:
                        act.wait_ge(act_stored, 16 * pair)
                    act.activation(act_sb[:, half * HALF:(half + 1) * HALF], a_ps[half][:, 0:HALF], ACT.Gelu_apprx_tanh).then_inc(act_read, 1)
                high_next(pair, 1)

            def high_next(pair, p):
                if isinstance(pair, int) and pair == PAIRS - 1:
                    return
                high(pair * 2 + 2 + p, p)

            high(0, 0)
            high(1, 1)
            evacuate(0, True)
            with act.Fori(1, PAIRS - 1) as pair:
                evacuate(pair, False)
            evacuate(PAIRS - 1, False)

        @block.sync
        def _(sp):
            def load(pair, p):
                sp.dma_start(u_raw[:, p], dram["peer_u"][bass.ds(pair + EARLY_FP32, 1), :, 4 * p:4 * p + 4].rearrange("o p k e -> (o p) k e")).then_inc(u_in[p], 16)

            def turn(pair):
                for s in range(2):
                    if not (isinstance(pair, int) and pair == PAIRS - 1):
                        sp.wait_ge(u_ready, 2 * pair + s + 1)
                        load(pair + 1, s)
                    m = pair * 2 + s
                    sp.wait_ge(gates_read, per * (m + 1))
                    sp.dma_start(gates_dram[:, :, bass.ds(m, 1)].rearrange("p g o i t -> p g (o i t)"),
                                 stage[:, s].rearrange("p (g i) t -> p g (i t)", i=GROUP)).then_inc(stored[s], 16)
                sp.wait_ge(act_read, 2 * pair + 2)
                sp.dma_start(dram["acts"][bass.ds(pair + EARLY_FP32, 1)].rearrange("o p t -> (o p) t"), act_sb[:]).then_inc(act_stored, 16)

            load(0, 0)
            load(0, 1)
            with sp.Fori(0, PAIRS - 1) as pair:
                turn(pair)
            turn(PAIRS - 1)
            for s in range(2):
                sp.wait_ge(stored[s], 16 * PAIRS)
            sp.wait_ge(act_stored, 16 * PAIRS)


def experts(nc, dram, keep):
    with ExitStack() as ctx:
        sb = lambda name, shape, dt=F32: ctx.enter_context(nc.sbuf_tensor(name, shape, dt))
        sem = lambda name: ctx.enter_context(nc.semaphore(name))
        hn_hi, hn_lo, y = keep["hn_split"][:, :, 0, ROW_TOKENS:], keep["hn_split"][:, :, 1, ROW_TOKENS:], keep["x"]
        hn_row = keep["wide"].rearrange("p (b c) -> p b c", c=SEQ // 2)[:, :, 0:P].rearrange("p (t k) c -> p t k c", t=ROW_TILES)
        u_raw, v_raw = sb("u_raw", [P, 2, NK, P]), sb("v_raw", [P, 2, D])
        u_hi, u_lo = sb("u_hi", [P, 2, NK, P], BF16), sb("u_lo", [P, 2, NK, P], BF16)
        v_hi, v_lo = sb("v_hi", [P, 2, GROUP, D], BF16), sb("v_lo", [P, 2, GROUP, D], BF16)
        gates = sb("gates", [P, 2, DENSE // TG, GROUP, TG])
        act_sb = sb("gelu", [P, 2, DENSE])
        h_hi, h_lo = sb("h_hi", [P, 2, GROUP, DENSE], BF16), sb("h_lo", [P, 2, GROUP, DENSE], BF16)
        u_rows, v_rows = sb("u_rows", [P, ROW_TILES, NK, P]), sb("v_rows", [P, ROW_TILES, D])
        picks = keep["picksT"][:].rearrange("p n t -> p (n t)").bitcast(F32)[:, 0:ROW_TILES * 4 * PICKS].rearrange(
            "p (t n j) -> p t n j", t=ROW_TILES, n=4)
        expert = sb("expert_index", [P, ROW_TILES, PICKS], U32)
        expert_now = sb("expert_index_now", [P, 2, ROW_TILES, GROUP], U32)
        dots, row_act = sb("dots", [P, 2, ROW_TILES, GROUP]), sb("row_gelu", [P, 2, ROW_TILES, GROUP])
        mark = sb("pool_mark", [P, 2])
        a_ps = [ctx.enter_context(nc.psum_tensor(f"act{b}", [P, 2, BANK], F32)) for b in range(2)]
        y_ps = [ctx.enter_context(nc.psum_tensor(f"y{b}", [P, BANK], F32)) for b in range(4)]
        u_loaded, v_loaded, g_loaded, a_loaded = ([sem(f"{n}_loaded{s}") for s in range(2)] for n in ("u", "v", "gates", "acts"))
        u_hi_ready, u_split, v_hi_ready, v_split = sem("u_hi_ready"), sem("u_split"), sem("v_hi_ready"), sem("v_split")
        u_mult, gelu_ready, h_gated, h_hi_ready, h_product = sem("u_multiplied"), sem("gelu_ready"), sem("h_gated"), sem("h_hi_ready"), sem("h_product")
        y_ready, y_added, out_done = sem("y_ready"), sem("y_added"), sem("out_stored")
        rows_in, index_steps, index_ready = sem("row_inputs_loaded"), sem("index_steps"), sem("index_ready")
        u_row_in, v_row_in = ([sem(f"{n}_row_loaded{t}") for t in range(ROW_TILES)] for n in ("u", "v"))
        dotted, row_gelu, row_gated, row_added, marked = sem("row_dotted"), sem("row_gelu_ready"), sem("row_gated"), sem("row_added"), sem("pool_marked")
        block = ctx.enter_context(nc.Block())
        u_dram, v_dram, g_dram, a_dram = dram["peer_u"], dram["peer_v"], dram["gates"], dram["acts"]
        LAST = NGROUP - 1
        UNITS = 2 * (NT - ROW_TILES)
        PER_CHUNK = UNITS // GROUP

        def over_groups(engine, body):
            body(0, 0, True)
            body(1, 1, True)
            with engine.Fori(1, EARLY_GROUPS // 2) as pair:
                body(pair * 2, 0, True)
                body(pair * 2 + 1, 1, True)
            body(EARLY_GROUPS - 1, 0, True)
            body(EARLY_GROUPS, 1, False)
            with engine.Fori(EARLY_GROUPS // 2 + 1, NGROUP // 2 - 1) as pair:
                body(pair * 2, 0, False)
                body(pair * 2 + 1, 1, False)
            body(NGROUP - 2, 0, False)
            body(LAST, 1, False)

        def first(g):
            return isinstance(g, int) and g == 0

        @block.sync
        def _(sp):
            def load_u(n, s):
                sp.dma_start(u_raw[:, s], u_dram[bass.ds(n, 1)].rearrange("o p k e -> (o p) k e")).then_inc(u_loaded[s], 16)

            def load_v(n, s):
                sp.dma_start(v_raw[:, s], v_dram[:, bass.ds(n, 1)].rearrange("p o d -> p (o d)")).then_inc(v_loaded[s], 16)

            def load_g(g, s):
                sp.dma_start(gates[:, s].rearrange("p g i t -> p (g i t)"),
                             g_dram[:, bass.ds(g, 1)].rearrange("p o g i t -> p (o g i t)")).then_inc(g_loaded[s], 16)

            sp.dma_start(hn_row, dram["hn_rows"].rearrange("p t (k c) -> p t k c", c=P)).then_inc(rows_in, 16)
            sp.dma_start(picks, dram["picks"][0:ROW_TILES].rearrange("t p n j -> p t n j")).then_inc(rows_in, 16)
            load_g(0, 0)
            for n in range(2):
                load_v(n, n)
            for n in range(2):
                load_u(n + EARLY, n)

            def group(g, s, early):
                for c in range(GROUP):
                    n = g * GROUP + c
                    if early:
                        if not (first(g) and c < 2):
                            sp.wait_ge(h_gated, 2 * n - 2)
                        sp.dma_start(act_sb[:, c % 2], a_dram[bass.ds(n, 1)].rearrange("o p t -> (o p) t")).then_inc(a_loaded[c % 2], 16)
                    if c == 0 and not (isinstance(g, int) and g == LAST):
                        if not first(g):
                            sp.wait_ge(h_gated, 2 * GROUP * g)
                        load_g(g + 1, 1 - s)
                    if isinstance(g, int) and n + 2 >= KEYS:
                        continue
                    if not early:
                        sp.wait_ge(u_split, n - EARLY + 1)
                        load_u(n + 2, c % 2)
                    sp.wait_ge(v_split, n + 1)
                    load_v(n + 2, c % 2)

            over_groups(sp, group)
            for i in range(ROW_TILES, NT):
                sp.wait_ge(y_added, UNITS * LAST + 2 * (i - ROW_TILES) + 2)
                sp.dma_start(dram["out"][i * P:(i + 1) * P], y[:, i]).then_inc(out_done, 16)
            for i in range(ROW_TILES):
                sp.wait_ge(row_added, ROW_TILES * PICKS)
                sp.dma_start(dram["out"][i * P:(i + 1) * P], y[:, i]).then_inc(out_done, 16)
            sp.wait_ge(out_done, 16 * NT)

        @block.scalar
        def _(act):
            def split_u(m, c):
                act.wait_ge(u_loaded[c % 2], (m - c % 2) * 8 + 16)
                act.activation(u_hi[:, c % 2], u_raw[:, c % 2], ACT.Copy).then_inc(u_hi_ready, 1)

            def split_v(g, s, c):
                n = g * GROUP + c
                act.wait_ge(v_loaded[c % 2], (n - c % 2) * 8 + 16)
                if not (isinstance(g, int) and g < 2):
                    act.wait_ge(y_ready, UNITS * (g - 1))
                act.activation(v_hi[:, s, c], v_raw[:, c % 2], ACT.Copy).then_inc(v_hi_ready, 1)

            def gelu_rows(g, s):
                act.wait_ge(dotted, ROW_TILES * GROUP * (g + 1))
                act.activation(row_act[:, s], dots[:, s], ACT.Gelu_apprx_tanh).then_inc(row_gelu, 1)

            def group(g, s, early):
                for c in range(GROUP):
                    n = g * GROUP + c
                    if not early:
                        act.wait_ge(u_mult, n - EARLY + 1)
                        act.wait_ge(h_gated, 2 * n - 2)
                        for half in range(2):
                            cols = slice(half * HALF, (half + 1) * HALF)
                            act.activation(act_sb[:, c % 2, cols], a_ps[c % 2][:, half, 0:HALF], ACT.Gelu_apprx_tanh).then_inc(gelu_ready, 1)
                        if not (isinstance(g, int) and n + 2 >= KEYS):
                            split_u(n - EARLY + 2, c)
                    split_v(g, s, c)
                    if c == 0 and not first(g):
                        gelu_rows(g - 1, 1 - s)
                    if first(g) and c == 1:
                        split_u(0, 0)
                        split_u(1, 1)

            over_groups(act, group)
            gelu_rows(LAST, 1)

        @block.vector
        def _(dve):
            def split_u(m, c):
                dve.wait_ge(u_hi_ready, m + 1)
                dve.tensor_tensor(u_lo[:, c % 2], u_raw[:, c % 2], u_hi[:, c % 2], ALU.subtract).then_inc(u_split, 1)

            def add_y(g, c):
                for b in range(PER_CHUNK):
                    unit = PER_CHUNK * c + b
                    dve.wait_ge(y_ready, UNITS * g + unit + 1)
                    part = y[:, ROW_TILES + unit // 2, (unit % 2) * BANK:(unit % 2 + 1) * BANK]
                    if not first(g):
                        dve.wait_ge(y_added, UNITS * (g - 1) + unit + 1)
                    dve.tensor_tensor(part, part, y_ps[unit % 4][:], ALU.add).then_inc(y_added, 1)

            def index_now(g, s):
                dve.tensor_copy(expert_now[:, s], expert[:, :, bass.ds(g * GROUP, GROUP)]).then_inc(index_ready, 1)

            def dot_rows(g, s, c):
                n = g * GROUP + c
                for t in range(ROW_TILES):
                    dve.wait_ge(u_row_in[t], 16 * n + 16)
                    dve.tensor_tensor_reduce(u_rows[:, t], u_rows[:, t], hn_row[:, t], 1.0, 0.0, ALU.mult, ALU.add,
                                             dots[:, s, t, c:c + 1]).then_inc(dotted, 1)

            def gate_rows(g, s):
                dve.wait_ge(row_gelu, g + 1)
                dve.tensor_tensor(row_act[:, s], row_act[:, s], picks[:, :, 2, bass.ds(g * GROUP, GROUP)], ALU.mult).then_inc(row_gated, 1)
                dve.wait_ge(row_gated, g + 1)

            def add_rows(g, s, c):
                n = g * GROUP + c
                for t in range(ROW_TILES):
                    dve.wait_ge(v_row_in[t], 16 * n + 16)
                    if not (first(g) and c == 0):
                        dve.wait_ge(row_added, ROW_TILES * (n - 1) + t + 1)
                    dve.scalar_tensor_tensor(out=y[:, t], in0=v_rows[:, t], scalar=row_act[:, s, t, c:c + 1], in1=y[:, t],
                                             op0=ALU.mult, op1=ALU.add).then_inc(row_added, 1)

            def group(g, s, early):
                dve.wait_ge(g_loaded[s], (g - s) * 8 + 16)
                for c in range(GROUP):
                    n = g * GROUP + c
                    if early:
                        dve.wait_ge(a_loaded[c % 2], (n - c % 2) * 8 + 16)
                    for half in range(2):
                        cols = slice(half * HALF, (half + 1) * HALF)
                        if not early:
                            dve.wait_ge(gelu_ready, 2 * (n - EARLY) + half + 1)
                        g_part = gates[:, s, half * (HALF // TG):(half + 1) * (HALF // TG), c]
                        a_part = act_sb[:, c % 2, cols].rearrange("p (g t) -> p g t", t=TG)
                        dve.tensor_tensor(a_part, a_part, g_part, ALU.mult).then_inc(h_product, 1)
                    if not (isinstance(g, int) and g < 2):
                        dve.wait_ge(y_ready, UNITS * (g - 1))
                    for half in range(2):
                        cols = slice(half * HALF, (half + 1) * HALF)
                        dve.wait_ge(h_product, 2 * n + half + 1)
                        dve.tensor_copy(h_hi[:, s, c, cols], act_sb[:, c % 2, cols]).then_inc(h_hi_ready, 1)
                    if not early and not (isinstance(g, int) and n + 2 >= KEYS):
                        split_u(n - EARLY + 2, c)
                    for half in range(2):
                        cols = slice(half * HALF, (half + 1) * HALF)
                        dve.wait_ge(h_hi_ready, 2 * n + half + 1)
                        dve.tensor_tensor(h_lo[:, s, c, cols], act_sb[:, c % 2, cols], h_hi[:, s, c, cols], ALU.subtract).then_inc(h_gated, 1)
                    dve.wait_ge(v_hi_ready, n + 1)
                    dve.tensor_tensor(v_lo[:, s, c], v_raw[:, c % 2], v_hi[:, s, c], ALU.subtract).then_inc(v_split, 1)
                    if first(g) and c == 1:
                        split_u(0, 0)
                        split_u(1, 1)
                    dot_rows(g, s, c)
                    if not first(g):
                        add_y(g - 1, c)
                        if c == 0:
                            gate_rows(g - 1, 1 - s)
                        add_rows(g - 1, 1 - s, c)
                if not (isinstance(g, int) and g == LAST):
                    index_now(g + 1, 1 - s)

            own = Steps(dve, index_steps)
            dve.wait_ge(rows_in, 32)
            own(dve.scalar_tensor_tensor(out=picks[:, :, 0], in0=picks[:, :, 0], scalar=float(KEYS), in1=picks[:, :, 1],
                                         op0=ALU.mult, op1=ALU.add))
            own(dve.tensor_tensor(picks[:, :, 2], picks[:, :, 2], picks[:, :, 3], ALU.add))
            own.done()
            own(dve.tensor_copy(expert[:], picks[:, :, 0]))
            own.done()
            index_now(0, 0)
            over_groups(dve, group)
            for c in range(GROUP):
                add_y(LAST, c)
                if c == 0:
                    gate_rows(LAST, 1)
                add_rows(LAST, 1, c)

        @block.gpsimd
        def _(pool):
            def gather(rows, table, indices, loaded):
                pool.indirect_dma_start(rows, None, table, bass.IndirectOffsetOnAxis(ap=indices, axis=0)).then_inc(loaded, 16)

            def wait_before_gather(n, at, semaphore, value):
                pool.wait_ge(marked, n * 2 * ROW_TILES + at + 1)
                pool.wait_ge(semaphore, value)
                pool.tensor_tensor(mark[:, 0:1], mark[:, 1:2], mark[:, 1:2], ALU.add).then_inc(marked, 1)

            def v_gathers(g, s, c, n):
                for t in range(ROW_TILES):
                    if first(g) and c == 0:
                        wait_before_gather(n, ROW_TILES + t, index_ready, 1)
                    else:
                        wait_before_gather(n, ROW_TILES + t, row_added, ROW_TILES * (g * GROUP + c - 1) + t + 1)
                    gather(v_rows[:, t], dram["peer_v"].rearrange("a b d -> (a b) d"), expert_now[:, s, t, c:c + 1], v_row_in[t])

            def group(g, s, early):
                for c in range(GROUP):
                    n = g * GROUP + c
                    for t in range(ROW_TILES):
                        if t == 0 and c == 0:
                            wait_before_gather(n, t, index_ready, g + 1)
                        elif not (first(g) and c == 0):
                            wait_before_gather(n, t, dotted, ROW_TILES * (n - 1) + t + 1)
                        else:
                            wait_before_gather(n, t, index_ready, 1)
                        gather(u_rows[:, t].rearrange("p k c -> p (k c)"), dram["u_rows"], expert_now[:, s, t, c:c + 1], u_row_in[t])
                    if first(g):
                        for t in range(ROW_TILES):
                            wait_before_gather(n, ROW_TILES + t, index_ready, 1)
                    else:
                        v_gathers(g - 1, 1 - s, c, n)

            pool.memset(mark[:], 0.0).then_inc(marked, 1)
            over_groups(pool, group)
            for c in range(GROUP):
                for t in range(ROW_TILES):
                    pool.wait_ge(row_added, ROW_TILES * (LAST * GROUP + c - 1) + t + 1)
                    gather(v_rows[:, t], dram["peer_v"].rearrange("a b d -> (a b) d"), expert_now[:, 1, t, c:c + 1], v_row_in[t])

        @block.tensor
        def _(pe):
            def up(n, c):
                m = n - EARLY
                pe.wait_ge(u_split, m + 1)
                if not (isinstance(n, int) and m < 2):
                    pe.wait_ge(gelu_ready, 2 * m - 2)
                for half in range(2):
                    cols = slice(half * HALF, (half + 1) * HALF)
                    terms = [(w, x, k) for k in range(NK) for w, x in ((u_hi, hn_hi), (u_hi, hn_lo), (u_lo, hn_hi))]
                    for t, (w, x, k) in enumerate(terms):
                        last = pe.matmul(a_ps[c % 2][:, half, 0:HALF], w[:, c % 2, k], x[:, k, cols], start=(t == 0), stop=(t == len(terms) - 1))
                last.then_inc(u_mult, 1)

            def down(g, s, c):
                if c == 0:
                    pe.wait_ge(h_gated, 2 * GROUP * (g + 1))
                    pe.wait_ge(v_split, GROUP * (g + 1))
                for b in range(PER_CHUNK):
                    unit = PER_CHUNK * c + b
                    if not (first(g) and unit < 4):
                        pe.wait_ge(y_added, UNITS * g + unit + 1 - 4)
                    i, cols = unit // 2, slice((unit % 2) * BANK, (unit % 2 + 1) * BANK)
                    terms = [(h, v, e) for e in range(GROUP) for h, v in ((h_hi, v_hi), (h_hi, v_lo), (h_lo, v_hi))]
                    for t, (h, v, e) in enumerate(terms):
                        last = pe.matmul(y_ps[unit % 4][:], h[:, s, e, i * P:(i + 1) * P], v[:, s, e, cols], start=(t == 0), stop=(t == len(terms) - 1))
                    last.then_inc(y_ready, 1)

            def group(g, s, early):
                for c in range(GROUP):
                    if not early:
                        up(g * GROUP + c, c)
                    if not first(g):
                        down(g - 1, 1 - s, c)

            over_groups(pe, group)
            for c in range(GROUP):
                down(LAST, 1, c)


def build(nc, dram):
    with ExitStack() as ctx:
        sb = lambda name, shape, dt=F32: ctx.enter_context(nc.sbuf_tensor(name, shape, dt))
        keep = {"x": sb("x", [P, NT, D]), "ident": sb("ident", [P, P])}
        wide = sb("wide", [P, NK * SEQ])
        keep["wide"] = wide[:]
        keep["hnT"] = wide[:].rearrange("p (k t) -> p k t", t=SEQ)
        keep["hn_split"] = wide[:].bitcast(BF16).rearrange("p (k s t) -> p k s t", s=2, t=SEQ)
        keep["picksT"] = sb("picksT", [P, 4, SEQ], BF16)
        with ExitStack() as mixed:
            for name in ("q", "u"):
                keep[name] = mixed.enter_context(nc.sbuf_tensor(name, [P, NT, DA], F32))
            with ExitStack() as inner:
                for name in ("k", "v", "va"):
                    keep[name] = inner.enter_context(nc.sbuf_tensor(name, [P, NT, DA], F32))
                input_projection(nc, dram, keep)
                attention_and_gating(nc, dram, keep)
            if dram.get("stop") == "attn":
                return dump(nc, dram, [keep["q"], keep["u"]])
            output_projection(nc, dram, keep)
        if dram.get("stop") == "hn":
            return dump(nc, dram, [keep["x"], keep["hnT"]])
        retrieval(nc, dram, keep)
        if dram.get("stop") == "picks":
            return dump(nc, dram, [keep["picksT"]])
        gate_matrices(nc, dram, keep)
        experts(nc, dram, keep)


def dump(nc, dram, tensors):
    with nc.semaphore("dumped") as s, nc.Block() as block:
        @block.sync
        def _(sp):
            for n, t in enumerate(tensors):
                sp.dma_start(dram[f"dump{n}"], t[:] ).then_inc(s, 16)
            sp.wait_ge(s, 16 * len(tensors))


def laid_out(inputs):
    a = {k: np.asarray(v) for k, v in inputs.items()}
    column = lambda w: w.reshape(-1, P).T
    w_s = a["sgu_w"][0]
    u = a["peer_u"][0].reshape(KEYS, KEYS, NK, P)
    arrays = {
        "x": a["x"][0], "xT": a["x"][0].T, "ln1": column(a["ln1_w"][0]), "w_in": a["w_in"][0],
        "q_norm_w": a["q_norm_w"][0].reshape(DH, 1), "k_norm_w": a["k_norm_w"][0].reshape(DH, 1),
        "sgu_norm_w": a["sgu_norm_w"][0].reshape(1, DA), "sgu_wT": w_s.transpose(2, 0, 1), "sgu_b": a["sgu_b"][0].T,
        "mix_norm_w": column(a["mix_norm_w"][0]), "w_out": a["w_out"][0], "ln2": column(a["ln2_w"][0]),
        "rel_bias": a["rel_bias"], "w_query": a["peer_w_query"][0],
        "keysT": np.stack([a["peer_keys1"][0], a["peer_keys2"][0]], 1).reshape(HALVES, KEYS, P).transpose(2, 0, 1),
        "peer_u": u.transpose(1, 3, 2, 0),
        "ln2_row": a["ln2_w"][0].reshape(1, D),
        "u_rows": a["peer_u"][0],
        "peer_v": a["peer_v"][0].reshape(KEYS, KEYS, D),
    }
    arrays.update(shape_constants())
    return {k: np.ascontiguousarray(v) for k, v in arrays.items()}


def kernel(**inputs):
    import concourse.bacc as bacc
    from concourse.bass_utils import run_bass_kernel_spmd as run

    nc = bacc.Bacc("TRN2", target_bir_lowering=False, num_devices=1)
    arrays = laid_out(inputs)
    dram = {k: nc.dram_tensor(f"in_{k}", v.shape, F32, kind="ExternalInput").ap() for k, v in arrays.items()}
    dram["bias_scratch"] = nc.dram_tensor("bias_scratch", (HEADS, BIAS_LEN), F32, kind="Internal").ap()
    for name, shape in SCRATCH.items():
        dram[name] = nc.dram_tensor(f"{name}_scratch", shape, F32, kind="Internal").ap()
    dram["out"] = nc.dram_tensor("out", (SEQ, D), F32, kind="ExternalOutput").ap()
    build(nc, dram)
    result = run(nc, [{f"in_{k}": v for k, v in arrays.items()}], core_ids=[0])
    return result.results[0]["out"].reshape(1, SEQ, D)
```

```python
from contextlib import ExitStack

import numpy as np
import concourse.bass as bass
from concourse import mybir

F32 = mybir.dt.float32
BF16 = mybir.dt.bfloat16
U32 = mybir.dt.uint32
ALU = mybir.AluOpType
ACT = mybir.ActivationFunctionType
AX_X = mybir.AxisListType.X

P = 128
SEQ = 1024
D = 1024
NT = SEQ // P
NK = D // P
HEADS = 8
DH = 64
DA = HEADS * DH
GROUPS = 4
D_IN = 5 * DA
NPROJ = D_IN // 512
EPS = 1e-6
NEG = -1e30
BUCKETS = 32
PH = 8
TOPK = 16
KEYS = 128
HALVES = 2 * PH
LOWEST = -3.0e38
BIAS_LEN = SEQ + P
GROUP = 4
NGROUP = KEYS // GROUP
TG = 32
BANK = 512
ROW_TILES = 2
ROW_TOKENS = ROW_TILES * P
DENSE = SEQ - ROW_TOKENS
HALF = DENSE // 2
PICKS = PH * TOPK


def patterns(distance):
    r = distance
    return sum(((r >= 0) & (r <= w) & (r % d == 0)).astype(np.int64) for w, d in ((128, 1), (512, 4), (2048, 16)))


def shape_constants():
    r = (SEQ - 1) - np.arange(BIAS_LEN)
    d = np.maximum(r, 0)
    exact = BUCKETS // 2
    large = exact + (np.log(np.maximum(d, exact).astype(np.float32) / np.float32(exact))
                     / np.float32(np.log(2048 / exact)) * np.float32(BUCKETS - exact)).astype(np.int32)
    bucket = np.where(d < exact, d, np.minimum(large, BUCKETS - 1))
    count = patterns(r)
    table = np.zeros((BUCKETS + 1, BIAS_LEN), np.float32)
    table[bucket, np.arange(BIAS_LEN)] = 1.0
    table[BUCKETS] = np.where(count > 0, np.log(np.maximum(count, 1)), NEG)
    ident = np.eye(P, dtype=np.float32)
    return {"bias_table": table, "ident": ident, "flip": np.ascontiguousarray(ident[::-1])}


class Steps:

    def __init__(self, engine, sem):
        self.engine, self.sem, self.count = engine, sem, 0

    def __call__(self, instruction):
        self.count += 1
        instruction.then_inc(self.sem, 1)
        return self.count

    def done(self, upto=None):
        self.engine.wait_ge(self.sem, self.count if upto is None else upto)


def input_projection(nc, dram, keep):
    with ExitStack() as ctx:
        sb = lambda name, shape, dt=F32: ctx.enter_context(nc.sbuf_tensor(name, shape, dt))
        sem = lambda name: ctx.enter_context(nc.semaphore(name))
        xs = keep["wide"].rearrange("p (k t) -> p k t", t=SEQ)
        w = keep["w"].rearrange("p (s k n) -> p s k n", s=2, k=NK)
        scratch = sb("projection_scratch", [P, 3 * D])
        x_tile = scratch[:, 0:2 * D].rearrange("p (s d) -> p s d", s=2)
        junk = scratch[:, 2 * D:3 * D]
        table = scratch[0:BUCKETS + 1, 0:BIAS_LEN]
        bias_sb = scratch[0:HEADS, BIAS_LEN:2 * BIAS_LEN]
        relb = sb("rel_bias", [BUCKETS + 1, HEADS])
        qw, kw = sb("q_norm_w", [P, 1]), sb("k_norm_w", [P, 1])
        ssq, ms, rms, rstd = (sb(f"ln1_{n}", [P, NT]) for n in ("ssq", "ms", "inv", "rstd"))
        ln1 = sb("ln1", [P, NK])
        sgn = sb("sgu_norm", [P, DA])
        square = sb("head_squares", [P, 2, DA])
        hs = [sb(f"head_ssq{n}", [P, NT * HEADS]) for n in range(3)]
        acc = [ctx.enter_context(nc.psum_tensor(f"proj_acc{b}", [P, BANK], F32)) for b in range(8)]
        x_in, ln1_in, sgn_in = [sem("x_loaded0"), sem("x_loaded1")], sem("ln1_loaded"), sem("sgu_norm_loaded")
        first_in = [sem(f"first_loaded{k}") for k in range(NK)]
        w_in = [sem("w_in_loaded0"), sem("w_in_loaded1")]
        ssq_ready, ms_ready, inv_ready, rstd_ready = sem("ssq_ready"), sem("ms_ready"), sem("inv_ready"), sem("rstd_ready")
        xs_ready, proj_ready, proj_read_v, proj_read_a = sem("xs_ready"), sem("proj_ready"), sem("proj_read_v"), sem("proj_read_a")
        dv, head_inv, head_std, normed = sem("dve_steps_p"), sem("head_inv"), sem("head_rstd"), sem("normed")
        small_in, relb_in, table_in, ones_row = sem("small_loaded"), sem("rel_bias_loaded"), sem("bias_table_loaded"), sem("ones_row_ready")
        sgu_in, masked = sem("sgu_w_loaded"), sem("sgu_w_masked")
        turned, turned_read = sem("qk_turned"), sem("qk_turned_read")
        row_ready, row_read, bias_out = sem("bias_row_ready"), sem("bias_row_read"), sem("bias_stored")
        ident, flip, qT, kT = keep["ident"], keep["flip"], keep["qT"], keep["kT"]
        t_ps = acc[6:8]
        TURNS = 16

        def bank(g):
            return acc[g] if g < NT else acc[(g - NT) % 6]

        groups = [("q", 0), ("k", 1), ("va", 4), ("u", 3), ("v", 2)]
        w_dram = dram["w_in"].rearrange("(k p) n -> p k n", p=P)
        block = ctx.enter_context(nc.Block())

        @block.sync
        def _(sp):
            def load_w(n):
                column = groups[n][1]
                sp.dma_start(w[:, n % 2], w_dram[:, :, column * 512:(column + 1) * 512]).then_inc(w_in[n % 2], 16)

            sp.dma_start(ln1[:], dram["ln1"]).then_inc(ln1_in, 16)
            for k in range(NK):
                sp.dma_start(xs[:, k], dram["xT"][k * P:(k + 1) * P]).then_inc(first_in[k], 16)
                sp.dma_start(w[:, 0, k], w_dram[:, k, 0:512]).then_inc(first_in[k], 16)
            for name in ("ident", "flip"):
                sp.dma_start(keep[name][:], dram[name]).then_inc(ln1_in, 16)
            for i in range(NT):
                if i >= 2:
                    sp.wait_ge(ssq_ready, i - 1)
                sp.dma_start(x_tile[:, i % 2], dram["x"][i * P:(i + 1) * P]).then_inc(x_in[i % 2], 16)
                if i == 1:
                    load_w(1)
            for dst, src in ((qw[0:DH], dram["q_norm_w"]), (qw[DH:P], dram["q_norm_w"]),
                             (kw[0:DH], dram["k_norm_w"]), (kw[DH:P], dram["k_norm_w"])):
                sp.dma_start(dst, src).then_inc(small_in, 16)
            sp.dma_start(relb[0:BUCKETS], dram["rel_bias"]).then_inc(relb_in, 16)
            sp.dma_start(keep["sgu_w"][:], dram["sgu_wT"]).then_inc(sgu_in, 16)
            sp.dma_start(sgn[:], dram["sgu_norm_w"].to_broadcast([P, DA])).then_inc(sgn_in, 16)
            sp.wait_ge(ssq_ready, NT)
            sp.dma_start(table, dram["bias_table"]).then_inc(table_in, 16)
            for n in range(2, NPROJ):
                sp.wait_ge(proj_ready, NT * (n - 1))
                load_w(n)
            sp.wait_ge(row_read, 3)
            sp.dma_start(dram["bias_scratch"], bias_sb).then_inc(bias_out, 16)
            sp.wait_ge(bias_out, 16)

        @block.gpsimd
        def _(pool):
            pool.memset(relb[BUCKETS:BUCKETS + 1], 1.0).then_inc(ones_row, 1)
            pool.wait_ge(ones_row, 1)
            pool.wait_ge(sgu_in, 16)
            sw = keep["sgu_w"][:]
            pool.affine_select(out=sw, in_=sw, compare_op=ALU.is_ge, fill=0.0, base=0,
                               pattern=[[0, GROUPS], [1, P]], channel_multiplier=-1).then_inc(masked, 1)
            pool.wait_ge(masked, 1)

        @block.vector
        def _(dve):
            own = Steps(dve, dv)
            dve.wait_ge(ln1_in, 16)
            for k in range(NK):
                dve.wait_ge(first_in[k], 32)
                dve.tensor_scalar(xs[:, k], xs[:, k], ln1[:, k:k + 1], None, ALU.mult).then_inc(xs_ready, 1)
            dve.wait_ge(ssq_ready, NT)
            dve.tensor_scalar(ms[:], ssq[:], 1.0 / D, EPS, ALU.mult, ALU.add).then_inc(ms_ready, 1)
            dve.wait_ge(ms_ready, 1)
            dve.reciprocal(rms[:], ms[:]).then_inc(inv_ready, 1)
            dve.wait_ge(rstd_ready, 1)

            def norm(n, t, dim):
                per = DA // dim
                summed = []
                for i in range(NT):
                    if i >= 2:
                        own.done(summed[i - 2])
                    own.done(own(dve.tensor_tensor(square[:, i % 2], t[:, i], t[:, i], ALU.mult)))
                    summed.append(own(dve.tensor_reduce(hs[n][:, i * per:(i + 1) * per],
                                                        square[:, i % 2].rearrange("p (h d) -> p h d", d=dim), AX_X, ALU.add)))
                own.done()
                runs, nrun = t.rearrange("p i (h d) -> p (i h) d", d=dim), NT * per
                own(dve.tensor_scalar(hs[n][:, 0:nrun], hs[n][:, 0:nrun], 1.0 / dim, EPS, ALU.mult, ALU.add))
                own.done()
                dve.reciprocal(hs[n][:, 0:nrun], hs[n][:, 0:nrun]).then_inc(head_inv, 1)
                dve.wait_ge(head_std, n + 1)
                dve.tensor_tensor(runs, runs, hs[n][:, 0:nrun].unsqueeze(2).broadcast_to([P, nrun, dim]), ALU.mult).then_inc(normed, 1)

            for n in (0, 1):
                out = keep[groups[n][0]]
                for i in range(NT):
                    g = n * NT + i
                    dve.wait_ge(proj_ready, g + 1)
                    dve.tensor_scalar(out[:, i], bank(g)[:], rstd[:, i:i + 1], None, ALU.mult).then_inc(proj_read_v, 1)
            for n in (0, 1):
                if n == 0:
                    dve.wait_ge(proj_read_v, 2 * NT)
                norm(n, keep[groups[n][0]], DH)
            dve.wait_ge(proj_read_a, NT)
            norm(2, keep["va"], P)
            dve.wait_ge(normed, 3)
            dve.wait_ge(sgn_in, 16)
            va = keep["va"]
            own(dve.tensor_tensor(va[:], va[:], sgn[:].unsqueeze(1).broadcast_to([P, NT, DA]), ALU.mult))
            for c in range(3):
                dve.wait_ge(row_ready, c + 1)
                dve.tensor_copy(bias_sb[:, c * 384:(c + 1) * 384], t_ps[c % 2][0:HEADS, 0:384]).then_inc(row_read, 1)
            dve.wait_ge(small_in, 16 * 4)
            dve.wait_ge(normed, 2)
            for n in range(TURNS):
                t, pair, half = n // 8, (n // 2) % 4, n % 2
                dve.wait_ge(turned, n + 1)
                dst = (qT if t == 0 else kT)[:, pair, half * 512:(half + 1) * 512]
                dve.tensor_scalar(dst, t_ps[n % 2][:], (qw if t == 0 else kw)[:, 0:1], DH ** -0.5 if t == 0 else 1.0,
                                  ALU.mult, ALU.mult).then_inc(turned_read, 1)

        @block.scalar
        def _(act):
            def head_rstd(n):
                act.wait_ge(head_inv, n + 1)
                c = NT * HEADS if n < 2 else NT * GROUPS
                act.activation(hs[n][:, 0:c], hs[n][:, 0:c], ACT.Sqrt).then_inc(head_std, 1)

            for i in range(NT):
                act.wait_ge(x_in[i % 2], 16 * (i // 2 + 1))
                if i:
                    act.wait_ge(ssq_ready, i)
                act.activation(junk, x_tile[:, i % 2], ACT.Square, accum_out=ssq[:, i:i + 1]).then_inc(ssq_ready, 1)
            act.wait_ge(inv_ready, 1)
            act.activation(rstd[:], rms[:], ACT.Sqrt).then_inc(rstd_ready, 1)
            act.wait_ge(rstd_ready, 1)
            for n in (2, 3, 4):
                name = groups[n][0]
                for i in range(NT):
                    g = n * NT + i
                    act.wait_ge(proj_ready, g + 1)
                    act.activation(keep[name][:, i], bank(g)[:], ACT.Copy if name == "v" else ACT.Gelu_apprx_tanh,
                                   scale=rstd[:, i:i + 1]).then_inc(proj_read_a, 1)
                    if n == 3 and i == 5:
                        head_rstd(2)
                if n == 2:
                    head_rstd(0)
                    head_rstd(1)

        @block.tensor
        def _(pe):
            for k in range(NK):
                pe.wait_ge(xs_ready, k + 1)
                pe.wait_ge(first_in[k], 32)
                for i in range(NT):
                    last = pe.matmul(acc[i][:], xs[:, k, i * P:(i + 1) * P], w[:, 0, k], start=(k == 0), stop=(k == NK - 1))
                    if k == NK - 1:
                        last.then_inc(proj_ready, 1)
            def turn(n):
                t, pair, half = n // 8, (n // 2) % 4, n % 2
                pe.wait_ge(normed, t + 1)
                if n >= 2:
                    pe.wait_ge(turned_read, n - 1)
                for j in range(4):
                    src, dst = keep["qk"[t]][:, half * 4 + j, pair * P:(pair + 1) * P], t_ps[n % 2][:, j * P:(j + 1) * P]
                    if t == 0:
                        last = pe.matmul(dst, src, flip[:], start=True, stop=True)
                    else:
                        last = pe.transpose(dst, src, ident[:])
                last.then_inc(turned, 1)

            for n in range(1, NPROJ):
                pe.wait_ge(w_in[n % 2], 16 * ((n + 1) // 2))
                for i in range(NT):
                    g = n * NT + i
                    before = g - NT if n == 1 and i < 6 else g - 6
                    if before < 2 * NT:
                        pe.wait_ge(proj_read_v, before + 1)
                    else:
                        pe.wait_ge(proj_read_a, before - 2 * NT + 1)
                    for k in range(NK):
                        last = pe.matmul(bank(g)[:], xs[:, k, i * P:(i + 1) * P], w[:, n % 2, k], start=(k == 0), stop=(k == NK - 1))
                    last.then_inc(proj_ready, 1)
                    row = {(3, 6): 0, (3, 7): 1, (4, 0): 2}.get((n, i))
                    if row is not None:
                        if row == 0:
                            pe.wait_ge(table_in, 16)
                            pe.wait_ge(relb_in, 16)
                            pe.wait_ge(ones_row, 1)
                            pe.wait_ge(proj_read_v, NT)
                        if row == 2:
                            pe.wait_ge(row_read, 1)
                        pe.matmul(t_ps[row % 2][0:HEADS, 0:384], relb[:], table[:, row * 384:(row + 1) * 384], start=True, stop=True).then_inc(row_ready, 1)
                    if n == 4:
                        if i == 0:
                            pe.wait_ge(ln1_in, 48)
                            pe.wait_ge(row_read, 3)
                        turn(2 * i)
                        turn(2 * i + 1)


def attention_and_gating(nc, dram, keep):
    with ExitStack() as ctx:
        sb = lambda name, shape, dt=F32: ctx.enter_context(nc.sbuf_tensor(name, shape, dt))
        sem = lambda name: ctx.enter_context(nc.semaphore(name))
        psum = lambda name: ctx.enter_context(nc.psum_tensor(name, [P, BANK], F32))
        q, k, v, u, va = (keep[n] for n in ("q", "k", "v", "u", "va"))
        ident, qT, kT = keep["ident"], keep["qT"], keep["kT"]
        bias = keep["wide"].rearrange("p (h t) -> p h t", t=SEQ)
        LOGITS = 3
        logits = sb("logits", [P, LOGITS, SEQ])
        probs = logits
        probsT = sb("probsT", [P, 2, SEQ])
        sw = keep["sgu_w"]
        sgb = sb("sgu_b", [P, GROUPS])
        mx, nmx, den, rden = (sb(f"row_{n}", [P, 4]) for n in ("max", "neg_max", "sum", "inv_sum"))
        s_ps = [ctx.enter_context(nc.psum_tensor(f"scores{b}", [P, 2 * BANK], F32)) for b in range(2)]
        t_ps = [psum("turned0"), psum("turned1")]
        o_ps = [psum("out0"), psum("out1")]
        mix_ps = [s_ps[b // 2][:, (b % 2) * BANK:(b % 2 + 1) * BANK] for b in range(4)] + [t[:] for t in t_ps + o_ps]
        bias_in = [sem("bias_loaded0"), sem("bias_loaded_rest")]
        sgu_in, w_out_in = sem("sgu_loaded"), sem("w_out_loaded")
        dv = sem("dve_steps")
        scored, biased, exped, nmax_ready = sem("scored"), sem("biased"), sem("exped"), sem("neg_max_ready")
        pt_ready, pt_read, pv_ready, pv_read = sem("probs_turned"), sem("probs_turned_read"), sem("pv_ready"), sem("pv_read")
        mixed, gated = sem("spatial_ready"), sem("spatial_read")
        block = ctx.enter_context(nc.Block())
        units = [(h, i) for h in range(HEADS) for i in (0, 1, 3, 5, 7, 6, 4, 2)]
        N = len(units)
        turns = [(n, c, min(4, i + 1 - c)) for n, (h, i) in enumerate(units) for c in range(0, i + 1, 4)]
        turns_of = lambda n: [j for j, t in enumerate(turns) if t[0] == n]
        scratch = dram["bias_scratch"]

        @block.sync
        def _(sp):
            sp.dma_start(sgb[:], dram["sgu_b"]).then_inc(sgu_in, 16)
            for h in range(HEADS):
                skewed = bass.AP(scratch.tensor, scratch.offset + h * BIAS_LEN, [[1, P], [1, SEQ]])
                sp.dma_start(bias[:, h], skewed).then_inc(bias_in[min(h, 1)], 16)
            for c in range(2):
                sp.dma_start(keep["w_out"][:, :, c * 512:(c + 1) * 512],
                             dram["w_out"].rearrange("(k p) n -> p k n", p=P)[:, :, c * 512:(c + 1) * 512]).then_inc(w_out_in, 16)
            sp.wait_ge(w_out_in, 32)

        @block.vector
        def _(dve):
            own = Steps(dve, dv)
            dve.wait_ge(sgu_in, 16)
            for n in range(2 * GROUPS):
                g, tiles = n // 2, slice(n % 2 * 4, n % 2 * 4 + 4)
                dve.wait_ge(mixed, n + 1)
                part = u[:, tiles, g * P:(g + 1) * P]
                dve.scalar_tensor_tensor(out=part, in0=mix_ps[n].rearrange("p (i c) -> p i c", c=P), scalar=sgb[:, g:g + 1],
                                         in1=part, op0=ALU.add, op1=ALU.mult).then_inc(gated, 1)

            def add_bias(n):
                h, i = units[n]
                w = (i + 1) * P
                if n == 0:
                    dve.wait_ge(bias_in[0], 16)
                if n == NT:
                    dve.wait_ge(bias_in[1], 16 * (HEADS - 1))
                dve.wait_ge(scored, n + 1)
                if n >= LOGITS:
                    dve.wait_ge(pt_ready, turns_of(n - LOGITS)[-1] + 1)
                dve.tensor_tensor_reduce(logits[:, n % LOGITS, 0:w], s_ps[n % 2][:, 0:w], bias[:, h, SEQ - w:SEQ], 1.0, LOWEST,
                                         ALU.add, ALU.max, mx[:, n % 4:n % 4 + 1]).then_inc(biased, 1)
                dve.wait_ge(biased, n + 1)
                dve.tensor_scalar(nmx[:, n % 4:n % 4 + 1], mx[:, n % 4:n % 4 + 1], -1.0, None, ALU.mult).then_inc(nmax_ready, 1)

            def out(n):
                h, i = units[n]
                dve.wait_ge(exped, n + 1)
                own(dve.reciprocal(rden[:, n % 4:n % 4 + 1], den[:, n % 4:n % 4 + 1]))
                own.done()
                dve.wait_ge(pv_ready, n + 1)
                dve.tensor_scalar(q[:, i, h * DH:(h + 1) * DH], o_ps[n % 2][:, 0:DH], rden[:, n % 4:n % 4 + 1], None, ALU.mult).then_inc(pv_read, 1)

            add_bias(0)
            add_bias(1)
            for n in range(N):
                if n + 2 < N:
                    add_bias(n + 2)
                if n >= 1:
                    out(n - 1)
            out(N - 1)

        @block.scalar
        def _(act):
            def exponents(n):
                w = (units[n][1] + 1) * P
                act.wait_ge(nmax_ready, n + 1)
                act.wait_ge(biased, n + 1)
                act.activation(probs[:, n % LOGITS, 0:w], logits[:, n % LOGITS, 0:w], ACT.Exp, bias=nmx[:, n % 4:n % 4 + 1],
                               accum_out=den[:, n % 4:n % 4 + 1]).then_inc(exped, 1)

            exponents(0)
            exponents(1)
            for n in range(N):
                if n >= 2:
                    act.wait_ge(pv_ready, n - 1)
                for j in turns_of(n):
                    _, c, m = turns[j]
                    act.wait_ge(pt_ready, j + 1)
                    act.activation(probsT[:, n % 2, c * P:(c + m) * P], t_ps[j % 2][:, 0:m * P], ACT.Copy).then_inc(pt_read, 1)
                if n + 2 < N:
                    exponents(n + 2)

        @block.tensor
        def _(pe):
            for n in range(2 * GROUPS):
                g = n // 2
                for j in range(4):
                    last = pe.matmul(mix_ps[n][:, j * P:(j + 1) * P], sw[:, g], va[:, n % 2 * 4 + j, g * P:(g + 1) * P], start=True, stop=True)
                last.then_inc(mixed, 1)

            def scores(n):
                h, i = units[n]
                base, w = DH * (h % 2), (i + 1) * P
                if n >= 2:
                    pe.wait_ge(biased, n - 1)
                else:
                    pe.wait_ge(gated, 2 * n + 2)
                for c in range(0, w, BANK):
                    m = min(BANK, w - c)
                    last = pe.matmul(s_ps[n % 2][:, c:c + m], qT[base:base + DH, h // 2, i * P:(i + 1) * P],
                                     kT[base:base + DH, h // 2, c:c + m], start=True, stop=True)
                last.then_inc(scored, 1)

            def turn(n):
                pe.wait_ge(exped, n + 1)
                for j in turns_of(n):
                    _, c, m = turns[j]
                    if j >= 2:
                        pe.wait_ge(pt_read, j - 1)
                    else:
                        pe.wait_ge(gated, j + 5)
                    for b in range(m):
                        last = pe.transpose(t_ps[j % 2][:, b * P:(b + 1) * P], probs[:, n % LOGITS, (c + b) * P:(c + b + 1) * P], ident[:])
                    last.then_inc(pt_ready, 1)

            def values(n):
                h, i = units[n]
                pe.wait_ge(pt_read, turns_of(n)[-1] + 1)
                if n >= 2:
                    pe.wait_ge(pv_read, n - 1)
                else:
                    pe.wait_ge(gated, n + 7)
                for j in range(i + 1):
                    last = pe.matmul(o_ps[n % 2][:, 0:DH], probsT[:, n % 2, j * P:(j + 1) * P], v[:, j, h * DH:(h + 1) * DH],
                                     start=(j == 0), stop=(j == i))
                last.then_inc(pv_ready, 1)

            scores(0)
            scores(1)
            turn(0)
            for n in range(N):
                if n + 2 < N:
                    scores(n + 2)
                if n + 1 < N:
                    turn(n + 1)
                values(n)


def output_projection(nc, dram, keep):
    with ExitStack() as ctx:
        sb = lambda name, shape, dt=F32: ctx.enter_context(nc.sbuf_tensor(name, shape, dt))
        sem = lambda name: ctx.enter_context(nc.semaphore(name))
        x_sb, attn, gate, ident, flip = keep["x"], keep["q"], keep["u"], keep["ident"], keep["flip"]
        hnT = keep["hnT"]
        mixT = sb("mixT", [P, 2, NK, P])
        w = keep["w_out"]
        junk = sb("square_junk2", [P, D])
        hn = sb("hn", [P, 2, D])
        mw, ln2 = sb("mix_norm_w", [P, NK]), sb("ln2", [P, NK])
        ln2_row, hn_rows = sb("ln2_row", [P, D]), sb("hn_rows", [P, ROW_TILES, D])
        ssq, rstd = sb("mix_ssq", [P, 2 * NT]), sb("mix_rstd", [P, 2 * NT])
        ssq2, rstd2 = sb("ln2_ssq", [P, NT]), sb("ln2_rstd", [P, NT])
        turn_ps = [ctx.enter_context(nc.psum_tensor(f"mix_turn{b}", [P, BANK], F32)) for b in range(4)]
        out_ps = [ctx.enter_context(nc.psum_tensor(f"mix_out{b}", [P, BANK], F32)) for b in range(4)]
        BATCHES = [(0, 1), (1, NT)]
        x_in, small_in, row_in = [sem("x_again_loaded0"), sem("x_again_loaded_rest")], sem("norms_loaded"), sem("ln2_row_loaded")
        dv = sem("dve_steps_o")
        ssq_ready, inv_ready, rstd_ready, scaled = sem("mix_ssq_ready"), sem("mix_inv_ready"), sem("mix_rstd_ready"), sem("mix_scaled")
        turned, turned_read, out_ready, added = sem("mix_turned"), sem("mix_turned_read"), sem("mix_product"), sem("x2_ready")
        ssq2_ready, inv2_ready, rstd2_ready = sem("x2_ssq_ready"), sem("x2_inv_ready"), sem("x2_rstd_ready")
        hn_ready, hn_turned, hn_read = sem("hn_ready"), sem("hn_turned"), sem("hn_turned_read")
        rows_ready, rows_stored = sem("hn_rows_ready"), sem("hn_rows_stored")
        block = ctx.enter_context(nc.Block())

        @block.sync
        def _(sp):
            sp.dma_start(mw[:], dram["mix_norm_w"]).then_inc(small_in, 16)
            sp.dma_start(ln2[:], dram["ln2"]).then_inc(small_in, 16)
            for i in range(NT):
                sp.dma_start(x_sb[:, i], dram["x"][i * P:(i + 1) * P]).then_inc(x_in[min(i, 1)], 16)
            sp.dma_start(ln2_row[:], dram["ln2_row"].to_broadcast([P, D])).then_inc(row_in, 16)
            sp.wait_ge(rows_ready, ROW_TILES)
            sp.dma_start(dram["hn_rows"], hn_rows[:]).then_inc(rows_stored, 16)
            sp.wait_ge(rows_stored, 16)

        @block.vector
        def _(dve):
            own = Steps(dve, dv)

            def mix_inverse(batch):
                lo, hi = BATCHES[batch]
                dve.wait_ge(ssq_ready, 2 * hi)
                own(dve.tensor_scalar(ssq[:, 2 * lo:2 * hi], ssq[:, 2 * lo:2 * hi], 1.0 / DA, EPS, ALU.mult, ALU.add))
                own.done()
                dve.reciprocal(ssq[:, 2 * lo:2 * hi], ssq[:, 2 * lo:2 * hi]).then_inc(inv_ready, 1)
                dve.wait_ge(rstd_ready, batch + 1)
                for i in range(lo, hi):
                    scale(i)

            def scale(i):
                dve.tensor_scalar(attn[:, i], attn[:, i], rstd[:, 2 * i:2 * i + 1], None, ALU.mult).then_inc(scaled, 1)
                dve.tensor_scalar(gate[:, i], gate[:, i], rstd[:, 2 * i + 1:2 * i + 2], None, ALU.mult).then_inc(scaled, 1)

            def mix_turned(i):
                if i >= 2:
                    dve.wait_ge(out_ready, 2 * (i - 1))
                for k in range(NK):
                    if k % 4 == 0:
                        dve.wait_ge(turned, 2 * i + k // 4 + 1)
                    last = dve.tensor_scalar(mixT[:, i % 2, k], turn_ps[2 * (i % 2) + k // 4][:, (k % 4) * P:(k % 4 + 1) * P],
                                             mw[:, k:k + 1], None, ALU.mult)
                    if k % 4 == 3:
                        last.then_inc(turned_read, 1)

            def residual(i):
                if i < 2:
                    dve.wait_ge(x_in[i], 16 if i == 0 else 16 * (NT - 1))
                for c in range(2):
                    dve.wait_ge(out_ready, 2 * i + c + 1)
                    dve.tensor_tensor(x_sb[:, i, c * 512:(c + 1) * 512], x_sb[:, i, c * 512:(c + 1) * 512],
                                      out_ps[2 * (i % 2) + c][:], ALU.add).then_inc(added, 1)

            def inverse(i):
                dve.wait_ge(ssq2_ready, i + 1)
                own(dve.tensor_scalar(ssq2[:, i:i + 1], ssq2[:, i:i + 1], 1.0 / D, EPS, ALU.mult, ALU.add))
                own.done()
                dve.reciprocal(ssq2[:, i:i + 1], ssq2[:, i:i + 1]).then_inc(inv2_ready, 1)
                dve.wait_ge(rstd2_ready, i + 1)
                if i >= 2:
                    dve.wait_ge(hn_turned, 2 * (i - 1))
                dve.tensor_scalar(hn[:, i % 2], x_sb[:, i], rstd2[:, i:i + 1], None, ALU.mult).then_inc(hn_ready, 1)
                if i < ROW_TILES:
                    dve.wait_ge(row_in, 16)
                    dve.wait_ge(hn_ready, i + 1)
                    dve.tensor_tensor(hn_rows[:, i], hn[:, i % 2], ln2_row[:], ALU.mult).then_inc(rows_ready, 1)

            def hn_out(i):
                cols = slice(i * P, (i + 1) * P)
                for k in range(NK):
                    if k % 4 == 0:
                        dve.wait_ge(hn_turned, 2 * i + k // 4 + 1)
                    last = dve.tensor_scalar(hnT[:, k, cols], out_ps[2 * (i % 2) + k // 4][:, (k % 4) * P:(k % 4 + 1) * P],
                                             ln2[:, k:k + 1], None, ALU.mult)
                    if k % 4 == 3:
                        last.then_inc(hn_read, 1)

            mix_inverse(0)
            dve.wait_ge(small_in, 32)
            mix_turned(0)
            mix_inverse(1)
            mix_turned(1)
            residual(0)
            inverse(0)
            for i in range(NT):
                if i + 2 < NT:
                    mix_turned(i + 2)
                if i + 1 < NT:
                    residual(i + 1)
                hn_out(i)
                if i + 1 < NT:
                    inverse(i + 1)

        @block.scalar
        def _(act):
            for batch, (lo, hi) in enumerate(BATCHES):
                for i in range(lo, hi):
                    for n, t in enumerate((attn, gate)):
                        if i or n:
                            act.wait_ge(ssq_ready, 2 * i + n)
                        act.activation(junk[:, 0:DA], t[:, i], ACT.Square, accum_out=ssq[:, 2 * i + n:2 * i + n + 1]).then_inc(ssq_ready, 1)
                act.wait_ge(inv_ready, batch + 1)
                act.activation(rstd[:, 2 * lo:2 * hi], ssq[:, 2 * lo:2 * hi], ACT.Sqrt).then_inc(rstd_ready, 1)
            for i in range(NT):
                act.wait_ge(added, 2 * i + 2)
                act.wait_ge(ssq_ready, 2 * NT)
                if i:
                    act.wait_ge(ssq2_ready, i)
                act.activation(junk[:], x_sb[:, i], ACT.Square, accum_out=ssq2[:, i:i + 1]).then_inc(ssq2_ready, 1)
                act.wait_ge(inv2_ready, i + 1)
                act.activation(rstd2[:, i:i + 1], ssq2[:, i:i + 1], ACT.Sqrt).then_inc(rstd2_ready, 1)

        @block.tensor
        def _(pe):
            def turn_mix(i):
                pe.wait_ge(scaled, 2 * (i + 1))
                if i >= 2:
                    pe.wait_ge(turned_read, 2 * (i - 1))
                for k in range(NK):
                    dst = turn_ps[2 * (i % 2) + k // 4][:, (k % 4) * P:(k % 4 + 1) * P]
                    if k < 4:
                        last = pe.matmul(dst, attn[:, i, k * P:(k + 1) * P], flip[:], start=True, stop=True)
                    else:
                        last = pe.transpose(dst, gate[:, i, (k - 4) * P:(k - 3) * P], ident[:])
                    if k % 4 == 3:
                        last.then_inc(turned, 1)

            def project(i):
                pe.wait_ge(turned_read, 2 * (i + 1))
                if i >= 2:
                    pe.wait_ge(hn_read, 2 * (i - 1))
                for c in range(2):
                    for k in range(NK):
                        last = pe.matmul(out_ps[2 * (i % 2) + c][:], mixT[:, i % 2, k], w[:, k, c * 512:(c + 1) * 512],
                                         start=(k == 0), stop=(k == NK - 1))
                    last.then_inc(out_ready, 1)

            def turn_hn(i):
                pe.wait_ge(hn_ready, i + 1)
                pe.wait_ge(added, 2 * (i + 1))
                for k in range(NK):
                    last = pe.transpose(out_ps[2 * (i % 2) + k // 4][:, (k % 4) * P:(k % 4 + 1) * P], hn[:, i % 2, k * P:(k + 1) * P], ident[:])
                    if k % 4 == 3:
                        last.then_inc(hn_turned, 1)

            turn_mix(0)
            project(0)
            turn_mix(1)
            for i in range(NT):
                if i + 2 < NT:
                    turn_mix(i + 2)
                if i + 1 < NT:
                    project(i + 1)
                turn_hn(i)


def first(n):
    return isinstance(n, int) and n == 0


def retrieval(nc, dram, keep):
    with ExitStack() as ctx:
        sb = lambda name, shape, dt=F32: ctx.enter_context(nc.sbuf_tensor(name, shape, dt))
        sem = lambda name: ctx.enter_context(nc.semaphore(name))
        psum = lambda name, shape: ctx.enter_context(nc.psum_tensor(name, shape, F32))
        hnT, hn_split, ident = keep["hnT"], keep["hn_split"], keep["ident"]
        wq = sb("w_query", [P, NK, HALVES * P])
        keys = sb("keysT", [P, HALVES, KEYS])
        qT = sb("queryT", [P, HALVES, P])
        scores = sb("key_scores", [P, HALVES, KEYS])
        top = sb("top_values", [P, HALVES, TOPK])
        topi = sb("top_index", [P, HALVES, TOPK], U32)
        topf = sb("top_index_bf16", [P, HALVES, TOPK], BF16)
        WIDE, NARROW = 4 * TOPK, (TOPK - 4) * 4
        cand = sb("candidates", [P, PH, WIDE + NARROW])
        best = sb("best", [P, PH, TOPK])
        pos = sb("best_pos", [P, PH, TOPK], U32)
        pa = [sb(f"pos_part{n}", [P, PH * TOPK], U32) for n in range(4)]
        wide_12 = sb("wide_row_12", [P, PH * TOPK])
        pf = [sb(f"pos_part_f{n}", [P, PH * TOPK]) for n in range(2)]
        onehot = [sb(f"pos_onehot{n}", [P, PH * TOPK, TOPK], BF16) for n in range(2)]
        picks = sb("picks", [P, 4, PH * TOPK])
        gates = sb("gates_by_token", [P, PH, TOPK])
        gate_hi = sb("gates_hi", [P, PH * TOPK], BF16)
        esum = sb("gate_sum", [P, PH])
        iota16 = sb("iota16", [P, TOPK])
        wait_mark = sb("wait_mark", [P, 32])
        u_raw, act_sb = sb("u_early", [P, NK, P]), sb("act_early", [P, DENSE])
        tile_copy = sb("tile_copy", [P, 2, DENSE])
        q_ps = [psum(f"query{b}", [P, 4, P]) for b in range(2)]
        s_ps = [psum(f"score_banks{b}", [P, 4, KEYS]) for b in range(2)]
        t_ps = psum("picks_bank", [P, 4, P])
        a_ps = [psum(f"act_bank{b}", [P, BANK]) for b in range(2)]
        keys_in, wq_in = sem("keys_loaded"), [sem(f"w_query_loaded{b}") for b in range(4)]
        dv = sem("dve_steps_r")
        iota_ready = sem("iota16_ready")
        q_ready, q_read, s_ready, s_read = sem("query_ready"), sem("query_read"), sem("key_scores_ready"), sem("key_scores_read")
        scores_used = sem("key_scores_used")
        shifted, exped, picked, turned, turned_read = (sem("best_shifted"), sem("gates_exped"), sem("picks_ready"),
                                                       sem("picks_turned"), sem("picks_turned_read"))
        u_in, act_ready, act_read, act_stored = sem("u_early_loaded"), sem("act_early_ready"), sem("act_early_read"), sem("act_early_stored")
        picks_stored = sem("picks_stored")
        copied, hi_done, lo_done = sem("hn_tile_copied"), sem("hn_hi_done"), sem("hn_lo_done")
        block = ctx.enter_context(nc.Block())

        @block.sync
        def _(sp):
            def load_u(e):
                sp.dma_start(u_raw[:], dram["peer_u"][bass.ds(e * GROUP, 1)].rearrange("o p k e -> (o p) k e")).then_inc(u_in, 16)

            def store_act(e):
                sp.wait_ge(act_read, 2 * e + 2)
                sp.dma_start(dram["acts"][bass.ds(e, 1)].rearrange("o p t -> (o p) t"), act_sb[:]).then_inc(act_stored, 16)

            def store_picks(i):
                sp.wait_ge(picked, 2 * i + 2)
                sp.dma_start(dram["picks"][bass.ds(i, 1)].rearrange("o p n j -> (o p) (n j)"), picks[:].rearrange("p n j -> p (n j)")).then_inc(picks_stored, 16)

            w_dram = dram["w_query"].rearrange("(k p) n -> p k n", p=P)
            for b in range(4):
                sp.dma_start(wq[:, :, b * 4 * P:(b + 1) * 4 * P], w_dram[:, :, b * 4 * P:(b + 1) * 4 * P]).then_inc(wq_in[b], 16)
                if b == 0:
                    sp.dma_start(keys[:], dram["keysT"]).then_inc(keys_in, 16)
            load_u(0)
            with sp.Fori(0, NT - 1) as i:
                sp.wait_ge(act_ready, 2 * i + 2)
                load_u(i + 1)
                store_act(i)
                store_picks(i)
            store_act(NT - 1)
            store_picks(NT - 1)
            sp.wait_ge(act_stored, 16 * EARLY_FP32)
            sp.wait_ge(picks_stored, 16 * NT)

        @block.gpsimd
        def _(pool):
            pool.iota(iota16[:], [[1, TOPK]], base=0, channel_multiplier=0, allow_small_or_imprecise_dtypes=True).then_inc(iota_ready, 1)
            pool.wait_ge(iota_ready, 1)
            pool.iota(keep["iota"][:], [[1, KEYS], [0, TG]], base=0, channel_multiplier=0, allow_small_or_imprecise_dtypes=True).then_inc(iota_ready, 1)
            pool.wait_ge(iota_ready, 2)
            for k in range(NK):
                pool.wait_ge(hi_done, k + 1)
                pool.tensor_tensor(hn_split[:, k, 1, ROW_TOKENS:], tile_copy[:, k % 2], hn_split[:, k, 0, ROW_TOKENS:], ALU.subtract).then_inc(lo_done, 1)
                pool.wait_ge(lo_done, k + 1)

        @block.tensor
        def _(pe):
            def query(i, b):
                if first(i):
                    pe.wait_ge(wq_in[b], 16)
                if not (first(i) and b < 2):
                    pe.wait_ge(q_read, 4 * i + b - 1)
                for n in range(4):
                    for k in range(NK):
                        last = pe.matmul(q_ps[b % 2][:, n], wq[:, k, (4 * b + n) * P:(4 * b + n + 1) * P], hnT[:, k, bass.ts(i, P)],
                                         start=(k == 0), stop=(k == NK - 1))
                last.then_inc(q_ready, 1)

            def score(i, b):
                if first(i) and b == 0:
                    pe.wait_ge(keys_in, 16)
                pe.wait_ge(q_read, 4 * i + b + 1)
                if not (first(i) and b < 2):
                    pe.wait_ge(s_read, 4 * i + b - 1)
                for n in range(4):
                    last = pe.matmul(s_ps[b % 2][:, n], qT[:, 4 * b + n], keys[:, 4 * b + n], start=True, stop=True)
                last.then_inc(s_ready, 1)

            def early_chunk(e):
                pe.wait_ge(u_in, 16 * e + 16)
                for half in range(2):
                    if not first(e):
                        pe.wait_ge(act_read, 2 * e + half - 1)
                    for k in range(NK):
                        last = pe.matmul(a_ps[half][:, 0:HALF], u_raw[:, k], hnT[:, k, ROW_TOKENS + half * HALF:ROW_TOKENS + (half + 1) * HALF],
                                         start=(k == 0), stop=(k == NK - 1))
                    last.then_inc(act_ready, 1)

            def turn(i):
                pe.wait_ge(picked, 2 * i + 2)
                for n in range(4):
                    last = pe.transpose(t_ps[:, n], picks[:, n], ident[:])
                last.then_inc(turned, 1)

            query(0, 0)
            for b in range(4):
                if b + 1 < 4:
                    query(0, b + 1)
                score(0, b)
            early_chunk(0)
            with pe.Fori(0, NT - 1) as i:
                for b in range(4):
                    query(i + 1, b)
                early_chunk(i + 1)
                for b in range(4):
                    score(i + 1, b)
                turn(i)
            turn(NT - 1)

        @block.scalar
        def _(act):
            def query_out(i, b):
                act.wait_ge(q_ready, 4 * i + b + 1)
                if not first(i):
                    act.wait_ge(s_ready, 4 * i)
                act.activation(qT[:, 4 * b:4 * b + 4], q_ps[b % 2][:], ACT.Copy).then_inc(q_read, 1)

            def scores_out(i, b):
                act.wait_ge(s_ready, 4 * i + b + 1)
                if not first(i):
                    act.wait_ge(scores_used, HALVES * i)
                act.activation(scores[:, 4 * b:4 * b + 4], s_ps[b % 2][:], ACT.Copy).then_inc(s_read, 1)

            def act_out(e):
                for half in range(2):
                    act.wait_ge(act_ready, 2 * e + half + 1)
                    if not first(e):
                        act.wait_ge(act_stored, 16 * e)
                    act.activation(act_sb[:, half * HALF:(half + 1) * HALF], a_ps[half][:, 0:HALF], ACT.Gelu_apprx_tanh).then_inc(act_read, 1)

            def exponents(i):
                act.wait_ge(shifted, i + 1)
                act.activation(gates[:], best[:], ACT.Exp).then_inc(exped, 1)

            def turned_out(i):
                act.wait_ge(turned, i + 1)
                act.wait_ge(picks_stored, 16 * i + 16)
                act.activation(keep["picksT"][:, :, bass.ts(i, P)], t_ps[:], ACT.Copy).then_inc(turned_read, 1)

            query_out(0, 0)
            for b in range(4):
                if b + 1 < 4:
                    query_out(0, b + 1)
                scores_out(0, b)
            act_out(0)
            with act.Fori(0, NT - 1) as i:
                for b in range(4):
                    query_out(i + 1, b)
                exponents(i)
                act_out(i + 1)
                for b in range(4):
                    scores_out(i + 1, b)
                turned_out(i)
            for k in range(NK):
                if k >= 2:
                    act.wait_ge(lo_done, k - 1)
                act.activation(tile_copy[:, k % 2], hnT[:, k, ROW_TOKENS:], ACT.Copy).then_inc(copied, 1)
                act.wait_ge(copied, k + 1)
                act.activation(hn_split[:, k, 0, ROW_TOKENS:], tile_copy[:, k % 2], ACT.Copy).then_inc(hi_done, 1)
            exponents(NT - 1)
            turned_out(NT - 1)

        @block.vector
        def _(dve):
            dve.wait_ge(iota_ready, 1)
            with dve.Fori(0, NT) as i:
                count, marks = [0], [0]

                def own(instruction):
                    count[0] += 1
                    instruction.then_inc(dv, 1)

                def wait_before_max(semaphore, value):
                    dve.wait_ge(semaphore, value)
                    dve.memset(wait_mark[:, marks[0]:marks[0] + 1], 0.0)
                    marks[0] += 1

                def done():
                    wait_before_max(dv, i * STEPS_PER_TILE + count[0])

                for hh in range(HALVES):
                    if hh % 4 == 0:
                        wait_before_max(s_read, 4 * i + hh // 4 + 1)
                    own(dve.max(top[:, hh, 0:8], scores[:, hh]))
                done()
                for hh in range(HALVES):
                    own(dve.max_index(topi[:, hh, 0:8], top[:, hh, 0:8], scores[:, hh]))
                done()
                for hh in range(HALVES):
                    own(dve.match_replace(scores[:, hh], top[:, hh, 0:8], scores[:, hh], LOWEST))
                done()
                for hh in range(HALVES):
                    own(dve.max(top[:, hh, 8:16], scores[:, hh]))
                done()
                for hh in range(HALVES):
                    dve.max_index(topi[:, hh, 8:16], top[:, hh, 8:16], scores[:, hh]).then_inc(scores_used, 1)
                halves = top[:].rearrange("p (h s) k -> p h s k", s=2)
                for part, rows, width in ((cand[:, :, 0:WIDE], slice(0, 4), TOPK), (cand[:, :, WIDE:], slice(4, TOPK), 4)):
                    shape = [P, PH, rows.stop - rows.start, width]
                    own(dve.tensor_tensor(part.rearrange("p h (a b) -> p h a b", b=width),
                                          halves[:, :, 0, rows].unsqueeze(3).broadcast_to(shape),
                                          halves[:, :, 1, 0:width].unsqueeze(2).broadcast_to(shape), ALU.add))
                dve.wait_ge(scores_used, HALVES * i + HALVES)
                own(dve.tensor_copy(topf[:], topi[:]))
                done()
                for h in range(PH):
                    own(dve.max(best[:, h, 0:8], cand[:, h]))
                done()
                for h in range(PH):
                    own(dve.max_index(pos[:, h, 0:8], best[:, h, 0:8], cand[:, h]))
                done()
                for h in range(PH):
                    own(dve.match_replace(cand[:, h], best[:, h, 0:8], cand[:, h], LOWEST))
                done()
                for h in range(PH):
                    own(dve.max(best[:, h, 8:16], cand[:, h]))
                done()
                for h in range(PH):
                    own(dve.max_index(pos[:, h, 8:16], best[:, h, 8:16], cand[:, h]))
                own(dve.tensor_copy(esum[:], best[:, :, 0]))
                done()
                dve.tensor_tensor(best[:], best[:], esum[:].unsqueeze(2).broadcast_to([P, PH, TOPK]), ALU.subtract).then_inc(shifted, 1)
                flat_pos = pos[:].rearrange("p h k -> p (h k)")
                for n, (number, op) in enumerate(((4, ALU.logical_shift_right), (2, ALU.logical_shift_right),
                                                  (15, ALU.bitwise_and), (3, ALU.bitwise_and))):
                    own(dve.tensor_single_scalar(pa[n][:], flat_pos, number, op))
                own(dve.tensor_scalar(wide_12[:], flat_pos, float(WIDE), 12.0, ALU.is_lt, ALU.mult))
                done()
                own(dve.tensor_tensor(wide_12[:], wide_12[:], pa[3][:], ALU.add))
                own(dve.scalar_tensor_tensor(out=pf[0][:], in0=pa[1][:], scalar=12.0, in1=pa[0][:], op0=ALU.subtract, op1=ALU.max))
                done()
                own(dve.tensor_tensor(pf[1][:], wide_12[:], pa[2][:], ALU.min))
                done()
                for n in range(2):
                    own(dve.tensor_tensor(onehot[n][:], pf[n][:].unsqueeze(2).broadcast_to([P, PH * TOPK, TOPK]),
                                          iota16[:].unsqueeze(1).broadcast_to([P, PH * TOPK, TOPK]), ALU.is_equal))
                done()
                pairs = topf[:].rearrange("p (h s) k -> p h s k", s=2)
                for n in range(2):
                    four = onehot[n][:].rearrange("p (h j) k -> p h j k", j=TOPK)
                    own(dve.tensor_tensor(four, four, pairs[:, :, n].unsqueeze(2).broadcast_to([P, PH, TOPK, TOPK]), ALU.mult))
                dve.wait_ge(exped, i + 1)
                own(dve.tensor_reduce(esum[:], gates[:], AX_X, ALU.add))
                done()
                own(dve.reciprocal(esum[:], esum[:]))
                for n in range(2):
                    own(dve.tensor_reduce(picks[:, n], onehot[n][:], AX_X, ALU.add))
                done()
                own(dve.tensor_tensor(gates[:], gates[:], esum[:].unsqueeze(2).broadcast_to([P, PH, TOPK]), ALU.mult))
                done()
                flat = gates[:].rearrange("p h k -> p (h k)")
                own(dve.tensor_copy(gate_hi[:], flat))
                done()
                dve.tensor_copy(picks[:, 2], gate_hi[:]).then_inc(picked, 1)
                dve.tensor_tensor(picks[:, 3], flat, gate_hi[:], ALU.subtract).then_inc(picked, 1)
                assert count[0] == STEPS_PER_TILE, count


STEPS_PER_TILE = 126
EARLY_FP32 = NT
EARLY = EARLY_FP32 + DENSE // TG
assert EARLY == NGROUP
SCRATCH = {"gates": (P, DENSE // TG, KEYS, TG), "acts": (EARLY, P, DENSE), "picks": (NT, P, 4, PICKS),
           "hn_rows": (P, ROW_TILES, D)}


def gate_matrices(nc, dram, keep):
    with ExitStack() as ctx:
        sb = lambda name, shape, dt=F32: ctx.enter_context(nc.sbuf_tensor(name, shape, dt))
        sem = lambda name: ctx.enter_context(nc.semaphore(name))
        iota = keep["iota"]
        a = sb("onehot_i1", [P, 2, KEYS, TG], BF16)
        b = sb("onehot_i2", [P, KEYS, TG], BF16)
        bh, bl = sb("gated_hi", [P, 2, KEYS, TG], BF16), sb("gated_lo", [P, 2, KEYS, TG], BF16)
        stage = sb("gate_stage", [P, 2, KEYS, TG])
        u_raw, u_hi, u_lo = sb("u_early_raw", [P, 2, NK, P]), sb("u_early_hi", [P, 2, NK, P], BF16), sb("u_early_lo", [P, 2, NK, P], BF16)
        act_sb = sb("act_early2", [P, DENSE])
        g_ps = [ctx.enter_context(nc.psum_tensor(f"gates{n}", [P, 4, KEYS], F32)) for n in range(4)]
        a_ps = [ctx.enter_context(nc.psum_tensor(f"act_bank_g{n}", [P, BANK], F32)) for n in range(4)]
        hn_split, picksT = keep["hn_split"], keep["picksT"]
        b_ready, onehots = sem("onehot_i2_ready"), sem("onehots_ready")
        gates_ready, gates_read = sem("gates_ready"), sem("gates_read")
        stored = [sem("gates_stored0"), sem("gates_stored1")]
        u_in = [sem("u_chunk_loaded0"), sem("u_chunk_loaded1")]
        hi_ready, u_ready = sem("u_chunk_hi_ready"), sem("u_chunk_ready")
        act_ready, act_read, act_stored = sem("act2_ready"), sem("act2_read"), sem("act2_stored")
        block = ctx.enter_context(nc.Block())
        per = TG // 4
        PAIRS = DENSE // TG // 2
        gates_dram = dram["gates"]

        def over_pairs(engine, body):
            body(0, True)
            with engine.Fori(1, PAIRS) as pair:
                body(pair, False)

        @block.vector
        def _(dve):
            def build(pair, fresh):
                for s in range(2):
                    m = pair * 2 + s
                    tokens = lambda n: picksT[:, n, bass.ts(m + ROW_TOKENS // TG, TG)].unsqueeze(1).broadcast_to([P, KEYS, TG])
                    dve.tensor_tensor(b[:], iota[:], tokens(1), ALU.is_equal).then_inc(b_ready, 1)
                    if not fresh:
                        dve.wait_ge(gates_ready, per * (m - 1))
                    dve.tensor_tensor(a[:, s], iota[:], tokens(0), ALU.is_equal).then_inc(onehots, 1)
                    dve.wait_ge(b_ready, m + 1)
                    dve.tensor_tensor(bh[:, s], b[:], tokens(2), ALU.mult).then_inc(onehots, 1)
                    dve.tensor_tensor(bl[:, s], b[:], tokens(3), ALU.mult).then_inc(onehots, 1)
                    dve.wait_ge(onehots, 3 * m + 3)

            over_pairs(dve, build)

        @block.gpsimd
        def _(pool):
            def low(m, s):
                pool.wait_ge(hi_ready, m + 1)
                pool.tensor_tensor(u_lo[:, s], u_raw[:, s], u_hi[:, s], ALU.subtract).then_inc(u_ready, 1)
                pool.wait_ge(u_ready, m + 1)

            with pool.Fori(0, PAIRS) as pair:
                for s in range(2):
                    low(pair * 2 + s, s)

        @block.tensor
        def _(pe):
            def multiply(pair, fresh):
                for s in range(2):
                    m = pair * 2 + s
                    pe.wait_ge(onehots, 3 * m + 3)
                    for n in range(per):
                        if not (fresh and s == 0 and n < 4):
                            pe.wait_ge(gates_read, per * m + n - 3)
                        for t in range(4):
                            at = 4 * n + t
                            pe.matmul(g_ps[n % 4][:, t], a[:, s, :, at], bh[:, s, :, at], start=True, stop=False)
                            last = pe.matmul(g_ps[n % 4][:, t], a[:, s, :, at], bl[:, s, :, at], start=False, stop=True)
                        last.then_inc(gates_ready, 1)
                        if n == 0:
                            pe.wait_ge(u_ready, m + 1)
                        for half in range(2):
                            if not fresh and n == 0:
                                pe.wait_ge(act_read, 2 * m + half - 3)
                            tokens = slice(ROW_TOKENS + half * HALF, ROW_TOKENS + (half + 1) * HALF)
                            for w, part in ((u_hi, 0), (u_hi, 1), (u_lo, 0)):
                                last = pe.matmul(a_ps[2 * s + half][:, 0:HALF], w[:, s, n], hn_split[:, n, part, tokens],
                                                 start=(n == 0 and w is u_hi and part == 0), stop=(n == NK - 1 and w is u_lo))
                            if n == NK - 1:
                                last.then_inc(act_ready, 1)

            over_pairs(pe, multiply)

        @block.scalar
        def _(act):
            def high(m, s):
                act.wait_ge(u_in[s], (m - s) * 8 + 16)
                act.activation(u_hi[:, s], u_raw[:, s], ACT.Copy).then_inc(hi_ready, 1)

            def evacuate(pair, fresh, final=False):
                for s in range(2):
                    m = pair * 2 + s
                    if not fresh:
                        act.wait_ge(stored[s], pair * 16)
                    for n in range(per):
                        act.wait_ge(gates_ready, per * m + n + 1)
                        act.activation(stage[:, s, :, 4 * n:4 * n + 4].rearrange("p i t -> p t i"), g_ps[n % 4][:], ACT.Copy).then_inc(gates_read, 1)
                    for half in range(2):
                        act.wait_ge(act_ready, 2 * m + half + 1)
                        if not (fresh and s == 0):
                            act.wait_ge(act_stored, 16 * m)
                        act.activation(act_sb[:, half * HALF:(half + 1) * HALF], a_ps[2 * s + half][:, 0:HALF], ACT.Gelu_apprx_tanh).then_inc(act_read, 1)
                    if not final:
                        high(m + 2, s)

            high(0, 0)
            high(1, 1)
            evacuate(0, True)
            with act.Fori(1, PAIRS - 1) as pair:
                evacuate(pair, False)
            evacuate(PAIRS - 1, False, True)

        @block.sync
        def _(sp):
            def load(m, s):
                sp.dma_start(u_raw[:, s], dram["peer_u"][bass.ds((m + EARLY_FP32) * GROUP, 1)].rearrange("o p k e -> (o p) k e")).then_inc(u_in[s], 16)

            def turn(pair, final):
                for s in range(2):
                    m = pair * 2 + s
                    if not final:
                        sp.wait_ge(u_ready, m + 1)
                        load(m + 2, s)
                    sp.wait_ge(gates_read, per * (m + 1))
                    sp.dma_start(gates_dram[:, bass.ds(m, 1)].rearrange("p o i t -> p (o i t)"),
                                 stage[:, s].rearrange("p i t -> p (i t)")).then_inc(stored[s], 16)
                    sp.wait_ge(act_read, 2 * m + 2)
                    sp.dma_start(dram["acts"][bass.ds(m + EARLY_FP32, 1)].rearrange("o p t -> (o p) t"), act_sb[:]).then_inc(act_stored, 16)

            load(0, 0)
            load(1, 1)
            with sp.Fori(0, PAIRS - 1) as pair:
                turn(pair, False)
            turn(PAIRS - 1, True)
            for s in range(2):
                sp.wait_ge(stored[s], 16 * PAIRS)
            sp.wait_ge(act_stored, 16 * 2 * PAIRS)


def experts(nc, dram, keep):
    with ExitStack() as ctx:
        sb = lambda name, shape, dt=F32: ctx.enter_context(nc.sbuf_tensor(name, shape, dt))
        sem = lambda name: ctx.enter_context(nc.semaphore(name))
        hn_hi, hn_lo, y = keep["hn_split"][:, :, 0, ROW_TOKENS:], keep["hn_split"][:, :, 1, ROW_TOKENS:], keep["x"]
        hn_row = keep["wide"].rearrange("p (b c) -> p b c", c=SEQ // 2)[:, :, 0:P].rearrange("p (t k) c -> p t k c", t=ROW_TILES)
        u_raw, v_raw = sb("u_raw", [P, 2, NK, P]), sb("v_raw", [P, 2, D])
        u_hi, u_lo = sb("u_hi", [P, 2, NK, P], BF16), sb("u_lo", [P, 2, NK, P], BF16)
        v_hi, v_lo = sb("v_hi", [P, 2, GROUP, D], BF16), sb("v_lo", [P, 2, GROUP, D], BF16)
        gates = sb("gates", [P, 2, DENSE // TG, GROUP, TG])
        act_sb = sb("gelu", [P, 2, DENSE])
        h_hi, h_lo = sb("h_hi", [P, 2, GROUP, DENSE], BF16), sb("h_lo", [P, 2, GROUP, DENSE], BF16)
        u_rows, v_rows = sb("u_rows", [P, ROW_TILES, NK, P]), sb("v_rows", [P, ROW_TILES, D])
        picks = keep["picksT"][:].rearrange("p n t -> p (n t)").bitcast(F32)[:, 0:ROW_TILES * 4 * PICKS].rearrange(
            "p (t n j) -> p t n j", t=ROW_TILES, n=4)
        expert = sb("expert_index", [P, ROW_TILES, PICKS], U32)
        expert_now = sb("expert_index_now", [P, 2, ROW_TILES, GROUP], U32)
        dots, row_act = sb("dots", [P, 2, ROW_TILES, GROUP]), sb("row_gelu", [P, 2, ROW_TILES, GROUP])
        mark = sb("pool_mark", [P, 2])
        a_ps = [ctx.enter_context(nc.psum_tensor(f"act{b}", [P, 2, BANK], F32)) for b in range(2)]
        y_ps = [ctx.enter_context(nc.psum_tensor(f"y{b}", [P, BANK], F32)) for b in range(4)]
        u_loaded, v_loaded, g_loaded = ([sem(f"{n}_loaded{s}") for s in range(2)] for n in ("u", "v", "gates"))
        a_loaded = sem("acts_loaded")
        u_hi_ready, u_split, v_hi_ready, v_split = sem("u_hi_ready"), sem("u_split"), sem("v_hi_ready"), sem("v_split")
        u_mult, gelu_ready, h_gated, h_hi_ready, h_product = sem("u_multiplied"), sem("gelu_ready"), sem("h_gated"), sem("h_hi_ready"), sem("h_product")
        y_ready, y_added, out_done = sem("y_ready"), sem("y_added"), sem("out_stored")
        rows_in, index_steps, index_ready = sem("row_inputs_loaded"), sem("index_steps"), sem("index_ready")
        u_row_in, v_row_in = ([sem(f"{n}_row_loaded{t}") for t in range(ROW_TILES)] for n in ("u", "v"))
        dotted, row_gelu, row_gated, row_added, marked = sem("row_dotted"), sem("row_gelu_ready"), sem("row_gated"), sem("row_added"), sem("pool_marked")
        block = ctx.enter_context(nc.Block())
        u_dram, v_dram, g_dram, a_dram = dram["peer_u"], dram["peer_v"], dram["gates"], dram["acts"]
        LAST = NGROUP - 1
        UNITS = 2 * (NT - ROW_TILES)
        PER_CHUNK = UNITS // GROUP

        def over_groups(engine, body):
            body(0, 0)
            body(1, 1)
            with engine.Fori(1, NGROUP // 2 - 1) as pair:
                body(pair * 2, 0)
                body(pair * 2 + 1, 1)
            body(NGROUP - 2, 0)
            body(LAST, 1)

        def computed(g, s, c):
            return g * (GROUP - 1) + c - 1, (s * (GROUP - 1) + c - 1) % 2

        def two_on(g, c):
            there = (g, c + 2) if c + 2 < GROUP else (g + 1, c + 3 - GROUP)
            return None if isinstance(there[0], int) and there[0] > LAST else there

        @block.sync
        def _(sp):
            def load_u(n, s):
                sp.dma_start(u_raw[:, s], u_dram[bass.ds(n, 1)].rearrange("o p k e -> (o p) k e")).then_inc(u_loaded[s], 16)

            def load_v(n, s):
                sp.dma_start(v_raw[:, s], v_dram[bass.ds(n, 1)].rearrange("o p d -> (o p) d")).then_inc(v_loaded[s], 16)

            def load_g(g, s):
                sp.dma_start(gates[:, s].rearrange("p m i t -> p m (i t)"),
                             g_dram[:, :, bass.ds(g * GROUP, GROUP)].rearrange("p m i t -> p m (i t)")).then_inc(g_loaded[s], 16)

            for m in range(2):
                load_u(m + 1, m)
            sp.dma_start(hn_row, dram["hn_rows"].rearrange("p t (k c) -> p t k c", c=P)).then_inc(rows_in, 16)
            sp.dma_start(picks, dram["picks"][0:ROW_TILES].rearrange("t p n j -> p t n j")).then_inc(rows_in, 16)
            load_g(0, 0)
            for n in range(2):
                load_v(n, n)

            def group(g, s):
                for c in range(GROUP):
                    n = g * GROUP + c
                    if c == 0:
                        if not first(g):
                            sp.wait_ge(h_gated, 2 * n - 2)
                        sp.dma_start(act_sb[:, 0], a_dram[bass.ds(g, 1)].rearrange("o p t -> (o p) t")).then_inc(a_loaded, 16)
                    if c == 0 and not (isinstance(g, int) and g == LAST):
                        if not first(g):
                            sp.wait_ge(h_gated, 2 * GROUP * g)
                        load_g(g + 1, 1 - s)
                    if c > 0 and two_on(g, c):
                        m, p = computed(g, s, c)
                        g2, c2 = two_on(g, c)
                        sp.wait_ge(u_split, m + 1)
                        load_u(g2 * GROUP + c2, p)
                    if isinstance(g, int) and n + 2 >= KEYS:
                        continue
                    sp.wait_ge(v_split, n + 1)
                    load_v(n + 2, c % 2)

            over_groups(sp, group)
            for i in range(ROW_TILES, NT):
                sp.wait_ge(y_added, UNITS * LAST + 2 * (i - ROW_TILES) + 2)
                sp.dma_start(dram["out"][i * P:(i + 1) * P], y[:, i]).then_inc(out_done, 16)
            for i in range(ROW_TILES):
                sp.wait_ge(row_added, ROW_TILES * PICKS)
                sp.dma_start(dram["out"][i * P:(i + 1) * P], y[:, i]).then_inc(out_done, 16)
            sp.wait_ge(out_done, 16 * NT)

        @block.scalar
        def _(act):
            def split_u(m, p):
                act.wait_ge(u_loaded[p], (m - p) * 8 + 16)
                act.activation(u_hi[:, p], u_raw[:, p], ACT.Copy).then_inc(u_hi_ready, 1)

            def split_v(g, s, c):
                n = g * GROUP + c
                act.wait_ge(v_loaded[c % 2], (n - c % 2) * 8 + 16)
                if not (isinstance(g, int) and g < 2):
                    act.wait_ge(y_ready, UNITS * (g - 1))
                act.activation(v_hi[:, s, c], v_raw[:, c % 2], ACT.Copy).then_inc(v_hi_ready, 1)

            def gelu_rows(g, s):
                act.wait_ge(dotted, ROW_TILES * GROUP * (g + 1))
                act.activation(row_act[:, s], dots[:, s], ACT.Gelu_apprx_tanh).then_inc(row_gelu, 1)

            def group(g, s):
                for c in range(GROUP):
                    n = g * GROUP + c
                    if c > 0:
                        m, p = computed(g, s, c)
                        act.wait_ge(u_mult, m + 1)
                        if not (first(g) and c < 2):
                            act.wait_ge(h_gated, 2 * n - 2)
                        for half in range(2):
                            cols = slice(half * HALF, (half + 1) * HALF)
                            act.activation(act_sb[:, c % 2, cols], a_ps[p][:, half, 0:HALF], ACT.Gelu_apprx_tanh).then_inc(gelu_ready, 1)
                        if two_on(g, c):
                            split_u(m + 2, p)
                    split_v(g, s, c)
                    if c == 0 and not first(g):
                        gelu_rows(g - 1, 1 - s)

            split_u(0, 0)
            split_u(1, 1)
            over_groups(act, group)
            gelu_rows(LAST, 1)

        @block.vector
        def _(dve):
            def split_u(m, p):
                dve.wait_ge(u_hi_ready, m + 1)
                dve.tensor_tensor(u_lo[:, p], u_raw[:, p], u_hi[:, p], ALU.subtract).then_inc(u_split, 1)

            def add_y(g, c):
                for b in range(PER_CHUNK):
                    unit = PER_CHUNK * c + b
                    dve.wait_ge(y_ready, UNITS * g + unit + 1)
                    part = y[:, ROW_TILES + unit // 2, (unit % 2) * BANK:(unit % 2 + 1) * BANK]
                    if not first(g):
                        dve.wait_ge(y_added, UNITS * (g - 1) + unit + 1)
                    dve.tensor_tensor(part, part, y_ps[unit % 4][:], ALU.add).then_inc(y_added, 1)

            def index_now(g, s):
                dve.tensor_copy(expert_now[:, s], expert[:, :, bass.ds(g * GROUP, GROUP)]).then_inc(index_ready, 1)

            def dot_rows(g, s, c):
                n = g * GROUP + c
                for t in range(ROW_TILES):
                    dve.wait_ge(u_row_in[t], 16 * n + 16)
                    dve.tensor_tensor_reduce(u_rows[:, t], u_rows[:, t], hn_row[:, t], 1.0, 0.0, ALU.mult, ALU.add,
                                             dots[:, s, t, c:c + 1]).then_inc(dotted, 1)

            def gate_rows(g, s):
                dve.wait_ge(row_gelu, g + 1)
                dve.tensor_tensor(row_act[:, s], row_act[:, s], picks[:, :, 2, bass.ds(g * GROUP, GROUP)], ALU.mult).then_inc(row_gated, 1)
                dve.wait_ge(row_gated, g + 1)

            def add_rows(g, s, c):
                n = g * GROUP + c
                for t in range(ROW_TILES):
                    dve.wait_ge(v_row_in[t], 16 * n + 16)
                    if not (first(g) and c == 0):
                        dve.wait_ge(row_added, ROW_TILES * (n - 1) + t + 1)
                    dve.scalar_tensor_tensor(out=y[:, t], in0=v_rows[:, t], scalar=row_act[:, s, t, c:c + 1], in1=y[:, t],
                                             op0=ALU.mult, op1=ALU.add).then_inc(row_added, 1)

            def group(g, s):
                dve.wait_ge(g_loaded[s], (g - s) * 8 + 16)
                for c in range(GROUP):
                    n = g * GROUP + c
                    m, p = computed(g, s, c)
                    if c == 0:
                        dve.wait_ge(a_loaded, 16 * g + 16)
                    for half in range(2):
                        cols = slice(half * HALF, (half + 1) * HALF)
                        if c > 0:
                            dve.wait_ge(gelu_ready, 2 * m + half + 1)
                        g_part = gates[:, s, half * (HALF // TG):(half + 1) * (HALF // TG), c]
                        a_part = act_sb[:, c % 2, cols].rearrange("p (g t) -> p g t", t=TG)
                        dve.tensor_tensor(a_part, a_part, g_part, ALU.mult).then_inc(h_product, 1)
                    if not (isinstance(g, int) and g < 2):
                        dve.wait_ge(y_ready, UNITS * (g - 1))
                    for half in range(2):
                        cols = slice(half * HALF, (half + 1) * HALF)
                        dve.wait_ge(h_product, 2 * n + half + 1)
                        dve.tensor_copy(h_hi[:, s, c, cols], act_sb[:, c % 2, cols]).then_inc(h_hi_ready, 1)
                    if c > 0 and two_on(g, c):
                        split_u(m + 2, p)
                    for half in range(2):
                        cols = slice(half * HALF, (half + 1) * HALF)
                        dve.wait_ge(h_hi_ready, 2 * n + half + 1)
                        dve.tensor_tensor(h_lo[:, s, c, cols], act_sb[:, c % 2, cols], h_hi[:, s, c, cols], ALU.subtract).then_inc(h_gated, 1)
                    dve.wait_ge(v_hi_ready, n + 1)
                    dve.tensor_tensor(v_lo[:, s, c], v_raw[:, c % 2], v_hi[:, s, c], ALU.subtract).then_inc(v_split, 1)
                    dot_rows(g, s, c)
                    if not first(g):
                        add_y(g - 1, c)
                        if c == 0:
                            gate_rows(g - 1, 1 - s)
                        add_rows(g - 1, 1 - s, c)
                if not (isinstance(g, int) and g == LAST):
                    index_now(g + 1, 1 - s)

            split_u(0, 0)
            split_u(1, 1)
            own = Steps(dve, index_steps)
            dve.wait_ge(rows_in, 32)
            own(dve.scalar_tensor_tensor(out=picks[:, :, 0], in0=picks[:, :, 1], scalar=float(KEYS), in1=picks[:, :, 0],
                                         op0=ALU.mult, op1=ALU.add))
            own(dve.tensor_tensor(picks[:, :, 2], picks[:, :, 2], picks[:, :, 3], ALU.add))
            own.done()
            own(dve.tensor_copy(expert[:], picks[:, :, 0]))
            own.done()
            index_now(0, 0)
            over_groups(dve, group)
            for c in range(GROUP):
                add_y(LAST, c)
                if c == 0:
                    gate_rows(LAST, 1)
                add_rows(LAST, 1, c)

        @block.gpsimd
        def _(pool):
            def gather(rows, table, indices, loaded):
                pool.indirect_dma_start(rows, None, table, bass.IndirectOffsetOnAxis(ap=indices, axis=0)).then_inc(loaded, 16)

            def wait_before_gather(n, at, semaphore, value):
                pool.wait_ge(marked, n * 2 * ROW_TILES + at + 1)
                pool.wait_ge(semaphore, value)
                pool.tensor_tensor(mark[:, 0:1], mark[:, 1:2], mark[:, 1:2], ALU.add).then_inc(marked, 1)

            def v_gathers(g, s, c, n):
                for t in range(ROW_TILES):
                    if first(g) and c == 0:
                        wait_before_gather(n, ROW_TILES + t, index_ready, 1)
                    else:
                        wait_before_gather(n, ROW_TILES + t, row_added, ROW_TILES * (g * GROUP + c - 1) + t + 1)
                    gather(v_rows[:, t], dram["peer_v"].rearrange("a b d -> (a b) d"), expert_now[:, s, t, c:c + 1], v_row_in[t])

            def group(g, s):
                for c in range(GROUP):
                    n = g * GROUP + c
                    for t in range(ROW_TILES):
                        if t == 0 and c == 0:
                            wait_before_gather(n, t, index_ready, g + 1)
                        elif not (first(g) and c == 0):
                            wait_before_gather(n, t, dotted, ROW_TILES * (n - 1) + t + 1)
                        else:
                            wait_before_gather(n, t, index_ready, 1)
                        gather(u_rows[:, t].rearrange("p k c -> p (k c)"), dram["u_rows"], expert_now[:, s, t, c:c + 1], u_row_in[t])
                    if first(g):
                        for t in range(ROW_TILES):
                            wait_before_gather(n, ROW_TILES + t, index_ready, 1)
                    else:
                        v_gathers(g - 1, 1 - s, c, n)

            pool.memset(mark[:], 0.0).then_inc(marked, 1)
            over_groups(pool, group)
            for c in range(GROUP):
                for t in range(ROW_TILES):
                    pool.wait_ge(row_added, ROW_TILES * (LAST * GROUP + c - 1) + t + 1)
                    gather(v_rows[:, t], dram["peer_v"].rearrange("a b d -> (a b) d"), expert_now[:, 1, t, c:c + 1], v_row_in[t])

        @block.tensor
        def _(pe):
            def up(m, p):
                pe.wait_ge(u_split, m + 1)
                if not (isinstance(m, int) and m < 2):
                    pe.wait_ge(gelu_ready, 2 * m - 2)
                for half in range(2):
                    cols = slice(half * HALF, (half + 1) * HALF)
                    terms = [(w, x, k) for k in range(NK) for w, x in ((u_hi, hn_hi), (u_hi, hn_lo), (u_lo, hn_hi))]
                    for t, (w, x, k) in enumerate(terms):
                        last = pe.matmul(a_ps[p][:, half, 0:HALF], w[:, p, k], x[:, k, cols], start=(t == 0), stop=(t == len(terms) - 1))
                last.then_inc(u_mult, 1)

            def down(g, s, c):
                if c == 0:
                    pe.wait_ge(h_gated, 2 * GROUP * (g + 1))
                    pe.wait_ge(v_split, GROUP * (g + 1))
                for b in range(PER_CHUNK):
                    unit = PER_CHUNK * c + b
                    if not (first(g) and unit < 4):
                        pe.wait_ge(y_added, UNITS * g + unit + 1 - 4)
                    i, cols = unit // 2, slice((unit % 2) * BANK, (unit % 2 + 1) * BANK)
                    terms = [(h, v, e) for e in range(GROUP) for h, v in ((h_hi, v_hi), (h_hi, v_lo), (h_lo, v_hi))]
                    for t, (h, v, e) in enumerate(terms):
                        last = pe.matmul(y_ps[unit % 4][:], h[:, s, e, i * P:(i + 1) * P], v[:, s, e, cols], start=(t == 0), stop=(t == len(terms) - 1))
                    last.then_inc(y_ready, 1)

            def group(g, s):
                for c in range(GROUP):
                    if c > 0:
                        up(*computed(g, s, c))
                    if not first(g):
                        down(g - 1, 1 - s, c)

            over_groups(pe, group)
            for c in range(GROUP):
                down(LAST, 1, c)


def build(nc, dram):
    with ExitStack() as ctx:
        sb = lambda name, shape, dt=F32: ctx.enter_context(nc.sbuf_tensor(name, shape, dt))
        keep = {"x": sb("x", [P, NT, D]), "ident": sb("ident", [P, P]), "flip": sb("flip", [P, P])}
        wide = sb("wide", [P, NK * SEQ])
        keep["wide"] = wide[:]
        keep["hnT"] = wide[:].rearrange("p (k t) -> p k t", t=SEQ)
        keep["hn_split"] = wide[:].bitcast(BF16).rearrange("p (k s t) -> p k s t", s=2, t=SEQ)
        keep["picksT"] = sb("picksT", [P, 4, SEQ], BF16)
        for n, name in enumerate(("qT", "kT")):
            keep[name] = keep["x"][:, 4 * n:4 * n + 4]
        with ExitStack() as mixed:
            weights = mixed.enter_context(nc.sbuf_tensor("weights", [P, NK * D], F32))
            keep["w"], keep["w_out"] = weights[:], weights[:].rearrange("p (k n) -> p k n", n=D)
            for name in ("q", "u"):
                keep[name] = mixed.enter_context(nc.sbuf_tensor(name, [P, NT, DA], F32))
            with ExitStack() as inner:
                keep["sgu_w"] = inner.enter_context(nc.sbuf_tensor("sgu_w", [P, GROUPS, P], F32))
                for name in ("k", "v", "va"):
                    keep[name] = inner.enter_context(nc.sbuf_tensor(name, [P, NT, DA], F32))
                input_projection(nc, dram, keep)
                attention_and_gating(nc, dram, keep)
            output_projection(nc, dram, keep)
        matching = ctx.enter_context(ExitStack())
        keep["iota"] = matching.enter_context(nc.sbuf_tensor("iota", [P, KEYS, TG], BF16))
        retrieval(nc, dram, keep)
        gate_matrices(nc, dram, keep)
        matching.close()
        experts(nc, dram, keep)


def laid_out(inputs):
    a = {k: np.asarray(v) for k, v in inputs.items()}
    column = lambda w: w.reshape(-1, P).T
    w_s = a["sgu_w"][0]
    u = a["peer_u"][0].reshape(KEYS, KEYS, NK, P)
    arrays = {
        "x": a["x"][0], "xT": a["x"][0].T, "ln1": column(a["ln1_w"][0]), "w_in": a["w_in"][0],
        "q_norm_w": a["q_norm_w"][0].reshape(DH, 1), "k_norm_w": a["k_norm_w"][0].reshape(DH, 1),
        "sgu_norm_w": a["sgu_norm_w"][0].reshape(1, DA), "sgu_wT": w_s.transpose(2, 0, 1), "sgu_b": a["sgu_b"][0].T,
        "mix_norm_w": column(a["mix_norm_w"][0]), "w_out": a["w_out"][0], "ln2": column(a["ln2_w"][0]),
        "rel_bias": a["rel_bias"], "w_query": a["peer_w_query"][0],
        "keysT": np.stack([a["peer_keys1"][0], a["peer_keys2"][0]], 1).reshape(HALVES, KEYS, P).transpose(2, 0, 1),
        "peer_u": u.transpose(1, 3, 2, 0),
        "ln2_row": a["ln2_w"][0].reshape(1, D),
        "u_rows": u.transpose(1, 0, 2, 3).reshape(KEYS * KEYS, D),
        "peer_v": a["peer_v"][0].reshape(KEYS, KEYS, D).transpose(1, 0, 2),
    }
    arrays.update(shape_constants())
    return {k: np.ascontiguousarray(v) for k, v in arrays.items()}


def kernel(**inputs):
    import concourse.bacc as bacc
    from concourse.bass_utils import run_bass_kernel_spmd as run

    nc = bacc.Bacc("TRN2", target_bir_lowering=False, num_devices=1)
    arrays = laid_out(inputs)
    dram = {k: nc.dram_tensor(f"in_{k}", v.shape, F32, kind="ExternalInput").ap() for k, v in arrays.items()}
    dram["bias_scratch"] = nc.dram_tensor("bias_scratch", (HEADS, BIAS_LEN), F32, kind="Internal").ap()
    for name, shape in SCRATCH.items():
        dram[name] = nc.dram_tensor(f"{name}_scratch", shape, F32, kind="Internal").ap()
    dram["out"] = nc.dram_tensor("out", (SEQ, D), F32, kind="ExternalOutput").ap()
    build(nc, dram)
    result = run(nc, [{f"in_{k}": v for k, v in arrays.items()}], core_ids=[0])
    return result.results[0]["out"].reshape(1, SEQ, D)
```
